# Optimizing a Trainium2 kernel written in Bass

```python
import jax
import jax.numpy as jnp
from jax import lax
import numpy as np
import jax, jax.numpy as jnp

D_MODEL = 1024
BATCH = 1
SEQ = 512
DEPTH = 1

HEAD_DIM = 64
H_NSA = 4
H_DIL = 6
H_SB = 6
DIL_PAIRS = ((128, 1), (512, 4), (2048, 16))
N_DIL_GROUPS = len(DIL_PAIRS)
H_PER_DIL = H_DIL // N_DIL_GROUPS
CMP_LEN = 32
CMP_STRIDE = 16
CMP_HIDDEN = 128
SEL_BLOCK = 64
SEL_TOPK = 16
WIN_NSA = 512
Q_BLOCK = 128
D_FF = 4 * D_MODEL
N_SOFTMAX_HEADS = H_NSA + H_DIL
RMS_EPS = 1e-6
NEG_INF = -1e30
FORCE_BONUS = 1e4

NSA_Q_W = H_NSA * HEAD_DIM
NSA_KV_W = 6 * HEAD_DIM
NSA_GATE_W = 3 * H_NSA
DIL_W = 3 * H_DIL * HEAD_DIM
SB_W = 3 * H_SB * HEAD_DIM
D_PROJ = NSA_Q_W + NSA_KV_W + NSA_GATE_W + DIL_W + SB_W
PROJ_SPLITS = (NSA_Q_W, NSA_Q_W + NSA_KV_W, NSA_Q_W + NSA_KV_W + NSA_GATE_W,
               NSA_Q_W + NSA_KV_W + NSA_GATE_W + DIL_W)
D_CAT = (H_NSA + H_PER_DIL + H_SB) * HEAD_DIM


def rms_norm(x, g):
    xf = x.astype(jnp.float32)
    y = xf * lax.rsqrt(jnp.mean(xf * xf, axis=-1, keepdims=True) + RMS_EPS)
    return (y * g.astype(jnp.float32)).astype(x.dtype)

def alibi_slopes():
    i = jnp.arange(1, N_SOFTMAX_HEADS + 1, dtype=jnp.float32)
    return jnp.exp2(-8.0 * i / N_SOFTMAX_HEADS)

def masked_softmax(s, mask):
    s = jnp.where(mask, s, NEG_INF)
    m = jnp.max(s, axis=-1, keepdims=True)
    p = jnp.where(mask, jnp.exp(s - m), 0.0)
    l = jnp.maximum(jnp.sum(p, axis=-1, keepdims=True), 1e-30)
    return p / l, (m + jnp.log(l))[..., 0]

def unblock(y):
    y = jnp.moveaxis(y, 0, 1)
    return y.reshape((y.shape[0], y.shape[1] * y.shape[2]) + y.shape[3:])

def nsa_mixer(q, kv, gate_logits, qk_gain, cmp_pe, cmp_w1, cmp_w2, slopes):
    B, S = q.shape[0], q.shape[1]
    dt = q.dtype
    scale = HEAD_DIM ** -0.5
    q = rms_norm(q, qk_gain[0])
    k_sel = rms_norm(kv[:, :, 2], qk_gain[2])
    v_sel = kv[:, :, 3]
    k_win = rms_norm(kv[:, :, 4], qk_gain[3])
    v_win = kv[:, :, 5]
    n_cmp = (S - CMP_LEN) // CMP_STRIDE + 1
    cmp_start = CMP_STRIDE * jnp.arange(n_cmp)
    cmp_end = cmp_start + CMP_LEN - 1
    cmp_idx = cmp_start[:, None] + jnp.arange(CMP_LEN)[None]
    raw = kv[:, :, 0:2].transpose(0, 2, 1, 3)[:, :, cmp_idx]
    raw = (raw + cmp_pe[None, :, None]).reshape(B, 2, n_cmp, CMP_LEN * HEAD_DIM)
    hid = jax.nn.gelu(jnp.einsum('bcnf,cfh->bcnh', raw, cmp_w1))
    kv_c = jnp.einsum('bcnh,chd->bcnd', hid, cmp_w2)
    k_c = rms_norm(kv_c[:, 0], qk_gain[1])
    v_c = kv_c[:, 1]
    n_sel = S // SEL_BLOCK
    sel_start = SEL_BLOCK * jnp.arange(n_sel)
    overlap = ((cmp_start[:, None] <= sel_start[None] + SEL_BLOCK - 1)
               & (cmp_end[:, None] >= sel_start[None])).astype(jnp.float32)
    k_top = min(SEL_TOPK, n_sel)
    sel_offsets = jnp.arange(SEL_BLOCK)
    sel_ids = jnp.arange(n_sel)
    k_win_p = jnp.pad(k_win, ((0, 0), (WIN_NSA, 0), (0, 0)))
    v_win_p = jnp.pad(v_win, ((0, 0), (WIN_NSA, 0), (0, 0)))
    win_offsets = jnp.arange(WIN_NSA + Q_BLOCK)
    gates = jax.nn.sigmoid(gate_logits.astype(jnp.float32)).astype(dt)
    gather_rows = jax.vmap(lambda a, i: a[i])

    def block(n):
        t0 = n * Q_BLOCK
        t = t0 + jnp.arange(Q_BLOCK)
        qb = lax.dynamic_slice_in_dim(q, t0, Q_BLOCK, axis=1)
        d_c = (t[:, None] - cmp_end[None]).astype(jnp.float32)
        s = jnp.einsum('bqhd,bnd->bhqn', qb, k_c).astype(jnp.float32) * scale - slopes[:, None, None] * d_c
        p_c, _ = masked_softmax(s, d_c >= 0)
        o_c = jnp.einsum('bhqn,bnd->bqhd', p_c.astype(dt), v_c)
        imp = jnp.einsum('bhqn,nj->bqj', p_c, overlap)
        cur = t // SEL_BLOCK
        forced = (sel_ids[None] == 0) | (sel_ids[None] == cur[:, None]) | (sel_ids[None] == cur[:, None] - 1)
        imp = jnp.where(forced, imp + FORCE_BONUS, imp)
        imp = jnp.where(sel_start[None] <= t[:, None], imp, NEG_INF)
        _, top = lax.top_k(imp, k_top)
        tok = (top[..., None] * SEL_BLOCK + sel_offsets).reshape(B, Q_BLOCK, k_top * SEL_BLOCK)
        k_g = gather_rows(k_sel, tok)
        v_g = gather_rows(v_sel, tok)
        d_s = (t[None, :, None] - tok).astype(jnp.float32)
        s = jnp.einsum('bqhd,bqkd->bhqk', qb, k_g).astype(jnp.float32) * scale - slopes[None, :, None, None] * d_s[:, None]
        p_s, _ = masked_softmax(s, (d_s >= 0)[:, None])
        o_s = jnp.einsum('bhqk,bqkd->bqhd', p_s.astype(dt), v_g)
        k_w = lax.dynamic_slice_in_dim(k_win_p, t0, WIN_NSA + Q_BLOCK, axis=1)
        v_w = lax.dynamic_slice_in_dim(v_win_p, t0, WIN_NSA + Q_BLOCK, axis=1)
        kpos = t0 - WIN_NSA + win_offsets
        d_w = (t[:, None] - kpos[None]).astype(jnp.float32)
        mask_w = (d_w >= 0) & (d_w < WIN_NSA) & (kpos[None] >= 0)
        s = jnp.einsum('bqhd,bkd->bhqk', qb, k_w).astype(jnp.float32) * scale - slopes[:, None, None] * d_w
        p_w, _ = masked_softmax(s, mask_w)
        o_w = jnp.einsum('bhqk,bkd->bqhd', p_w.astype(dt), v_w)
        g = lax.dynamic_slice_in_dim(gates, t0, Q_BLOCK, axis=1)
        return g[..., 0:1] * o_c + g[..., 1:2] * o_s + g[..., 2:3] * o_w

    return unblock(lax.map(block, jnp.arange(S // Q_BLOCK)))

def dilated_mixer(qkv, qk_gain, slopes):
    S = qkv.shape[1]
    dt = qkv.dtype
    scale = HEAD_DIM ** -0.5
    q = rms_norm(qkv[:, :, 0], qk_gain[0])
    k = rms_norm(qkv[:, :, 1], qk_gain[1])
    v = qkv[:, :, 2]
    k_groups = [k[:, :, g] for g in range(N_DIL_GROUPS)]
    v_groups = [v[:, :, g] for g in range(N_DIL_GROUPS)]
    slopes_g = slopes.reshape(N_DIL_GROUPS, H_PER_DIL)

    def block(n):
        t0 = n * Q_BLOCK
        t = t0 + jnp.arange(Q_BLOCK)
        qb = lax.dynamic_slice_in_dim(q, t0, Q_BLOCK, axis=1)
        outs, lses = [], []
        for g, (w, r) in enumerate(DIL_PAIRS):
            dist = r * jnp.arange(w // r + 1)
            kidx = t[:, None] - dist[None]
            valid = kidx >= 0
            kidx = jnp.maximum(kidx, 0)
            k_g = k_groups[g][:, kidx]
            v_g = v_groups[g][:, kidx]
            s = (jnp.einsum('bqhd,bqjhd->bhqj', qb[:, :, g], k_g).astype(jnp.float32) * scale
                 - slopes_g[g][:, None, None] * dist.astype(jnp.float32))
            p, lse = masked_softmax(s, valid)
            outs.append(jnp.einsum('bhqj,bqjhd->bqhd', p.astype(dt), v_g))
            lses.append(lse)
        alpha = jax.nn.softmax(jnp.stack(lses), axis=0)
        alpha = jnp.transpose(alpha, (0, 1, 3, 2))[..., None].astype(dt)
        return jnp.sum(alpha * jnp.stack(outs), axis=0)

    return unblock(lax.map(block, jnp.arange(S // Q_BLOCK)))

def stick_breaking_mixer(qkv):
    S = qkv.shape[1]
    dt = qkv.dtype
    scale = HEAD_DIM ** -0.5
    q, k, v = qkv[:, :, 0], qkv[:, :, 1], qkv[:, :, 2]
    kpos = jnp.arange(S)

    def block(n):
        t0 = n * Q_BLOCK
        t = t0 + jnp.arange(Q_BLOCK)
        qb = lax.dynamic_slice_in_dim(q, t0, Q_BLOCK, axis=1)
        z = jnp.einsum('bqhd,bshd->bhqs', qb, k).astype(jnp.float32) * scale
        causal = kpos[None] < t[:, None]
        log_beta = jax.nn.log_sigmoid(z)
        log_fail = jnp.where(causal, jax.nn.log_sigmoid(-z), 0.0)
        after = lax.cumsum(log_fail, axis=3, reverse=True) - log_fail
        a = jnp.where(causal, jnp.exp(log_beta + after), 0.0)
        return jnp.einsum('bhqs,bshd->bqhd', a.astype(dt), v)

    return unblock(lax.map(block, jnp.arange(S // Q_BLOCK)))

def first_inputs(seed: int = 0) -> dict:
    key = jax.random.key(seed)
    ks = jax.random.split(key, 12)
    f32 = jnp.float32

    def nrm(k, shape, fan_in):
        return jax.random.normal(k, shape, f32) * (fan_in ** -0.5)

    def gain(k, shape):
        return 1.0 + 0.02 * jax.random.normal(k, shape, f32)

    return {
        'x': jax.random.normal(ks[0], (BATCH, SEQ, D_MODEL), f32),
        'norm_mix': gain(ks[1], (DEPTH, D_MODEL)),
        'norm_mlp': gain(ks[2], (DEPTH, D_MODEL)),
        'w_in': nrm(ks[3], (DEPTH, D_MODEL, D_PROJ), D_MODEL),
        'qk_gain_nsa': gain(ks[4], (DEPTH, 4, HEAD_DIM)),
        'qk_gain_dil': gain(ks[5], (DEPTH, 2, HEAD_DIM)),
        'cmp_pe': 0.1 * jax.random.normal(ks[6], (DEPTH, 2, CMP_LEN, HEAD_DIM), f32),
        'cmp_w1': nrm(ks[7], (DEPTH, 2, CMP_LEN * HEAD_DIM, CMP_HIDDEN), CMP_LEN * HEAD_DIM),
        'cmp_w2': nrm(ks[8], (DEPTH, 2, CMP_HIDDEN, HEAD_DIM), CMP_HIDDEN),
        'w_out': nrm(ks[9], (DEPTH, D_CAT, D_MODEL), D_CAT),
        'w_up': nrm(ks[10], (DEPTH, D_MODEL, D_FF), D_MODEL),
        'w_down': nrm(ks[11], (DEPTH, D_FF, D_MODEL), D_FF),
    }

def first_block(x, norm_mix, norm_mlp, w_in, qk_gain_nsa, qk_gain_dil, cmp_pe, cmp_w1, cmp_w2,
              w_out, w_up, w_down):
    B, S, _ = x.shape
    slopes = alibi_slopes()
    slopes_dil = slopes[:H_DIL]
    slopes_nsa = slopes[H_DIL:]
    for l in range(DEPTH):
        h = rms_norm(x, norm_mix[l])
        proj = h @ w_in[l]
        a_q, a_kv, a_g, b_qkv, c_qkv = jnp.split(proj, PROJ_SPLITS, axis=-1)
        o_a = nsa_mixer(a_q.reshape(B, S, H_NSA, HEAD_DIM), a_kv.reshape(B, S, 6, HEAD_DIM),
                        a_g.reshape(B, S, H_NSA, 3), qk_gain_nsa[l], cmp_pe[l], cmp_w1[l],
                        cmp_w2[l], slopes_nsa)
        o_b = dilated_mixer(b_qkv.reshape(B, S, 3, N_DIL_GROUPS, H_PER_DIL, HEAD_DIM),
                            qk_gain_dil[l], slopes_dil)
        o_c = stick_breaking_mixer(c_qkv.reshape(B, S, 3, H_SB, HEAD_DIM))
        cat = jnp.concatenate([o_a.reshape(B, S, -1), o_b.reshape(B, S, -1),
                               o_c.reshape(B, S, -1)], axis=-1)
        x = x + cat @ w_out[l]
        h = rms_norm(x, norm_mlp[l])
        x = x + jnp.square(jax.nn.relu(h @ w_up[l])) @ w_down[l]
    return x


DEPTH_2 = 2

CHUNK = 64
N_MIXERS = 2
RWKV_HEAD = 64
RWKV_HEADS = D_MODEL // RWKV_HEAD
DECAY_LORA = 64
AAA_LORA = 64
MV_LORA = 32
GATE_LORA = 160
GN_EPS = 64e-5
CONV_WIDTH = 31
FFN_CONV_WIDTH = 3
D_FF_2 = 2816
MEM_TOKENS = 256
XATTN_HEADS = 4
XATTN_HEAD_DIM = D_MODEL // XATTN_HEADS
NORM_EPS = 1e-6
LN_EPS = 1e-5


def rmsnorm(x, g):
    x32 = x.astype(jnp.float32)
    y = x32 * lax.rsqrt(jnp.mean(x32 * x32, axis=-1, keepdims=True) + NORM_EPS)
    return (y * g).astype(x.dtype)

def layernorm(x, g, b):
    x32 = x.astype(jnp.float32)
    mu = jnp.mean(x32, axis=-1, keepdims=True)
    var = jnp.mean(jnp.square(x32 - mu), axis=-1, keepdims=True)
    return ((x32 - mu) * lax.rsqrt(var + LN_EPS) * g + b).astype(x.dtype)

def causal_dwconv(x, w):
    k_w = w.shape[0]
    return lax.conv_general_dilated(
        x, w[:, None, :].astype(x.dtype), window_strides=(1,), padding=[(k_w - 1, 0)],
        dimension_numbers=('NWC', 'WIO', 'NWC'), feature_group_count=x.shape[-1])

def rwkv7_step(S, inp):
    r_t, dec_t, k_t, v_t, kk_t, a_t = inp
    sa = jnp.einsum('bhij,bhj->bhi', S, -kk_t)
    S = (S * dec_t[:, :, None, :]
         + sa[..., None] * (kk_t * a_t)[:, :, None, :]
         + v_t[..., None] * k_t[:, :, None, :])
    y = jnp.einsum('bhij,bhj->bhi', S, r_t)
    return S, y

def rwkv7_time_mix(h, mu, w_r, w_k, w_v, w_o, w0, w1, w2, a0, a1, a2, g1, g2,
                   k_k, k_a, r_k, ln_g, ln_b, v_first, v_res):
    B, T, D = h.shape
    H, N = RWKV_HEADS, RWKV_HEAD
    xx = jnp.pad(h, ((0, 0), (1, 0), (0, 0)))[:, :T] - h
    xr, xw, xk, xv, xa, xg = (h + xx * mu[i] for i in range(6))
    r = xr @ w_r
    k = xk @ w_k
    v = xv @ w_v
    logw = -jax.nn.softplus(-(w0 + jnp.tanh(xw @ w1) @ w2)) - 0.5
    decay = jnp.exp(-jnp.exp(logw.astype(jnp.float32)))
    a = jax.nn.sigmoid(a0 + (xa @ a1) @ a2)
    g = jax.nn.sigmoid(xg @ g1) @ g2
    kk = (k * k_k).astype(jnp.float32).reshape(B, T, H, N)
    kk = kk / jnp.maximum(jnp.sqrt(jnp.sum(kk * kk, axis=-1, keepdims=True)), 1e-12)
    k = k * (1.0 + (a - 1.0) * k_a)
    if v_res is not None:
        v0, v1, v2 = v_res
        v = v + (v_first - v) * jax.nn.sigmoid(v0 + (xv @ v1) @ v2)

    def heads_t(t):
        return t.astype(jnp.float32).reshape(B, T, H, N).transpose(1, 0, 2, 3)

    seq = (heads_t(r), heads_t(decay), heads_t(k), heads_t(v),
           kk.transpose(1, 0, 2, 3), heads_t(a))
    S0 = jnp.zeros((B, H, N, N), jnp.float32)
    _, y = lax.scan(rwkv7_step, S0, seq)
    y = y.transpose(1, 0, 2, 3)
    m = jnp.mean(y, axis=-1, keepdims=True)
    var = jnp.mean(jnp.square(y - m), axis=-1, keepdims=True)
    y = ((y - m) * lax.rsqrt(var + GN_EPS)).reshape(B, T, D) * ln_g + ln_b
    rh = r.astype(jnp.float32).reshape(B, T, H, N)
    kh = k.astype(jnp.float32).reshape(B, T, H, N)
    vh = v.astype(jnp.float32).reshape(B, T, H, N)
    bonus = (jnp.sum(rh * kh * r_k, axis=-1, keepdims=True) * vh).reshape(B, T, D)
    out = ((y + bonus) * g).astype(h.dtype) @ w_o
    return out, v

def conformer_conv(h, w_in, b_in, dw, dw_b, ln_g, ln_b, w_out, b_out):
    D = h.shape[-1]
    u = h @ w_in + b_in
    u = u[..., :D] * jax.nn.sigmoid(u[..., D:])
    u = causal_dwconv(u, dw) + dw_b
    u = jax.nn.silu(layernorm(u, ln_g, ln_b))
    return u @ w_out + b_out

def memory_cross_attention(h, memn, w_q, w_kv, w_o):
    B, T, D = h.shape
    q = (h @ w_q).reshape(B, T, XATTN_HEADS, XATTN_HEAD_DIM)
    kv = memn @ w_kv
    km = kv[..., :D].reshape(B, -1, XATTN_HEADS, XATTN_HEAD_DIM)
    vm = kv[..., D:].reshape(B, -1, XATTN_HEADS, XATTN_HEAD_DIM)
    s = jnp.einsum('bthd,bmhd->bhtm', q, km).astype(jnp.float32) * (XATTN_HEAD_DIM ** -0.5)
    p = jax.nn.softmax(s, axis=-1).astype(h.dtype)
    o = jnp.einsum('bhtm,bmhd->bthd', p, vm).reshape(B, T, D)
    return o @ w_o

def conv_ffn(h, w_in, dw, w_out):
    u = causal_dwconv(h @ w_in, dw)
    gate, val = u[..., :D_FF_2], u[..., D_FF_2:]
    return (jax.nn.silu(gate) * val) @ w_out

def second_inputs(seed: int = 0) -> dict:
    key = jax.random.key(seed)
    ks = iter(jax.random.split(key, 64))
    D = D_MODEL
    NA = (DEPTH_2 + 1) // 2
    NB = DEPTH_2 // 2
    NV = max(NA - 1, 0)

    def nrm(shape, scale):
        return jax.random.normal(next(ks), shape, jnp.float32) * scale

    def unif(shape, lo, hi):
        return jax.random.uniform(next(ks), shape, jnp.float32, lo, hi)

    def gain(shape):
        return 1.0 + nrm(shape, 0.05)

    sd = D ** -0.5
    return {
        'x': nrm((BATCH, SEQ, D), 1.0),
        'mem': nrm((BATCH, MEM_TOKENS, D), 1.0),
        'mem_norm_g': gain((D,)),
        'norm_mix_g': gain((DEPTH_2, D)),
        'norm_xattn_g': gain((DEPTH_2, D)),
        'norm_ffn_g': gain((DEPTH_2, D)),
        'final_norm_g': gain((D,)),
        'rwkv_mu': unif((NA, 6, D), 0.0, 1.0),
        'rwkv_w_r': nrm((NA, D, D), sd),
        'rwkv_w_k': nrm((NA, D, D), sd),
        'rwkv_w_v': nrm((NA, D, D), sd),
        'rwkv_w_o': nrm((NA, D, D), sd),
        'rwkv_w0': unif((NA, D), -6.0, 1.0),
        'rwkv_w1': nrm((NA, D, DECAY_LORA), sd),
        'rwkv_w2': nrm((NA, DECAY_LORA, D), 0.5 * DECAY_LORA ** -0.5),
        'rwkv_a0': nrm((NA, D), 0.3),
        'rwkv_a1': nrm((NA, D, AAA_LORA), sd),
        'rwkv_a2': nrm((NA, AAA_LORA, D), 0.5 * AAA_LORA ** -0.5),
        'rwkv_g1': nrm((NA, D, GATE_LORA), sd),
        'rwkv_g2': nrm((NA, GATE_LORA, D), GATE_LORA ** -0.5),
        'rwkv_k_k': 0.85 + nrm((NA, D), 0.05),
        'rwkv_k_a': 1.0 + nrm((NA, D), 0.05),
        'rwkv_r_k': nrm((NA, RWKV_HEADS, RWKV_HEAD), 0.1),
        'rwkv_ln_g': gain((NA, D)),
        'rwkv_ln_b': nrm((NA, D), 0.02),
        'rwkv_v0': nrm((NV, D), 0.3),
        'rwkv_v1': nrm((NV, D, MV_LORA), sd),
        'rwkv_v2': nrm((NV, MV_LORA, D), 0.5 * MV_LORA ** -0.5),
        'conv_w_in': nrm((NB, D, 2 * D), sd),
        'conv_b_in': nrm((NB, 2 * D), 0.02),
        'conv_dw': nrm((NB, CONV_WIDTH, D), CONV_WIDTH ** -0.5),
        'conv_dw_b': nrm((NB, D), 0.02),
        'conv_ln_g': gain((NB, D)),
        'conv_ln_b': nrm((NB, D), 0.02),
        'conv_w_out': nrm((NB, D, D), sd),
        'conv_b_out': nrm((NB, D), 0.02),
        'xattn_w_q': nrm((DEPTH_2, D, D), sd),
        'xattn_w_kv': nrm((DEPTH_2, D, 2 * D), sd),
        'xattn_w_o': nrm((DEPTH_2, D, D), sd),
        'ffn_w_in': nrm((DEPTH_2, D, 2 * D_FF_2), sd),
        'ffn_dw': nrm((DEPTH_2, FFN_CONV_WIDTH, 2 * D_FF_2), FFN_CONV_WIDTH ** -0.5),
        'ffn_w_out': nrm((DEPTH_2, D_FF_2, D), D_FF_2 ** -0.5),
    }

def second_block(x, mem, mem_norm_g, norm_mix_g, norm_xattn_g, norm_ffn_g, final_norm_g,
              rwkv_mu, rwkv_w_r, rwkv_w_k, rwkv_w_v, rwkv_w_o, rwkv_w0, rwkv_w1, rwkv_w2,
              rwkv_a0, rwkv_a1, rwkv_a2, rwkv_g1, rwkv_g2, rwkv_k_k, rwkv_k_a, rwkv_r_k,
              rwkv_ln_g, rwkv_ln_b, rwkv_v0, rwkv_v1, rwkv_v2,
              conv_w_in, conv_b_in, conv_dw, conv_dw_b, conv_ln_g, conv_ln_b,
              conv_w_out, conv_b_out, xattn_w_q, xattn_w_kv, xattn_w_o,
              ffn_w_in, ffn_dw, ffn_w_out):
    memn = rmsnorm(mem, mem_norm_g)
    v_first = None
    ia = 0
    ib = 0
    for layer in range(DEPTH_2):
        h = rmsnorm(x, norm_mix_g[layer])
        if layer % N_MIXERS == 0:
            v_res = None if ia == 0 else (rwkv_v0[ia - 1], rwkv_v1[ia - 1], rwkv_v2[ia - 1])
            out, v = rwkv7_time_mix(
                h, rwkv_mu[ia], rwkv_w_r[ia], rwkv_w_k[ia], rwkv_w_v[ia], rwkv_w_o[ia],
                rwkv_w0[ia], rwkv_w1[ia], rwkv_w2[ia], rwkv_a0[ia], rwkv_a1[ia], rwkv_a2[ia],
                rwkv_g1[ia], rwkv_g2[ia], rwkv_k_k[ia], rwkv_k_a[ia], rwkv_r_k[ia],
                rwkv_ln_g[ia], rwkv_ln_b[ia], v_first, v_res)
            if ia == 0:
                v_first = v
            ia += 1
        else:
            out = conformer_conv(h, conv_w_in[ib], conv_b_in[ib], conv_dw[ib], conv_dw_b[ib],
                                 conv_ln_g[ib], conv_ln_b[ib], conv_w_out[ib], conv_b_out[ib])
            ib += 1
        x = x + out
        x = x + memory_cross_attention(rmsnorm(x, norm_xattn_g[layer]), memn,
                                       xattn_w_q[layer], xattn_w_kv[layer], xattn_w_o[layer])
        x = x + conv_ffn(rmsnorm(x, norm_ffn_g[layer]), ffn_w_in[layer], ffn_dw[layer],
                         ffn_w_out[layer])
    return rmsnorm(x, final_norm_g)


def setup_inputs(seed=0):
    out = dict(first_inputs(seed))
    for name, value in second_inputs(seed + 1).items():
        if name != "x":
            out[name + "_2"] = value
    return out


def reference(
    x, norm_mix, norm_mlp, w_in, qk_gain_nsa, qk_gain_dil, cmp_pe, cmp_w1, cmp_w2, w_out, w_up,
    w_down, mem_2, mem_norm_g_2, norm_mix_g_2, norm_xattn_g_2, norm_ffn_g_2, final_norm_g_2,
    rwkv_mu_2, rwkv_w_r_2, rwkv_w_k_2, rwkv_w_v_2, rwkv_w_o_2, rwkv_w0_2, rwkv_w1_2, rwkv_w2_2,
    rwkv_a0_2, rwkv_a1_2, rwkv_a2_2, rwkv_g1_2, rwkv_g2_2, rwkv_k_k_2, rwkv_k_a_2, rwkv_r_k_2,
    rwkv_ln_g_2, rwkv_ln_b_2, rwkv_v0_2, rwkv_v1_2, rwkv_v2_2, conv_w_in_2, conv_b_in_2,
    conv_dw_2, conv_dw_b_2, conv_ln_g_2, conv_ln_b_2, conv_w_out_2, conv_b_out_2, xattn_w_q_2,
    xattn_w_kv_2, xattn_w_o_2, ffn_w_in_2, ffn_dw_2, ffn_w_out_2,
):
    x = first_block(
        x, norm_mix, norm_mlp, w_in, qk_gain_nsa, qk_gain_dil, cmp_pe, cmp_w1, cmp_w2, w_out,
        w_up, w_down,
    )
    return second_block(
        x, mem_2, mem_norm_g_2, norm_mix_g_2, norm_xattn_g_2, norm_ffn_g_2, final_norm_g_2,
        rwkv_mu_2, rwkv_w_r_2, rwkv_w_k_2, rwkv_w_v_2, rwkv_w_o_2, rwkv_w0_2, rwkv_w1_2,
        rwkv_w2_2, rwkv_a0_2, rwkv_a1_2, rwkv_a2_2, rwkv_g1_2, rwkv_g2_2, rwkv_k_k_2,
        rwkv_k_a_2, rwkv_r_k_2, rwkv_ln_g_2, rwkv_ln_b_2, rwkv_v0_2, rwkv_v1_2, rwkv_v2_2,
        conv_w_in_2, conv_b_in_2, conv_dw_2, conv_dw_b_2, conv_ln_g_2, conv_ln_b_2,
        conv_w_out_2, conv_b_out_2, xattn_w_q_2, xattn_w_kv_2, xattn_w_o_2, ffn_w_in_2,
        ffn_dw_2, ffn_w_out_2,
    )


_drawn_inputs = setup_inputs


def setup_inputs(seed=0):
    import zlib

    import numpy as np

    out = dict(_drawn_inputs(seed))
    spreads = {}
    factors = {'norm_mix': 3.493,
     'qk_gain_nsa': 8.0,
     'qk_gain_dil': 8.0,
     'cmp_pe': 2.995,
     'mem_norm_g_2': 8.0,
     'norm_xattn_g_2': 8.0,
     'rwkv_w1_2': 3.434,
     'rwkv_w2_2': 3.43,
     'rwkv_ln_g_2': 3.316,
     'rwkv_ln_b_2': 8.0,
     'conv_b_in_2': 7.59,
     'conv_dw_b_2': 4.285,
     'conv_ln_g_2': 2.875,
     'conv_ln_b_2': 8.0,
     'conv_b_out_2': 5.16}
    for name, (base, spread) in spreads.items():
        noise = np.random.default_rng([zlib.crc32(name.encode()), seed]).standard_normal(out[name].shape)
        drawn = base * np.exp(spread * noise) if base else spread * noise
        out[name] = jnp.asarray(drawn.astype(out[name].dtype))
    for name, factor in factors.items():
        out[name] = (out[name] * factor).astype(out[name].dtype)
    return out
```

```python
from contextlib import ExitStack

import numpy as np
import concourse.bass as bass
from concourse import mybir

F32 = mybir.dt.float32
F32R = mybir.dt.float32r
ACT = mybir.ActivationFunctionType
ALU = mybir.AluOpType
AX = mybir.AxisListType

P = 128
T = 512
D = 1024
KD = D // P
HD = 64
NB = T // P
MEM = 256
RING = 4
AHEAD = 2
N_CMP = 31
SLOPES = [float(2.0 ** (-8.0 * i / 10)) for i in range(1, 11)]
DECAY = float(np.exp(-0.5))
NEG = -1e30

T_Q, T_CMP, T_KSEL, T_KWIN, T_V, T_DQ, T_DK, T_DV, T_SQ, T_SK, T_SV = 0, 2, 3, 4, 5, 6, 9, 12, 15, 18, 21
N_PROJ = 24
V_TILES = [T_V, T_DV, T_DV + 1, T_DV + 2, T_SV, T_SV + 1, T_SV + 2]

START = 0
F1 = 4096
F2 = 2816
FFN_PARTS = (12, 10)
TAPS = 31
PE_TAPS = 13

VEC_SIZES = [("norm_mix", 8), ("norm_mlp", 8), ("mem_norm", 8), ("mix0", 8), ("mix1", 8),
             ("xattn0", 8), ("xattn1", 8), ("ffn0", 8), ("ffn1", 8), ("final", 8), ("mu", 48),
             ("w0", 8), ("a0", 8), ("k_k", 8), ("k_a", 8), ("r_k", 8), ("ln_g", 8), ("ln_b", 8),
             ("cb_in", 16), ("cdw", 8 * TAPS), ("cdw_b", 8), ("cln_g", 8), ("cln_b", 8), ("cb_out", 8),
             ("fdw0", 44 * 3), ("fdw1", 44 * 3), ("gains", 6)]
VEC = {}
_at = 0
for _n, _s in VEC_SIZES:
    VEC[_n] = _at
    _at += _s
N_VEC = _at

CONST_SIZES = [("ident", 128), ("blockones", 128), ("negtri", 128), ("m4", 512), ("levels", 7 * 128),
               ("dist", 4 * 512), ("dist_cmp", 4 * 32), ("valid", 1)]
CST = {}
_at = 0
for _n, _s in CONST_SIZES:
    CST[_n] = _at
    _at += _s
N_CONST = _at
N_KEEP = CST["dist"]


class Signal:

    def __init__(self, nc, name):
        self.sem = nc.alloc_semaphore(name)
        self.base = 0

    def __call__(self, n):
        return self.base + n


class Core:

    def __init__(self, nc):
        self.nc = nc
        self.signals = {}
        self.tiles = 0
        self.chunk = 0
        self.first = self.limit = 0

    def tile(self, name, shape, dtype):
        self.tiles += 1
        return self.nc.sbuf_tensor(f"{name}_{self.tiles}", shape, dtype)

    def sig(self, *names):
        for n in names:
            if n not in self.signals:
                self.signals[n] = Signal(self.nc, n)
        out = [self.signals[n] for n in names]
        return out if len(out) > 1 else out[0]

    def slots(self):
        return [self.sig(f"slot{j}_loaded") for j in range(RING)]

    def vec(self, name, i):
        c = VEC[name] + i
        return self.vecs[:, c:c + 1]

    def cst(self, name, w):
        return self.consts[:, CST[name]:CST[name] + w]


class Split:

    def __init__(self, stack, k, name, *shape):
        self.hi = stack.enter_context(k.tile(f"{name}_hi", [P, *shape], F32R))
        self.lo = stack.enter_context(k.tile(f"{name}_lo", [P, *shape], F32R))


def as_float(t):
    return t.bitcast(F32)


def load_everything(k, a):
    loaded, made, free, used, sq, ac = k.sig("loaded", "made", "bank_free", "chunk_used", "squared", "squares_added")
    with k.tile("sq0", [P, KD, T], F32) as sqt, k.nc.Block() as block:
        @block.sync
        def _(sp):
            sp.dma_start(k.x[:, :, :], a["x"]).then_inc(loaded.sem, 16)

        @block.scalar
        def _(act):
            act.dma_start(k.vecs[:, :], a["vecs"]).then_inc(loaded.sem, 16)
            act.dma_start(k.consts[:, :], a["consts"][:, 0:N_KEEP]).then_inc(loaded.sem, 16)
            act.wait_ge(loaded.sem, loaded(48))
            for m in range(KD):
                act.activation(sqt[:, m, :], k.x[:, m, :], ACT.Square).then_inc(sq.sem, 1)

        @block.vector
        def _(v):
            v.memset(k.ones[:, :], 1.0).then_inc(made.sem, 1)
            v.memset(k.negones[:, :], -1.0).then_inc(made.sem, 1)
            for n, value in enumerate([1e-6, 64e-6, 64e-5, 1e-5, 1.0]):
                v.memset(k.eps[:, n:n + 1], value).then_inc(made.sem, 1)
            v.wait_ge(made.sem, made(7))
            v.sem_inc(free.sem, RING)
            v.sem_inc(used.sem, RING)
            v.wait_ge(sq.sem, sq(2))
            v.tensor_tensor(k.squares[:, :], sqt[:, 0, :], sqt[:, 1, :], ALU.add).then_inc(ac.sem, 1)
            for m in range(2, KD):
                v.wait_ge(sq.sem, sq(m + 1))
                v.wait_ge(ac.sem, ac(m - 1))
                v.tensor_tensor(k.squares[:, :], k.squares[:, :], sqt[:, m, :], ALU.add).then_inc(ac.sem, 1)
    loaded.base += 48
    made.base += 7
    sq.base += KD
    ac.base += KD - 1
    used.base += RING
    k.bias = {1e-6: k.eps[:, 0:1], 64e-6: k.eps[:, 1:2], 64e-5: k.eps[:, 2:3], 1e-5: k.eps[:, 3:4], 1.0: k.eps[:, 4:5]}


def split_weights_hi(k, act, n, value):
    used, hi_r = k.sig("chunk_used", "weights_hi")
    act.wait_ge(k.slots()[n % RING].sem, value)
    act.activation(k.w.hi[:, n % RING, :], k.raw[:, n % RING, :], ACT.Copy).then_inc(hi_r.sem, 1)


def open_ring(k, stack, n_chunks):
    k.raw = stack.enter_context(k.tile("raw", [P, RING, 1024], F32))
    k.w = Split(stack, k, "w", RING, 1024)
    k.first, k.limit = k.chunk, k.chunk + n_chunks
    hi_r, lo_r = k.sig("weights_hi", "weights_lo")
    slots = k.slots()
    with k.nc.Block() as block:
        @block.sync
        def _(sp):
            for n in range(RING + AHEAD):
                if n >= RING:
                    sp.wait_ge(lo_r.sem, lo_r(n - RING + 1))
                sp.dma_start(k.raw[:, n % RING, :], k.wall[k.first + n]).then_inc(slots[n % RING].sem, 16)

        @block.scalar
        def _(act):
            for n in range(AHEAD):
                act.wait_ge(slots[n].sem, slots[n](16))
                act.activation(k.w.hi[:, n, :], k.raw[:, n, :], ACT.Copy).then_inc(hi_r.sem, 1)

        @block.gpsimd
        def _(g):
            for n in range(AHEAD):
                g.wait_ge(hi_r.sem, hi_r(n + 1))
                g.tensor_tensor(k.w.lo[:, n, :], k.raw[:, n, :], as_float(k.w.hi[:, n, :]), ALU.subtract
                                ).then_inc(lo_r.sem, 1)


def close_ring(k):
    for s in k.slots():
        s.base += 16 * ((k.limit - k.first) // RING)


def passes(e, n, first, last):
    a = 1 if first else 0
    b = max(n - 1, a) if last else n
    yield from range(a)
    if b - a == 1:
        yield a
    elif b > a:
        with e.Fori(a, b) as i:
            yield i
    yield from range(b, n)


def linear(k, m_tiles, kt, src, act=None, vector=None, pool=None, width=T, feed=None, unroll=False):
    nc = k.nc
    used, free, hi_r, lo_r, fed = k.sig("chunk_used", "bank_free", "weights_hi", "weights_lo", "fed")
    slots = k.slots()
    per = -(-kt // 8)
    n_groups, N = m_tiles // 4, m_tiles * per
    c0 = k.chunk - k.first
    n_split = min(N, k.limit - k.chunk - AHEAD)
    n_load = min(N, k.limit - k.chunk - AHEAD - RING)
    ending = n_split < N

    def sums(pe, bank, n, q, c, first, last):
        t = 8 * c + q
        w = (n % RING, slice(q * P, (q + 1) * P))
        hi, lo = k.w.hi[:, w[0], w[1]], k.w.lo[:, w[0], w[1]]
        pe.matmul(bank, hi, src.hi[:, t, 0:width], start=first, stop=False)
        pe.matmul(bank, hi, src.lo[:, t, 0:width], start=False, stop=False)
        return pe.matmul(bank, lo, src.hi[:, t, 0:width], start=False, stop=last)

    with nc.Block() as block:
        @block.sync
        def _(sp):
            ahead = AHEAD + RING

            def load(i, j):
                sp.wait_ge(lo_r.sem, lo_r(i * RING + (j + 1 + AHEAD)))
                s = (j + ahead) % RING
                at = k.chunk + j + ahead
                source = k.wall[at + i * RING] if isinstance(i, int) else \
                    k.wall[bass.ds(i * RING + at, 1)].rearrange("o p n -> (o p) n")
                sp.dma_start(k.raw[:, s, :], source).then_inc(slots[s].sem, 16)
            if n_load >= RING:
                for i in passes(sp, n_load // RING, False, False):
                    for j in range(RING):
                        load(i, j)
            for j in range(max(n_load, 0) % RING):
                load(n_load // RING, j)

        @block.tensor
        def _(pe):
            if feed is not None:
                feed.tensor(pe)
            for i in passes(pe, n_groups, feed is not None, False):
                if isinstance(i, int) and i == 0 and feed is not None:
                    assert per == 1
                    for q in range(kt):
                        pe.wait_ge(fed.sem, fed(q + 1))
                        for j in range(4):
                            if q == 0:
                                pe.wait_ge(lo_r.sem, lo_r(j + 1))
                                pe.wait_ge(free.sem, free(j + 1))
                            mm = sums(pe, k.ps[:, j, 0:width], j, q, 0, q == 0, q == kt - 1)
                            if q == kt - 1:
                                mm.then_inc(used.sem, 1)
                    continue
                for j in range(4):
                    pe.wait_ge(free.sem, free(i * 4 + (j + 1)))
                    for c in range(per):
                        n = j * per + c
                        pe.wait_ge(lo_r.sem, lo_r(i * (4 * per) + (n + 1)))
                        for q in range(min(kt - 8 * c, 8)):
                            mm = sums(pe, k.ps[:, j, 0:width], n, q, c, c == 0 and q == 0, 8 * c + q == kt - 1)
                        mm.then_inc(used.sem, 1)

        def splitter(e, step):
            def run(i, j):
                for c in range(per):
                    n = j * per + c
                    if isinstance(i, int) and i * 4 * per + n >= n_split:
                        continue
                    step(i, n)
            return run

        @block.scalar
        def _(e):
            def step(i, n):
                s = (n + AHEAD) % RING
                e.wait_ge(slots[s].sem, (i * per + (c0 // RING + (n + AHEAD) // RING + 1)) * 16 + slots[s].base)
                e.wait_ge(used.sem, used(i * (4 * per) + (n + 1 + AHEAD - RING)))
                e.activation(k.w.hi[:, s, :], k.raw[:, s, :], ACT.Copy).then_inc(hi_r.sem, 1)
            run = splitter(e, step)
            if feed is not None:
                run(0, 0)
                run(0, 1)
                feed.scalar(e)
            for i in (range(n_groups) if unroll else passes(e, n_groups, feed is not None, ending)):
                for j in range(4):
                    if not (feed is not None and isinstance(i, int) and i == 0 and j < 2):
                        run(i, j)
                    if act is not None:
                        act(e, i, j)

        @block.gpsimd
        def _(e):
            def step(i, n):
                s = (n + AHEAD) % RING
                e.wait_ge(hi_r.sem, hi_r(i * (4 * per) + (n + 1 + AHEAD)))
                e.tensor_tensor(k.w.lo[:, s, :], k.raw[:, s, :], as_float(k.w.hi[:, s, :]), ALU.subtract
                                ).then_inc(lo_r.sem, 1)
            run = splitter(e, step)
            if feed is not None:
                run(0, 0)
                run(0, 1)
                feed.gpsimd(e)
            for i in (range(n_groups) if unroll else passes(e, n_groups, feed is not None, ending)):
                for j in range(4):
                    if not (feed is not None and isinstance(i, int) and i == 0 and j < 2):
                        run(i, j)
                    if pool is not None:
                        pool(e, i, j)

        @block.vector
        def _(e):
            if feed is not None:
                feed.vector(e)
            if vector is not None:
                for i in (range(n_groups) if unroll else passes(e, n_groups, False, False)):
                    for j in range(4):
                        vector(e, i, j)
    k.chunk += N
    for s in (used, hi_r, lo_r):
        s.base += N
    free.base += m_tiles
    if feed is not None:
        feed.done()
        fed.base += kt


def dyn(t, m):
    if isinstance(m, int):
        return t[:, m, :]
    return t[:, bass.ds(m, 1), :].rearrange("p o n -> p (o n)")


def copy_out(k, out, scale=1.0, width=T):
    used, free = k.sig("chunk_used", "bank_free")

    def act(e, i, j):
        e.wait_ge(used.sem, used(i * 4 + (j + 1)))
        e.activation(dyn(out, i * 4 + j)[:, 0:width], k.ps[:, j, 0:width], ACT.Copy, scale=scale).then_inc(free.sem, 1)
    return act


def residual(k, kt, src, per=1, bias=None, squares=True):
    used, free, added, sq, ac = k.sig("chunk_used", "bank_free", "added", "squared", "squares_added")
    with k.tile("sqr", [P, 2, T], F32) as sqt:
        def vector(e, i, j):
            m = 4 * i + j
            e.wait_ge(used.sem, used((m + 1) * per))
            if bias is None:
                ins = e.tensor_tensor(k.x[:, m, :], k.x[:, m, :], k.ps[:, j, :], ALU.add)
            else:
                ins = e.scalar_tensor_tensor(k.x[:, m, :], k.x[:, m, :], k.vec(bias, m), k.ps[:, j, :], ALU.add, ALU.add)
            ins.then_inc(free.sem, 1)
            if squares:
                e.sem_inc(added.sem, 1)

        def act(e, i, j):
            m = 4 * i + j
            e.wait_ge(free.sem, free(m + 1 + RING))
            if m >= 2:
                e.wait_ge(ac.sem, ac(m - 1))
            e.activation(sqt[:, m % 2, :], k.x[:, m, :], ACT.Square).then_inc(sq.sem, 1)

        def pool(e, i, j):
            m = 4 * i + j
            e.wait_ge(sq.sem, sq(m + 1))
            if m == 0:
                e.tensor_copy(k.squares[:, :], sqt[:, 0, :]).then_inc(ac.sem, 1)
            else:
                e.wait_ge(ac.sem, ac(m))
                e.tensor_tensor(k.squares[:, :], k.squares[:, :], sqt[:, m % 2, :], ALU.add).then_inc(ac.sem, 1)
        squares_ = squares
        linear(k, KD, kt, src, vector=vector, act=act if squares_ else None, pool=pool if squares_ else None, unroll=True)
    if squares:
        added.base += KD
        sq.base += KD
        ac.base += KD


class Norm:

    def __init__(self, k, gain, dst, whole):
        self.k, self.gain, self.dst, self.whole = k, gain, dst, whole

    def tensor(self, pe):
        k = self.k
        pe.matmul(k.ps[:, 4, :], k.ones[:, :], k.squares[:, :], start=True, stop=True).then_inc(k.sig("summed").sem, 1)

    def scalar(self, act):
        k = self.k
        summed, root, whole_r, hi = k.sig("summed", "root", "normed", "fed_hi")
        act.wait_ge(summed.sem, summed(1))
        act.activation(k.root[:, :], k.ps[:, 4, :], ACT.Sqrt, scale=1.0 / D, bias=k.bias[1e-6]).then_inc(root.sem, 1)
        for m in range(KD):
            act.wait_ge(whole_r.sem, whole_r(m + 1))
            act.activation(self.dst.hi[:, m, :], self.whole[:, m, :], ACT.Copy).then_inc(hi.sem, 1)

    def vector(self, v):
        k = self.k
        root, inverse, whole_r, hi, fed = k.sig("root", "inverse", "normed", "fed_hi", "fed")
        v.wait_ge(root.sem, root(1))
        v.reciprocal(k.root[:, :], k.root[:, :]).then_inc(inverse.sem, 1)
        v.wait_ge(inverse.sem, inverse(1))

        def rest(m):
            v.wait_ge(hi.sem, hi(m + 1))
            v.tensor_tensor(self.dst.lo[:, m, :], self.whole[:, m, :], as_float(self.dst.hi[:, m, :]), ALU.subtract
                            ).then_inc(fed.sem, 1)
        for m in range(KD):
            v.scalar_tensor_tensor(self.whole[:, m, :], k.x[:, m, :], k.vec(self.gain, m), k.root[:, :],
                                   ALU.mult, ALU.mult).then_inc(whole_r.sem, 1)
            if m:
                rest(m - 1)
        rest(KD - 1)

    def gpsimd(self, g):
        pass

    def done(self):
        for n, c in (("summed", 1), ("root", 1), ("inverse", 1), ("normed", KD), ("fed_hi", KD)):
            self.k.sig(n).base += c


class Parts:

    def __init__(self, k, whole, dst, n):
        self.k, self.whole, self.dst, self.n = k, whole, dst, n

    def tensor(self, pe):
        pass

    def scalar(self, act):
        hi = self.k.sig("fed_hi")
        for m in range(self.n):
            act.activation(self.dst.hi[:, m, :], self.whole[:, m, :], ACT.Copy).then_inc(hi.sem, 1)

    def vector(self, v):
        hi, fed = self.k.sig("fed_hi", "fed")
        for m in range(self.n):
            v.wait_ge(hi.sem, hi(m + 1))
            v.tensor_tensor(self.dst.lo[:, m, :], self.whole[:, m, :], as_float(self.dst.hi[:, m, :]), ALU.subtract
                            ).then_inc(fed.sem, 1)

    def gpsimd(self, g):
        pass

    def done(self):
        self.k.sig("fed_hi").base += self.n


class Mix:

    def __init__(self, k, h, xx, xm, dst, i):
        self.k, self.h, self.xx, self.xm, self.dst, self.i = k, h, xx, xm, dst, i

    def tensor(self, pe):
        pass

    def scalar(self, act):
        whole_r, hi = self.k.sig("normed", "fed_hi")
        for m in range(KD):
            act.wait_ge(whole_r.sem, whole_r(m + 1))
            act.activation(self.dst.hi[:, m, :], self.xm[:, m % 4, :], ACT.Copy).then_inc(hi.sem, 1)

    def vector(self, v):
        k = self.k
        whole_r, hi, fed = k.sig("normed", "fed_hi", "fed")

        def rest(m):
            v.wait_ge(hi.sem, hi(m + 1))
            v.tensor_tensor(self.dst.lo[:, m, :], self.xm[:, m % 4, :], as_float(self.dst.hi[:, m, :]), ALU.subtract
                            ).then_inc(fed.sem, 1)
        for m in range(KD):
            if m >= 4:
                v.wait_ge(fed.sem, fed(m - 3))
            v.scalar_tensor_tensor(self.xm[:, m % 4, :], self.xx[:, m, :], k.vec("mu", 8 * self.i + m), self.h[:, m, :],
                                   ALU.mult, ALU.add).then_inc(whole_r.sem, 1)
            if m:
                rest(m - 1)
        rest(KD - 1)

    def gpsimd(self, g):
        pass

    def done(self):
        for n in ("normed", "fed_hi"):
            self.k.sig(n).base += KD



def gates_of(k, wg, h, gates_w, gates, valid):
    wgl, gs, gt, gv = k.sig("gate_w_loaded", "gate_sums", "gates_made", "gates_masked")
    with k.nc.Block() as block:
        @block.sync
        def _(sp):
            sp.dma_start(gates_w[:, :, :], wg).then_inc(wgl.sem, 16)

        @block.tensor
        def _(pe):
            pe.wait_ge(wgl.sem, wgl(16))
            for b in range(NB):
                for m in range(KD):
                    mm = pe.matmul(k.ps[:, 4, b * 16:b * 16 + 12], h[:, m, b * P:(b + 1) * P], gates_w[:, m, :],
                                   start=(m == 0), stop=(m == KD - 1))
            mm.then_inc(gs.sem, 1)

        @block.scalar
        def _(act):
            act.wait_ge(gs.sem, gs(1))
            act.activation(gates[:, :, :], k.ps[:, 4, 0:64].rearrange("p (b g) -> p b g", b=NB)[:, :, 0:12],
                           ACT.Sigmoid).then_inc(gt.sem, 1)

        @block.vector
        def _(v):
            v.wait_ge(gt.sem, gt(1))
            v.tensor_scalar(gates[:, 0, 0:12:3], gates[:, 0, 0:12:3], valid, None, ALU.mult).then_inc(gv.sem, 1)
    wgl.base += 16
    gs.base += 1
    gt.base += 1
    gv.base += 1


def values_by_token(k, pr, vt):
    tr, te = k.sig("transposed", "transposed_out")
    with k.nc.Block() as block:
        @block.tensor
        def _(pe):
            for n, tile in enumerate(V_TILES):
                if n >= 4:
                    pe.wait_ge(te.sem, te(n - 3))
                for b in range(NB):
                    mm = pe.transpose(k.ps[:, 4 + n % 4, b * P:(b + 1) * P], pr[:, tile, b * P:(b + 1) * P], k.ident)
                mm.then_inc(tr.sem, 1)

        @block.scalar
        def _(act):
            for n in range(len(V_TILES)):
                act.wait_ge(tr.sem, tr(n + 1))
                act.activation(vt[:, :, n, :], k.ps[:, 4 + n % 4, :].rearrange("p (b d) -> p b d", b=NB), ACT.Copy
                               ).then_inc(te.sem, 1)
    tr.base += len(V_TILES)
    te.base += len(V_TILES)


def head_norms(k, pr):
    tiles = [(T_Q, 0, True), (T_Q + 1, 0, True), (T_KSEL, 2, False), (T_KWIN, 3, False)]
    tiles += [(T_DQ + i, 4, True) for i in range(3)] + [(T_DK + i, 5, False) for i in range(3)]
    sq_r, ss_r, rt_r, inv_r, nr, qs = k.sig("squared", "summed", "root", "inverse", "normed", "q_scaled")
    n = len(tiles)
    with k.tile("hn_sq", [P, 2, T], F32) as sq, k.tile("hn_rt", [P, 2, T], F32) as rt, \
         k.nc.Block() as block:
        @block.scalar
        def _(act):
            def square(t):
                if t >= 2:
                    act.wait_ge(ss_r.sem, ss_r(t - 1))
                act.activation(sq[:, t % 2, :], pr[:, tiles[t][0], :], ACT.Square).then_inc(sq_r.sem, 1)
            square(0)
            for t in range(n):
                if t + 1 < n:
                    square(t + 1)
                act.wait_ge(ss_r.sem, ss_r(t + 1))
                if t >= 2:
                    act.wait_ge(inv_r.sem, inv_r(t - 1))
                q = tiles[t][2]
                act.activation(rt[:, t % 2, :], k.ps[:, t % 2, :], ACT.Sqrt, scale=1.0 if q else 1.0 / HD,
                               bias=k.bias[64e-6 if q else 1e-6]).then_inc(rt_r.sem, 1)

        @block.tensor
        def _(pe):
            for t in range(n):
                pe.wait_ge(sq_r.sem, sq_r(t + 1))
                if t >= 2:
                    pe.wait_ge(rt_r.sem, rt_r(t - 1))
                pe.matmul(k.ps[:, t % 2, :], k.blockones, sq[:, t % 2, :], start=True, stop=True).then_inc(ss_r.sem, 1)

        @block.vector
        def _(v):
            for t in range(n):
                v.wait_ge(rt_r.sem, rt_r(t + 1))
                if t >= 2:
                    v.wait_ge(nr.sem, nr(t - 1))
                v.reciprocal(k.ps[:, 4 + t % 2, :], rt[:, t % 2, :]).then_inc(inv_r.sem, 1)
                v.wait_ge(inv_r.sem, inv_r(t + 1))
                v.scalar_tensor_tensor(pr[:, tiles[t][0], :], pr[:, tiles[t][0], :], k.vec("gains", tiles[t][1]),
                                       k.ps[:, 4 + t % 2, :], ALU.mult, ALU.mult).then_inc(nr.sem, 1)

        @block.gpsimd
        def _(g):
            for i in range(3):
                g.tensor_scalar(pr[:, T_SQ + i, :], pr[:, T_SQ + i, :], 0.125, None, ALU.mult).then_inc(qs.sem, 1)
    sq_r.base += n
    ss_r.base += n
    rt_r.base += n
    inv_r.base += n
    nr.base += n
    qs.base += 3


def compress(k, pr, w1_in, w2_in, pe_in, kc, vc):
    ld, raw_r, hs, ge, out_r, c1, c2, c3, c4, c5 = k.sig(
        "cmp_loaded", "cmp_raw", "cmp_hidden", "cmp_gelu", "cmp_out", "cmp_sq", "cmp_ss", "cmp_rt", "cmp_inv", "cmp_done")
    nc = k.nc
    with k.tile("cw1", [P, 32, 128], F32) as w1, k.tile("cw2", [P, 192], F32) as w2, \
         k.tile("cpe", [P, 32], F32) as pos, k.tile("craw", [P, 32, N_CMP], F32) as raw, \
         k.tile("chid", [P, 2, N_CMP], F32) as hid, k.tile("ck", [P, 4, 32], F32) as tmp, \
         nc.Block() as block:
        @block.sync
        def _(sp):
            sp.dma_start(pos[:, :], pe_in).then_inc(ld.sem, 16)
            sp.dma_start(w1[:, :, :], w1_in).then_inc(ld.sem, 16)
            sp.dma_start(w2[:, :], w2_in).then_inc(ld.sem, 16)

        @block.vector
        def _(v):
            v.wait_ge(ld.sem, ld(48))
            kv = pr[:, T_CMP, :].rearrange("p (n j) -> p j n", j=16)
            for half in range(2):
                v.tensor_tensor(raw[:, 16 * half:16 * half + 16, :], kv[:, :, half:half + N_CMP],
                                pos[:, 16 * half:16 * half + 16].unsqueeze(2).to_broadcast([P, 16, N_CMP]),
                                ALU.add).then_inc(raw_r.sem, 1)
            v.wait_ge(out_r.sem, out_r(2))
            v.wait_ge(c1.sem, c1(1))
            v.tensor_copy(tmp[:, 0, 0:N_CMP], k.ps[:, 2, 0:N_CMP]).then_inc(c5.sem, 1)
            v.tensor_copy(vc[0:N_CMP, :], k.ps[0:N_CMP, 3, 0:64]).then_inc(c5.sem, 1)
            v.wait_ge(c3.sem, c3(1))
            v.reciprocal(tmp[:, 3, 0:N_CMP], tmp[:, 2, 0:N_CMP]).then_inc(c4.sem, 1)
            v.wait_ge(c4.sem, c4(1))
            v.scalar_tensor_tensor(kc[:, 0:N_CMP], tmp[:, 0, 0:N_CMP], k.vec("gains", 1), tmp[:, 3, 0:N_CMP],
                                   ALU.mult, ALU.mult).then_inc(c5.sem, 1)

        @block.tensor
        def _(pe):
            pe.wait_ge(raw_r.sem, raw_r(2))
            pe.wait_ge(ld.sem, ld(48))
            for c in range(2):
                o = 64 * c
                for j in range(32):
                    mm = pe.matmul(k.ps[:, c, 0:N_CMP], w1[o:o + 64, j, :], raw[o:o + 64, j, :],
                                   start=(j == 0), stop=(j == 31))
                mm.then_inc(hs.sem, 1)
            pe.wait_ge(ge.sem, ge(2))
            pe.matmul(k.ps[:, 2, 0:N_CMP], w2[:, 0:128], hid[:, 0, :], start=True, stop=True).then_inc(out_r.sem, 1)
            pe.matmul(k.ps[0:N_CMP, 3, 0:64], hid[:, 1, :], w2[:, 128:192], start=True, stop=True).then_inc(out_r.sem, 1)
            pe.wait_ge(c1.sem, c1(1))
            pe.matmul(k.ps[:, 4, 0:N_CMP], k.blockones, tmp[:, 1, 0:N_CMP], start=True, stop=True).then_inc(c2.sem, 1)

        @block.scalar
        def _(act):
            for c in range(2):
                act.wait_ge(hs.sem, hs(c + 1))
                act.activation(hid[:, c, :], k.ps[:, c, 0:N_CMP], ACT.Gelu_apprx_tanh).then_inc(ge.sem, 1)
            act.wait_ge(out_r.sem, out_r(1))
            act.activation(tmp[:, 1, 0:N_CMP], k.ps[:, 2, 0:N_CMP], ACT.Square).then_inc(c1.sem, 1)
            act.wait_ge(c2.sem, c2(1))
            act.activation(tmp[:, 2, 0:N_CMP], k.ps[:, 4, 0:N_CMP], ACT.Sqrt, scale=1.0 / HD, bias=k.bias[1e-6]
                           ).then_inc(c3.sem, 1)
    ld.base += 48
    raw_r.base += 2
    hs.base += 2
    ge.base += 2
    out_r.base += 2
    c1.base += 1
    c2.base += 1
    c3.base += 1
    c4.base += 1
    c5.base += 3


def softmax_mixers(k, pr, vt, gates, dist, dist_cmp, kc, vc, cat):
    nc = k.nc
    units = []
    for h in range(4):
        for b, key in ((0, None), (1, T_KSEL), (2, T_KWIN)):
            units.append((T_Q + h // 2, h % 2, key, (0, 64 * (b == 2)), 0, SLOPES[6 + h]))
    for j in range(2):
        for g in range(3):
            units.append((T_DQ + g, j, T_DK + g, (1 + g, 64 * j), 1 + g, SLOPES[2 * g + j]))
    U = len(units)
    sc, bi, mx, ex, wt, scaled, tr, pt_r, pv, oe, sm, mg = k.sig(
        "scores", "biased", "maxima", "exps", "weights", "scaled", "transposed", "transposed_out", "pv_done",
        "mixer_out", "small_steps", "merged_exps")
    with k.tile("sm_p", [P, U, T], F32) as p, k.tile("sm_pt", [P, 3, T], F32) as pt, \
         k.tile("sm_st", [P, 6, 32], F32) as st, nc.Block() as block:
        nm, l, w, e, nmm = st[:, 0, :], st[:, 1, :], st[:, 2, :], st[:, 3, :], st[:, 4, :]
        el = st[:, 5, :]

        def width(u, qb):
            return N_CMP if units[u][2] is None else (qb + 1) * P

        @block.tensor
        def _(pe):
            for qb in range(NB):
                for u, (qt, half, key, _, _, _) in enumerate(units):
                    g = qb * U + u
                    o, w_ = 64 * half, width(u, qb)
                    if g >= 4:
                        pe.wait_ge(bi.sem, bi(g - 3))
                    keys = kc[o:o + 64, 0:w_] if key is None else pr[o:o + 64, key, 0:w_]
                    pe.matmul(k.ps[:, g % 4, 0:w_], pr[o:o + 64, qt, qb * P:(qb + 1) * P], keys,
                              start=True, stop=True).then_inc(sc.sem, 1)

                def turn(u):
                    g = qb * U + u
                    w_ = width(u, qb)
                    pe.wait_ge(scaled.sem, scaled(g + 1))
                    if g >= 2:
                        pe.wait_ge(pt_r.sem, pt_r(g - 1))
                    for b in range(-(-w_ // P)):
                        r = min(P, w_ - b * P)
                        mm = pe.transpose(k.ps[0:r, 4 + g % 2, b * P:(b + 1) * P], p[:, u, b * P:b * P + r], k.ident)
                    mm.then_inc(tr.sem, 1)

                def values(u):
                    g = qb * U + u
                    _, half, key, (vtile, vcol), _, _ = units[u]
                    w_, o = width(u, qb), 64 * half
                    head = u // 3
                    out = 3 * qb + head // 2
                    if u % 3 == 0 and out >= 2:
                        pe.wait_ge(oe.sem, oe(out - 1))
                    pe.wait_ge(pt_r.sem, pt_r(g + 1))
                    nblk = -(-w_ // P)
                    for b in range(nblk):
                        r = min(P, w_ - b * P)
                        val = vc[0:r, :] if key is None else vt[:, b, vtile, vcol:vcol + 64]
                        mm = pe.matmul(k.ps[o:o + 64, 6 + out % 2, 0:P], val, pt[0:r, g % 3, b * P:(b + 1) * P],
                                       start=(u % 3 == 0 and b == 0), stop=(u % 3 == 2 and b == nblk - 1))
                    mm.then_inc(pv.sem, 1)

                turn(0)
                for u in range(U):
                    if u + 1 < U:
                        turn(u + 1)
                    values(u)

        @block.vector
        def _(v):
            steps = 0
            for qb in range(NB):
                def bias(u):
                    g = qb * U + u
                    w_ = width(u, qb)
                    table, slope = units[u][4], units[u][5]
                    d = dist_cmp[:, qb, 0:w_] if units[u][2] is None else dist[:, table, T - w_:T]
                    v.wait_ge(sc.sem, sc(g + 1))
                    if qb >= 1:
                        v.wait_ge(tr.sem, tr(g - U + 1))
                    v.scalar_tensor_tensor(p[:, u, 0:w_], d, slope, k.ps[:, g % 4, 0:w_], ALU.mult, ALU.add
                                           ).then_inc(bi.sem, 1)

                def maximum(u):
                    g = qb * U + u
                    v.wait_ge(bi.sem, bi(g + 1))
                    if qb >= 1 and u == 0:
                        v.wait_ge(scaled.sem, scaled(g))
                    v.tensor_reduce(nm[:, u:u + 1], p[:, u, 0:width(u, qb)], AX.X, ALU.max, negate=True
                                    ).then_inc(mx.sem, 1)
                bias(0)
                for u in range(U):
                    if u + 1 < U:
                        bias(u + 1)
                    maximum(u)
                v.wait_ge(mx.sem, mx((qb + 1) * U))
                v.tensor_reduce(nmm[:, 0:2], nm[:, 12:18].rearrange("p (a b) -> p a b", a=2), AX.X, ALU.min
                                ).then_inc(sm.sem, 1)
                v.wait_ge(ex.sem, ex((qb + 1) * U))
                v.reciprocal(el[:, 0:12], l[:, 0:12]).then_inc(sm.sem, 1)
                v.wait_ge(mg.sem, mg(2 * (qb + 1)))
                v.tensor_tensor(el[:, 12:18], e[:, 0:6], l[:, 12:18], ALU.mult).then_inc(sm.sem, 1)
                v.wait_ge(sm.sem, sm(6 * qb + 3))
                v.tensor_tensor(w[:, 0:12], el[:, 0:12], gates[:, qb, :], ALU.mult).then_inc(wt.sem, 1)
                v.tensor_reduce(nmm[:, 2:4], el[:, 12:18].rearrange("p (a b) -> p a b", a=2), AX.X, ALU.add
                                ).then_inc(sm.sem, 1)
                v.wait_ge(sm.sem, sm(6 * qb + 4))
                v.reciprocal(nmm[:, 4:6], nmm[:, 2:4]).then_inc(sm.sem, 1)
                v.wait_ge(sm.sem, sm(6 * qb + 5))
                v.tensor_tensor(w[:, 12:18].rearrange("p (a b) -> p a b", a=2),
                                e[:, 0:6].rearrange("p (a b) -> p a b", a=2),
                                nmm[:, 4:6].unsqueeze(2).to_broadcast([P, 2, 3]), ALU.mult).then_inc(wt.sem, 1)
                v.sem_inc(sm.sem, 1)
                for i in range(3):
                    v.wait_ge(pv.sem, pv(qb * U + 6 * (i + 1)))
                    v.tensor_copy(cat[:, i, qb * P:(qb + 1) * P], k.ps[:, 6 + (3 * qb + i) % 2, 0:P]).then_inc(oe.sem, 1)

        @block.scalar
        def _(act):
            for qb in range(NB):
                for u in range(U):
                    g = qb * U + u
                    act.wait_ge(mx.sem, mx(g + 1))
                    act.activation(p[:, u, 0:width(u, qb)], p[:, u, 0:width(u, qb)], ACT.Exp, bias=nm[:, u:u + 1],
                                   accum_out=l[:, u:u + 1]).then_inc(ex.sem, 1)
                act.wait_ge(sm.sem, sm(6 * qb + 1))
                for j in range(2):
                    act.activation(e[:, 3 * j:3 * j + 3], nm[:, 12 + 3 * j:15 + 3 * j], ACT.Exp, scale=-1.0,
                                   bias=nmm[:, j:j + 1]).then_inc(mg.sem, 1)
                for u in range(U):
                    g = qb * U + u
                    w_ = width(u, qb)
                    act.wait_ge(tr.sem, tr(g + 1))
                    if g >= 3:
                        act.wait_ge(pv.sem, pv(g - 2))
                    r, c = (w_, P) if units[u][2] is None else (P, w_)
                    act.activation(pt[0:r, g % 3, 0:c], k.ps[0:r, 4 + g % 2, 0:c], ACT.Copy).then_inc(pt_r.sem, 1)

        @block.gpsimd
        def _(gp):
            for qb in range(NB):
                gp.wait_ge(wt.sem, wt(2 * (qb + 1)))
                for u in range(U):
                    gp.tensor_scalar(p[:, u, 0:width(u, qb)], p[:, u, 0:width(u, qb)], w[:, u:u + 1], None, ALU.mult
                                     ).then_inc(scaled.sem, 1)
    for s in (sc, bi, mx, ex, scaled, tr, pt_r, pv):
        s.base += NB * U
    wt.base += 2 * NB
    oe.base += 3 * NB
    sm.base += 6 * NB
    mg.base += 2 * NB


def stick_breaking(k, pr, vt, cat):
    nc = k.nc
    H = 6
    units = [(h, kb) for h in range(H) for kb in (3, 2, 1, 0)]
    z_r, chain, ln_r, sp_raw, sp_r, l_r, at_raw, at_r, o_r, oe = k.sig(
        "z_ready", "softplus_steps", "softplus_log", "softplus_raw", "softplus_ready", "log_weights", "weights_raw",
        "weights_ready", "sb_out", "sb_out_taken")
    n = len(units)
    with k.tile("sb_sp", [P, 8, T], F32) as sp_t, k.tile("sb_at", [P, 8, T], F32) as at, \
         k.tile("sb_t", [P, 2, T], F32) as t1, nc.Block() as block:
        @block.tensor
        def _(pe):
            def z(u):
                h, kb = units[u]
                o, w = 64 * (h % 2), T - kb * P
                if u >= 4:
                    pe.wait_ge(at_raw.sem, at_raw(u - 3))
                pe.matmul(k.ps[:, u % 4, 0:w], pr[o:o + 64, T_SK + h // 2, kb * P:(kb + 1) * P],
                          pr[o:o + 64, T_SQ + h // 2, kb * P:T], start=True, stop=False,
                          skip_group_check=True).then_inc(z_r.sem, 1)

            def accumulate(u):
                h, kb = units[u]
                pe.wait_ge(sp_r.sem, sp_r(u + 1))
                mm = pe.matmul(k.ps[:, u % 4, 0:T - kb * P], k.negtri, sp_t[:, u % 8, 0:T - kb * P],
                               start=False, stop=(kb == 3), skip_group_check=True)
                for later in range(kb + 1, 4):
                    mm = pe.matmul(k.ps[:, u % 4, (later - kb) * P:T - kb * P], k.negones[:, :],
                                   sp_t[:, (4 * h + 3 - later) % 8, 0:T - later * P], start=False,
                                   stop=(later == 3), skip_group_check=True)
                mm.then_inc(l_r.sem, 1)

            def values(h):
                o = 64 * (h % 2)
                pe.wait_ge(at_r.sem, at_r(4 * h + 4))
                if h >= 2:
                    pe.wait_ge(oe.sem, oe(h - 1))
                for kb in range(4):
                    mm = pe.matmul(k.ps[o:o + 64, 4 + h % 2, kb * P:T], vt[:, kb, 4 + h // 2, o:o + 64],
                                   at[:, (4 * h + 3 - kb) % 8, 0:T - kb * P], start=(kb == 0), stop=(kb == 3),
                                   skip_group_check=True)
                mm.then_inc(o_r.sem, 1)

            z(0)
            for u in range(n):
                if u + 1 < n:
                    z(u + 1)
                accumulate(u)
                if u % 4 == 0 and u > 0:
                    values(u // 4 - 1)
            values(H - 1)

        @block.scalar
        def _(act):
            def softplus(u):
                w = T - units[u][1] * P
                act.wait_ge(z_r.sem, z_r(u + 1))
                if u >= 2:
                    act.wait_ge(sp_raw.sem, sp_raw(u - 1))
                act.activation(t1[:, u % 2, 0:w], k.ps[:, u % 4, 0:w], ACT.Abs).then_inc(chain.sem, 1)
                act.wait_ge(chain.sem, chain(2 * u + 1))
                act.activation(t1[:, u % 2, 0:w], t1[:, u % 2, 0:w], ACT.Exp, scale=-1.0).then_inc(chain.sem, 1)
                act.wait_ge(chain.sem, chain(2 * u + 2))
                act.activation(t1[:, u % 2, 0:w], t1[:, u % 2, 0:w], ACT.Ln, bias=k.bias[1.0]).then_inc(ln_r.sem, 1)

            def weights(u):
                h, kb = units[u]
                w = T - kb * P
                act.wait_ge(l_r.sem, l_r(u + 1))
                if h >= 2:
                    act.wait_ge(o_r.sem, o_r(h - 1))
                act.activation(at[:, u % 8, 0:w], k.ps[:, u % 4, 0:w], ACT.Exp).then_inc(at_raw.sem, 1)

            softplus(0)
            for u in range(n):
                if u + 1 < n:
                    softplus(u + 1)
                weights(u)

        @block.vector
        def _(v):
            def out(h):
                o = 64 * (h % 2)
                v.wait_ge(o_r.sem, o_r(h + 1))
                v.tensor_copy(cat[o:o + 64, 3 + h // 2, :], k.ps[o:o + 64, 4 + h % 2, :]).then_inc(oe.sem, 1)

            for u in range(n):
                h, kb = units[u]
                w = T - kb * P
                v.wait_ge(ln_r.sem, ln_r(u + 1))
                if h >= 2:
                    v.wait_ge(l_r.sem, l_r(4 * (h - 1)))
                v.scalar_tensor_tensor(sp_t[:, u % 8, 0:w], k.ps[:, u % 4, 0:w], 0.0, t1[:, u % 2, 0:w],
                                       ALU.max, ALU.add).then_inc(sp_raw.sem, 1)
                if u % 4 == 1 and u > 4:
                    out(u // 4 - 1)
            out(H - 1)

        @block.gpsimd
        def _(g):
            def strict(t):
                return g.affine_select(t, t, [[1, P]], ALU.is_ge, 0.0, base=-1, channel_multiplier=-1)

            g.wait_ge(sp_raw.sem, sp_raw(1))
            strict(sp_t[:, 0, 0:P]).then_inc(sp_r.sem, 1)
            for u in range(n):
                if u + 1 < n:
                    g.wait_ge(sp_raw.sem, sp_raw(u + 2))
                    strict(sp_t[:, (u + 1) % 8, 0:P]).then_inc(sp_r.sem, 1)
                g.wait_ge(at_raw.sem, at_raw(u + 1))
                strict(at[:, u % 8, 0:P]).then_inc(at_r.sem, 1)
    for s in (z_r, ln_r, sp_raw, sp_r, l_r, at_raw, at_r):
        s.base += n
    chain.base += 2 * n
    o_r.base += H
    oe.base += H


def first_block(k, a, stop):
    nc = k.nc
    with ExitStack() as outer:
        tile = lambda st, name, *shape: st.enter_context(k.tile(name, [P, *shape], F32))
        cat = tile(outer, "cat", 6, T)
        with ExitStack() as mixers:
            pr = tile(mixers, "proj", N_PROJ, T)
            far = tile(mixers, "dist", N_CONST - N_KEEP)
            gates = tile(mixers, "gates", NB, 12)
            kc = tile(mixers, "kc", 32)
            vc = tile(mixers, "vc", 64)
            dist = far[:, 0:2048].rearrange("p (a t) -> p a t", a=4)
            dist_cmp = far[:, 2048:2048 + 128].rearrange("p (a t) -> p a t", a=4)
            with ExitStack() as st:
                h = tile(st, "h", KD, T)
                gw = tile(st, "gates_w", KD, 12)
                with ExitStack() as st2:
                    hs = Split(st2, k, "h", KD, T)
                    far_loaded = k.sig("distances_loaded")
                    out = copy_out(k, pr)

                    def act(e, i, j):
                        if isinstance(i, int) and i == 0 and j == 0:
                            e.dma_start(far[:, :], a["consts"][:, N_KEEP:N_CONST]).then_inc(far_loaded.sem, 16)
                        out(e, i, j)
                    linear(k, N_PROJ, KD, hs, act=act, feed=Norm(k, "norm_mix", hs, h))
                gates_of_valid = far[:, 2176:2177]
                with nc.Block() as block:
                    @block.vector
                    def _(v):
                        v.wait_ge(far_loaded.sem, far_loaded(16))
                gates_of(k, a["w_gate"], h, gw, gates, gates_of_valid)
            vt = tile(mixers, "values", NB, 7, P)
            values_by_token(k, pr, vt)
            head_norms(k, pr)
            compress(k, pr, a["cmp_w1"], a["cmp_w2"], a["cmp_pe"], kc, vc)
            stick_breaking(k, pr, vt, cat)
            softmax_mixers(k, pr, vt, gates, dist, dist_cmp, kc, vc, cat)
        cs = Split(outer, k, "cat", 6, T)
        split_tiles(k, cat, cs, 6)
        residual(k, 6, cs)
    if stop == 1:
        return
    mlp(k)


def split_tiles(k, whole, dst, n):
    hi, lo = k.sig("fed_hi", "fed_lo")
    with k.nc.Block() as block:
        @block.scalar
        def _(act):
            for m in range(n):
                act.activation(dst.hi[:, m, :], whole[:, m, :], ACT.Copy).then_inc(hi.sem, 1)

        @block.vector
        def _(v):
            for m in range(n):
                v.wait_ge(hi.sem, hi(m + 1))
                v.tensor_tensor(dst.lo[:, m, :], whole[:, m, :], as_float(dst.hi[:, m, :]), ALU.subtract).then_inc(lo.sem, 1)
    hi.base += n
    lo.base += n


def mlp(k):
    used, free, relued, whole_r, hi, lo = k.sig("chunk_used", "bank_free", "relued", "hidden_whole", "hidden_hi", "hidden_lo")
    half = F1 // P // 2
    with ExitStack() as st:
        hs = Split(st, k, "h", KD, T)
        h = st.enter_context(k.tile("h", [P, KD, T], F32))
        hid = Split(st, k, "hidden", half, T)
        rl = st.enter_context(k.tile("relu", [P, 2, T], F32))
        sq = st.enter_context(k.tile("relu2", [P, 2, T], F32))

        def act(e, i, j):
            e.wait_ge(used.sem, used(i * 4 + (j + 1)))
            e.wait_ge(free.sem, free(i * 4 + (j + RING - 1)))
            e.activation(rl[:, j % 2, :], k.ps[:, j, :], ACT.Relu).then_inc(relued.sem, 1)
            e.wait_ge(relued.sem, relued(i * 4 + (j + 1)))
            e.activation(dyn(hid.hi, i * 4 + j), rl[:, j % 2, :], ACT.Square).then_inc(hi.sem, 1)

        def vector(e, i, j):
            e.wait_ge(relued.sem, relued(i * 4 + (j + 1)))
            e.tensor_tensor(sq[:, j % 2, :], rl[:, j % 2, :], k.ps[:, j, :], ALU.mult).then_inc(free.sem, 1)
            e.wait_ge(free.sem, free(i * 4 + (j + 1 + RING)))
            e.wait_ge(hi.sem, hi(i * 4 + (j + 1)))
            e.tensor_tensor(dyn(hid.lo, i * 4 + j), sq[:, j % 2, :], as_float(dyn(hid.hi, i * 4 + j)), ALU.subtract
                            ).then_inc(lo.sem, 1)
        for n in range(2):
            linear(k, half, KD, hs, act=act, vector=vector, feed=None if n else Norm(k, "norm_mlp", hs, h))
            for s in (relued, hi, lo):
                s.base += half
            residual(k, half, hid, per=2, squares=(n == 1))



def time_mix_inputs(k, a, r, kk, vv, inner_w, inner_a, inner_g):
    nc = k.nc
    summed, root, inverse, normed, shifted, ld, mixed, sums, inner_r, xu = k.sig(
        "summed", "root", "inverse", "normed", "shifted", "lora_loaded", "mixed", "lora_sums", "lora_inner", "mix_used")
    with ExitStack() as st:
        tile = lambda name, *shape: st.enter_context(k.tile(name, [P, *shape], F32))
        h, xx, xm = tile("h", KD, T), tile("xx", KD, T), tile("xm", 4, T)
        with nc.Block() as block:
            @block.tensor
            def _(pe):
                pe.matmul(k.ps[:, 4, :], k.ones[:, :], k.squares[:, :], start=True, stop=True).then_inc(summed.sem, 1)

            @block.scalar
            def _(act):
                act.wait_ge(summed.sem, summed(1))
                act.activation(k.root[:, :], k.ps[:, 4, :], ACT.Sqrt, scale=1.0 / D, bias=k.bias[1e-6]).then_inc(root.sem, 1)

            @block.vector
            def _(v):
                v.wait_ge(root.sem, root(1))
                v.reciprocal(k.root[:, :], k.root[:, :]).then_inc(inverse.sem, 1)
                v.wait_ge(inverse.sem, inverse(1))
                for m in range(KD):
                    v.scalar_tensor_tensor(h[:, m, :], k.x[:, m, :], k.vec("mix0", m), k.root[:, :],
                                           ALU.mult, ALU.mult).then_inc(normed.sem, 1)
                for m in range(KD):
                    v.wait_ge(normed.sem, normed(m + 1))
                    v.tensor_tensor(xx[:, m, 1:T], h[:, m, 0:T - 1], h[:, m, 1:T], ALU.subtract).then_inc(shifted.sem, 1)
                v.tensor_scalar(xx[:, :, 0:1], h[:, :, 0:1], -1.0, None, ALU.mult).then_inc(shifted.sem, 1)
        for s, c in ((summed, 1), (root, 1), (inverse, 1), (normed, KD), (shifted, KD + 1)):
            s.base += c
        with ExitStack() as st2:
            xs = Split(st2, k, "xs", KD, T)
            for i, out in ((0, r), (2, kk), (3, vv)):
                linear(k, KD, KD, xs, act=copy_out(k, out), feed=Mix(k, h, xx, xm, xs, i))
        with k.tile("lora_a", [P, KD, 288], F32) as wa, nc.Block() as block:
            parts = [(1, 4, 0, 64), (4, 5, 64, 64), (5, 6, 128, P), (5, 7, 256, 32)]

            @block.sync
            def _(sp):
                sp.dma_start(wa[:, :, :], a["lora_a"]).then_inc(ld.sem, 16)

            @block.vector
            def _(v):
                for n, i in enumerate((1, 4, 5)):
                    for m in range(KD):
                        t = n * KD + m
                        if t >= 4:
                            v.wait_ge(xu.sem, xu(t - 3))
                        v.scalar_tensor_tensor(xm[:, t % 4, :], xx[:, m, :], k.vec("mu", 8 * i + m), h[:, m, :],
                                               ALU.mult, ALU.add).then_inc(mixed.sem, 1)

            @block.tensor
            def _(pe):
                pe.wait_ge(ld.sem, ld(16))
                for n, i in enumerate((1, 4, 5)):
                    for m in range(KD):
                        t = n * KD + m
                        pe.wait_ge(mixed.sem, mixed(t + 1))
                        for mu, bank, c, w in parts:
                            if mu == i:
                                mm = pe.matmul(k.ps[0:w, bank, :], wa[:, m, c:c + w], xm[:, t % 4, :], start=(m == 0),
                                               stop=(m == KD - 1))
                        mm.then_inc(xu.sem, 1)

            @block.scalar
            def _(act):
                act.wait_ge(xu.sem, xu(KD))
                act.activation(inner_w[0:64, :], k.ps[0:64, 4, :], ACT.Tanh).then_inc(inner_r.sem, 1)
                act.wait_ge(xu.sem, xu(2 * KD))
                act.activation(inner_a[0:64, :], k.ps[0:64, 5, :], ACT.Copy).then_inc(inner_r.sem, 1)
                act.wait_ge(xu.sem, xu(3 * KD))
                act.activation(inner_g[:, 0, :], k.ps[:, 6, :], ACT.Sigmoid).then_inc(inner_r.sem, 1)
                act.activation(inner_g[0:32, 1, :], k.ps[0:32, 7, :], ACT.Sigmoid).then_inc(inner_r.sem, 1)
        ld.base += 16
        mixed.base += 3 * KD
        xu.base += 3 * KD
        inner_r.base += 4


def low_rank_outputs(k, a, inner_w, inner_a, sg, aa):
    ld, s2, t2 = k.sig("lora_loaded", "lora_out", "lora_taken")
    with k.tile("lora_b", [P, 2, D], F32) as wb, k.nc.Block() as block:
        @block.sync
        def _(sp):
            sp.dma_start(wb[0:64, :, :], a["lora_b"][0:64, 0:2, :]).then_inc(ld.sem, 16)

        @block.tensor
        def _(pe):
            pe.wait_ge(ld.sem, ld(16))
            for n, src in enumerate((inner_w, inner_a)):
                for m in range(KD):
                    t = n * KD + m
                    if t >= 4:
                        pe.wait_ge(t2.sem, t2(t - 3))
                    pe.matmul(k.ps[:, 4 + t % 4, :], wb[0:64, n, m * P:(m + 1) * P], src[0:64, :], start=True, stop=True
                              ).then_inc(s2.sem, 1)

        @block.scalar
        def _(act):
            for n, (dst, bias) in enumerate(((sg, "w0"), (aa, "a0"))):
                for m in range(KD):
                    t = n * KD + m
                    act.wait_ge(s2.sem, s2(t + 1))
                    act.activation(dst[:, m, :], k.ps[:, 4 + t % 4, :], ACT.Sigmoid, bias=k.vec(bias, m)).then_inc(t2.sem, 1)
    ld.base += 16
    s2.base += 2 * KD
    t2.base += 2 * KD


def pair_products(k, p, r, kk, vv, sg, aa, buf):
    nc = k.nc
    (kkn, kn, ba, t0, t1, L, Em, AR, B, K, BT, KT, VT, M, Tm, Tt, U, Mo, S, Ss, Spc, W, SA, sm) = buf
    C = NB
    d, e, c, g = k.sig("pair_vector", "pair_tensor", "pair_scalar", "pair_pool")
    vo, eo, ao, po = d.sem, e.sem, c.sem, g.sem
    R_, K_, V_, S_, A_ = r[:, p, :], kk[:, p, :], vv[:, p, :], sg[:, p, :], aa[:, p, :]
    mid = 64

    def units(t, b):
        return t[:, 4 * b:4 * b + 4, 0:P]

    def bank(n):
        return k.ps[:, n, :].rearrange("p (u t) -> p u t", u=4)

    with nc.Block() as block:
        @block.vector
        def _(v):
            v.tensor_scalar(kkn[:, :], K_, k.vec("k_k", p), None, ALU.mult).then_inc(vo, 1)
            v.tensor_scalar(t0[:, :], A_, -1.0, k.vec("k_a", p), ALU.add, ALU.mult).then_inc(vo, 1)
            for i in range(C):
                v.tensor_tensor_scan(L[:, i, 1:P + 1], k.ones[:, :], S_[:, i * P:(i + 1) * P], 0.0, ALU.mult, ALU.add
                                     ).then_inc(vo, 1)
            v.wait_ge(vo, d(6))
            v.scalar_tensor_tensor(kn[:, :], t0[:, :], 1.0, K_, ALU.add, ALU.mult).then_inc(vo, 1)
            v.tensor_scalar(sm[:, 0:4], L[:, :, mid], DECAY, None, ALU.mult).then_inc(vo, 1)
            v.tensor_scalar(sm[:, 4:8], L[:, :, mid], -DECAY, None, ALU.mult).then_inc(vo, 1)
            v.wait_ge(vo, d(7))
            v.scalar_tensor_tensor(t0[:, :], R_, k.vec("r_k", p), kn[:, :], ALU.mult, ALU.mult).then_inc(vo, 1)
            v.wait_ge(ao, c(2))
            v.tensor_scalar(t1[:, :], t1[:, :], 1e-12, None, ALU.max).then_inc(vo, 1)
            v.wait_ge(vo, d(11))
            v.reciprocal(k.ps[:, 1, :], t1[:, :]).then_inc(vo, 1)
            v.wait_ge(vo, d(12))
            v.tensor_tensor(kkn[:, :], kkn[:, :], k.ps[:, 1, :], ALU.mult).then_inc(vo, 1)
            v.wait_ge(vo, d(13))
            v.tensor_tensor(ba[:, :], kkn[:, :], A_, ALU.mult).then_inc(vo, 1)
            v.wait_ge(eo, e(2))
            v.tensor_tensor(K_, V_, k.ps[:, 2, :], ALU.mult).then_inc(vo, 1)
            v.wait_ge(ao, c(12))
            v.scalar_tensor_tensor(AR[:, :, 0:P], kkn[:, :].rearrange("p (c t) -> p c t", c=C), -1.0, L[:, :, 0:P],
                                   ALU.mult, ALU.mult).then_inc(vo, 1)
            v.tensor_tensor(AR[:, :, P:2 * P], R_.rearrange("p (c t) -> p c t", c=C), L[:, :, 1:P + 1], ALU.mult
                            ).then_inc(vo, 1)
            v.wait_ge(vo, d(14))
            v.tensor_tensor(B[:, :, :], ba[:, :].rearrange("p (c t) -> p c t", c=C), Em[:, :, :], ALU.mult).then_inc(vo, 1)
            v.tensor_tensor(K[:, :, :], kn[:, :].rearrange("p (c t) -> p c t", c=C), Em[:, :, :], ALU.mult).then_inc(vo, 1)
            for q in range(8):
                v.wait_ge(eo, e(5 + q + 1))
                v.tensor_tensor(M[:, q, :], k.ps[:, 3 + q % 2, :], k.cst("m4", 512), ALU.mult).then_inc(vo, 1)
            lv = lambda n: k.consts[:, CST["levels"] + n * P:CST["levels"] + (n + 1) * P].unsqueeze(1).to_broadcast([P, 4, P])
            ident = k.ident.unsqueeze(1).to_broadcast([P, 4, P])
            for b in range(2):
                v.wait_ge(vo, d(23 + 4 * b))
                v.tensor_tensor(units(Tt, b), units(M, b), lv(0), ALU.mult).then_inc(vo, 1)
            for b in range(2):
                v.wait_ge(vo, d(28 + b))
                v.tensor_tensor(units(Tt, b), units(Tt, b), ident, ALU.add).then_inc(vo, 1)
            n = 31
            for l in range(1, 7):
                for b in range(2):
                    v.wait_ge(eo, e(15 + 6 * (l - 1) + 3 * b + 3))
                    v.tensor_tensor(units(Tt, b), units(Tt, b), bank(2 + 3 * b), ALU.add).then_inc(vo, 1)
                    if l < 6:
                        v.tensor_tensor(units(Tm, b), units(Tm, b), bank(1 + 3 * b), ALU.add).then_inc(vo, 1)
                        n += 1
                    n += 1
            assert n == 53
            v.memset(S[:, :], 0.0).then_inc(vo, 1)
            n = 54
            for i in range(C):
                v.wait_ge(vo, d(n))
                v.tensor_scalar(Ss[:, i % 2, :], S[:, :], sm[:, 8 + i:9 + i], None, ALU.mult).then_inc(vo, 1)
                v.tensor_scalar(Spc[:, :], S[:, :], sm[:, 12 + i:13 + i], None, ALU.mult).then_inc(vo, 1)
                v.wait_ge(eo, e(51 + 4 * i + 2))
                v.tensor_copy(SA[:, :], k.ps[:, 1, 0:P]).then_inc(vo, 1)
                v.wait_ge(eo, e(51 + 4 * i + 3))
                v.scalar_tensor_tensor(S[:, :], k.ps[:, 2, 0:64], L[:, i, P:P + 1], Spc[:, :], ALU.mult, ALU.add
                                       ).then_inc(vo, 1)
                n += 4
            assert n == 70

        @block.scalar
        def _(act):
            act.wait_ge(vo, d(1))
            act.activation(t1[:, :], kkn[:, :], ACT.Square).then_inc(ao, 1)
            act.wait_ge(eo, e(1))
            act.activation(t1[:, :], k.ps[:, 0, :], ACT.Sqrt).then_inc(ao, 1)
            act.wait_ge(vo, d(9))
            act.activation(sm[:, 8:12], L[:, :, mid], ACT.Exp, scale=-DECAY).then_inc(ao, 1)
            act.activation(sm[:, 12:16], L[:, :, P], ACT.Exp, scale=-DECAY).then_inc(ao, 1)
            for i in range(C):
                act.activation(Em[:, i, :], L[:, i, 1:P + 1], ACT.Exp, scale=DECAY, bias=sm[:, 4 + i:5 + i]).then_inc(ao, 1)
            act.wait_ge(ao, c(8))
            for i in range(C):
                act.activation(L[:, i, :], L[:, i, :], ACT.Exp, scale=-DECAY, bias=sm[:, i:i + 1]).then_inc(ao, 1)
            for i, dst in enumerate((BT, KT, VT)):
                act.wait_ge(eo, e(3 + i))
                act.activation(dst[:, :, :], bank(5 + i), ACT.Copy).then_inc(ao, 1)
            for b in range(2):
                act.wait_ge(eo, e(14 + b))
                act.activation(units(Tm, b), bank(3 * b), ACT.Copy).then_inc(ao, 1)
            for l in range(1, 7):
                for b in range(2):
                    act.wait_ge(eo, e(15 + 6 * (l - 1) + 3 * b + 1))
                    act.activation(units(U, b), bank(3 * b), ACT.Copy).then_inc(ao, 1)
            for i in range(C):
                act.wait_ge(eo, e(51 + 4 * i + 1))
                act.activation(W[:, :].rearrange("p (h j) -> p h j", h=2), k.ps[:, 0:5:4, 0:64], ACT.Copy).then_inc(ao, 1)
                act.wait_ge(eo, e(51 + 4 * i + 4))
                act.activation(R_[:, i * P:(i + 1) * P], k.ps[:, 3, 0:P], ACT.Copy).then_inc(ao, 1)

        @block.gpsimd
        def _(gp):
            for l in range(1, 7):
                for b in range(2):
                    gp.wait_ge(vo, d(23 + 4 * b))
                    if l > 1:
                        gp.wait_ge(eo, e(15 + 6 * (l - 2) + 3 * b + 1))
                    mask = k.consts[:, CST["levels"] + l * P:CST["levels"] + (l + 1) * P].unsqueeze(1).to_broadcast([P, 4, P])
                    gp.tensor_tensor(units(Mo, b), units(M, b), mask, ALU.mult).then_inc(po, 1)

        @block.tensor
        def _(pe):
            pe.wait_ge(ao, c(1))
            pe.matmul(k.ps[:, 0, :], k.blockones, t1[:, :], start=True, stop=True).then_inc(eo, 1)
            pe.wait_ge(vo, d(10))
            pe.matmul(k.ps[:, 2, :], k.blockones, t0[:, :], start=True, stop=True).then_inc(eo, 1)
            for i, src in enumerate((B, K, None)):
                if i < 2:
                    pe.wait_ge(vo, d(18 + i))
                for q in range(C):
                    s_ = V_[:, q * P:(q + 1) * P] if src is None else src[:, q, :]
                    mm = pe.transpose(bank(5 + i)[:, q, :], s_, k.ident)
                mm.then_inc(eo, 1)
            for q in range(8):
                i, o = q // 2, 64 * (q % 2)
                if q >= 2:
                    pe.wait_ge(vo, d(20 + q - 1))
                pe.matmul(k.ps[:, 3 + q % 2, 0:256], B[o:o + 64, i, :], AR[o:o + 64, i, :], start=True, stop=True)
                pe.matmul(k.ps[:, 3 + q % 2, 256:512], K[o:o + 64, i, :], AR[o:o + 64, i, :], start=True, stop=True
                          ).then_inc(eo, 1)
            for b in range(2):
                pe.wait_ge(vo, d(30 + b))
                if b:
                    pe.wait_ge(vo, d(27))
                for q in range(4):
                    mm = pe.transpose(bank(3 * b)[:, q, :], Tt[:, 4 * b + q, :], k.ident)
                mm.then_inc(eo, 1)
            pe.wait_ge(ao, c(15))
            for l in range(1, 7):
                for b in range(2):
                    pe.wait_ge(po, g(2 * (l - 1) + b + 1))
                    if l == 1:
                        pe.wait_ge(ao, c(16 + b))
                    else:
                        pe.wait_ge(vo, d(31 + 4 * (l - 2) + 2 * b + 2))
                    for q in range(4):
                        mm = pe.matmul(bank(3 * b)[:, q, :], Mo[:, 4 * b + q, :], Tm[:, 4 * b + q, :], start=True, stop=True)
                    mm.then_inc(eo, 1)
                    pe.wait_ge(ao, c(17 + 2 * (l - 1) + b + 1))
                    if l < 6:
                        for q in range(4):
                            mm = pe.matmul(bank(1 + 3 * b)[:, q, :], Tt[:, 4 * b + q, :], U[:, 4 * b + q, :], start=True, stop=True)
                        mm.then_inc(eo, 1)
                    else:
                        pe.sem_inc(eo, 1)
                    for q in range(4):
                        mm = pe.matmul(bank(2 + 3 * b)[:, q, :], U[:, 4 * b + q, :], Tt[:, 4 * b + q, :], start=True, stop=True)
                    mm.then_inc(eo, 1)
            pe.wait_ge(vo, d(53))
            for i in range(C):
                pe.wait_ge(vo, d(54 + 4 * i + 2))
                for hh in range(2):
                    o, q = 64 * hh, 2 * i + hh
                    pe.matmul(k.ps[:, 4 * hh, 0:64], AR[o:o + 64, i, 0:P], Ss[o:o + 64, i % 2, :], start=True, stop=False)
                    mm = pe.matmul(k.ps[:, 4 * hh, 0:64], M[:, q, 256:384], VT[:, i, o:o + 64], start=False, stop=True)
                mm.then_inc(eo, 1)
                pe.wait_ge(ao, c(29 + 2 * i + 1))
                for hh in range(2):
                    o, q = 64 * hh, 2 * i + hh
                    mm = pe.matmul(k.ps[:, 1, o:o + 64], Tt[:, q, :], W[:, o:o + 64], start=True, stop=True)
                mm.then_inc(eo, 1)
                pe.wait_ge(vo, d(54 + 4 * i + 3))
                for hh in range(2):
                    o = 64 * hh
                    pe.matmul(k.ps[o:o + 64, 2, 0:64], BT[:, i, o:o + 64], SA[:, o:o + 64], start=True, stop=False)
                    mm = pe.matmul(k.ps[o:o + 64, 2, 0:64], KT[:, i, o:o + 64], VT[:, i, o:o + 64], start=False, stop=True)
                mm.then_inc(eo, 1)
                if i:
                    pe.wait_ge(ao, c(29 + 2 * i))
                for hh in range(2):
                    o, q = 64 * hh, 2 * i + hh
                    pe.matmul(k.ps[o:o + 64, 3, 0:P], Ss[o:o + 64, i % 2, :], AR[o:o + 64, i, P:2 * P], start=True, stop=False)
                    pe.matmul(k.ps[o:o + 64, 3, 0:P], SA[:, o:o + 64], M[:, q, 128:256], start=False, stop=False)
                    mm = pe.matmul(k.ps[o:o + 64, 3, 0:P], VT[:, i, o:o + 64], M[:, q, 384:512], start=False, stop=True)
                mm.then_inc(eo, 1)
    d.base += 70
    e.base += 51 + 16
    c.base += 29 + 8
    g.base += 12


def group_norm_and_gate(k, a, y, bonus, inner, z):
    nc = k.nc
    ld, go = k.sig("lora_loaded", "lora_out")
    me, ce, sq, va, rt, iv, n1, n2, nd = k.sig("gn_mean", "gn_centred", "gn_squared", "gn_var", "gn_root", "gn_inverse",
                                                "gn_scaled", "gn_shifted", "gn_done")
    with k.tile("gwb", [P, 2, D], F32) as wb, k.tile("gsq", [P, 2, T], F32) as sqt, \
         k.tile("grt", [P, 2, T], F32) as rtt, nc.Block() as block:
        @block.sync
        def _(sp):
            sp.dma_start(wb[:, :, :], a["lora_b"][:, 2:4, :]).then_inc(ld.sem, 16)

        @block.vector
        def _(v):
            for m in range(KD):
                v.wait_ge(me.sem, me(m + 1))
                v.scalar_tensor_tensor(y[:, m, :], k.ps[:, m % 2, :], -1.0 / 64, y[:, m, :], ALU.mult, ALU.add
                                       ).then_inc(ce.sem, 1)
                v.wait_ge(rt.sem, rt(m + 1))
                v.reciprocal(k.ps[:, 4, :], rtt[:, m % 2, :]).then_inc(iv.sem, 1)
                v.wait_ge(iv.sem, iv(m + 1))
                v.scalar_tensor_tensor(y[:, m, :], y[:, m, :], k.vec("ln_g", m), k.ps[:, 4, :], ALU.mult, ALU.mult
                                       ).then_inc(n1.sem, 1)
                v.wait_ge(n1.sem, n1(m + 1))
                v.scalar_tensor_tensor(y[:, m, :], y[:, m, :], k.vec("ln_b", m), bonus[:, m, :], ALU.add, ALU.add
                                       ).then_inc(n2.sem, 1)
                v.wait_ge(n2.sem, n2(m + 1))
                v.wait_ge(go.sem, go(m + 1))
                v.tensor_tensor(z[:, m, :], y[:, m, :], k.ps[:, 5 + m % 2, :], ALU.mult).then_inc(nd.sem, 1)

        @block.tensor
        def _(pe):
            pe.wait_ge(ld.sem, ld(16))

            def mean(m):
                if m >= 2:
                    pe.wait_ge(ce.sem, ce(m - 1))
                pe.matmul(k.ps[:, m % 2, :], k.blockones, y[:, m, :], start=True, stop=True).then_inc(me.sem, 1)
            mean(0)
            for m in range(KD):
                if m + 1 < KD:
                    mean(m + 1)
                if m >= 2:
                    pe.wait_ge(nd.sem, nd(m - 1))
                pe.matmul(k.ps[:, 5 + m % 2, :], wb[:, 0, m * P:(m + 1) * P], inner[:, 0, :], start=True, stop=False)
                pe.matmul(k.ps[:, 5 + m % 2, :], wb[0:32, 1, m * P:(m + 1) * P], inner[0:32, 1, :], start=False, stop=True
                          ).then_inc(go.sem, 1)
                pe.wait_ge(sq.sem, sq(m + 1))
                if m >= 2:
                    pe.wait_ge(rt.sem, rt(m - 1))
                pe.matmul(k.ps[:, 2 + m % 2, :], k.blockones, sqt[:, m % 2, :], start=True, stop=True).then_inc(va.sem, 1)

        @block.scalar
        def _(act):
            for m in range(KD):
                act.wait_ge(ce.sem, ce(m + 1))
                if m >= 2:
                    act.wait_ge(va.sem, va(m - 1))
                act.activation(sqt[:, m % 2, :], y[:, m, :], ACT.Square).then_inc(sq.sem, 1)
                act.wait_ge(va.sem, va(m + 1))
                if m >= 2:
                    act.wait_ge(iv.sem, iv(m - 1))
                act.activation(rtt[:, m % 2, :], k.ps[:, 2 + m % 2, :], ACT.Sqrt, scale=1.0 / 64, bias=k.bias[64e-5]
                               ).then_inc(rt.sem, 1)
    ld.base += 16
    for s in (me, ce, sq, va, rt, iv, n1, n2, nd, go):
        s.base += KD


def rwkv(k, a, ring):
    nc = k.nc
    with ExitStack() as outer:
        tile = lambda st, name, *shape: st.enter_context(k.tile(name, [P, *shape], F32))
        r, kk, vv = (tile(outer, n, KD, T) for n in ("r", "kk", "vv"))
        inner_g, inner_w, inner_a = tile(outer, "inner_g", 2, T), tile(outer, "inner_w", T), tile(outer, "inner_a", T)
        with ExitStack() as first:
            open_ring(k, first, 3 * KD)
            time_mix_inputs(k, a, r, kk, vv, inner_w, inner_a, inner_g)
            close_ring(k)
        with ExitStack() as stack:
            sg, aa = tile(stack, "sg", KD, T), tile(stack, "aa", KD, T)
            low_rank_outputs(k, a, inner_w, inner_a, sg, aa)
            sb = lambda name, *shape: tile(stack, f"pair_{name}", *shape)
            buf = [sb("kkn", T), sb("kn", T), sb("ba", T), sb("t0", T), sb("t1", T), sb("L", NB, P + 1),
                   sb("Em", NB, P), sb("AR", NB, 2 * P), sb("B", NB, P), sb("K", NB, P), sb("BT", NB, P),
                   sb("KT", NB, P), sb("VT", NB, P), sb("M", 8, T), sb("Tm", 8, P), sb("Tt", 8, P), sb("U", 8, P),
                   sb("Mo", 8, P), sb("S", 64), sb("Ss", 2, 64), sb("Spc", 64), sb("W", P), sb("SA", P), sb("sm", 16)]
            L = buf[5]
            zeroed = k.sig("zeroed")
            for p in range(KD):
                with nc.Block() as block:
                    @block.gpsimd
                    def _(g):
                        g.memset(L[:, :, 0:1], 0.0).then_inc(zeroed.sem, 1)
                pair_products(k, p, r, kk, vv, sg, aa, buf)
        with ExitStack() as last:
            z = tile(last, "z", KD, T)
            group_norm_and_gate(k, a, r, kk, inner_g, z)
            open_ring(k, last, KD)
            zs = Split(last, k, "z", KD, T)
            split_tiles(k, z, zs, KD)
            residual(k, KD, zs)
            close_ring(k)



def norm_memory(k, mem):
    squared, summed, root, inverse, normed = k.sig("squared", "summed", "root", "inverse", "normed")
    with k.tile("sqm", [P, KD, MEM], F32) as sq, k.nc.Block() as block:
        @block.scalar
        def _(act):
            for m in range(KD):
                act.activation(sq[:, m, :], mem[:, m, :], ACT.Square).then_inc(squared.sem, 1)
            act.wait_ge(summed.sem, summed(1))
            act.activation(k.root[:, 0:MEM], k.ps[:, 4, 0:MEM], ACT.Sqrt, scale=1.0 / D, bias=k.bias[1e-6]
                           ).then_inc(root.sem, 1)

        @block.tensor
        def _(pe):
            for m in range(KD):
                pe.wait_ge(squared.sem, squared(m + 1))
                mm = pe.matmul(k.ps[:, 4, 0:MEM], k.ones[:, :], sq[:, m, :], start=(m == 0), stop=(m == KD - 1))
            mm.then_inc(summed.sem, 1)

        @block.vector
        def _(v):
            v.wait_ge(root.sem, root(1))
            v.reciprocal(k.root[:, 0:MEM], k.root[:, 0:MEM]).then_inc(inverse.sem, 1)
            v.wait_ge(inverse.sem, inverse(1))
            for m in range(KD):
                v.scalar_tensor_tensor(mem[:, m, :], mem[:, m, :], k.vec("mem_norm", m), k.root[:, 0:MEM],
                                       ALU.mult, ALU.mult).then_inc(normed.sem, 1)
    for s, c in ((squared, KD), (summed, 1), (root, 1), (inverse, 1), (normed, KD)):
        s.base += c


def cross_attention(k, a, layer):
    nc = k.nc
    ml = k.sig("memory_loaded")
    with k.tile("km", [P, KD, MEM], F32) as km, k.tile("vt", [P, 2, D], F32) as vt:
        with k.tile("mem", [P, KD, MEM], F32) as mem, k.tile("kvm", [P, 2 * KD, MEM], F32) as kv:
            with nc.Block() as block:
                @block.sync
                def _(sp):
                    sp.dma_start(mem[:, :, :], a["mem"]).then_inc(ml.sem, 16)
                    sp.wait_ge(ml.sem, ml(16))
            ml.base += 16
            norm_memory(k, mem)
            with ExitStack() as st:
                ms = Split(st, k, "ms", KD, MEM)
                linear(k, 2 * KD, KD, ms, act=copy_out(k, kv, width=MEM), width=MEM, feed=Parts(k, mem, ms, KD))
            tr, te, kc = k.sig("transposed", "transposed_out", "keys_copied")
            with nc.Block() as block:
                @block.tensor
                def _(pe):
                    for n in range(4):
                        mb, half = n % 2, n // 2
                        for q in range(4):
                            mm = pe.transpose(k.ps[:, n, q * P:(q + 1) * P], kv[:, KD + 4 * half + q, mb * P:(mb + 1) * P], k.ident)
                        mm.then_inc(tr.sem, 1)

                @block.scalar
                def _(act):
                    for n in range(4):
                        act.wait_ge(tr.sem, tr(n + 1))
                        act.activation(vt[:, n % 2, (n // 2) * 512:(n // 2) * 512 + 512], k.ps[:, n, :], ACT.Copy
                                       ).then_inc(te.sem, 1)

                @block.gpsimd
                def _(g):
                    g.tensor_copy(km[:, :, :], kv[:, 0:KD, :]).then_inc(kc.sem, 1)
            tr.base += 4
            te.base += 4
            kc.base += 1
        with k.tile("q", [P, KD, T], F32) as q_, k.tile("o", [P, KD, T], F32) as o_:
            with ExitStack() as st:
                h = st.enter_context(k.tile("h", [P, KD, T], F32))
                hs = Split(st, k, "h", KD, T)
                linear(k, KD, KD, hs, act=copy_out(k, q_, scale=1.0 / 16), feed=Norm(k, f"xattn{layer}", hs, h))
            sc, mx, ex, rc, wt, tr, te, po, oe = k.sig("scores", "maxima", "exps", "sums_inverted", "scaled", "transposed",
                                                       "transposed_out", "pv_done", "mixer_out")
            with k.tile("xp", [P, 4, MEM], F32) as p, k.tile("xpt", [P, 2, 2, T], F32) as pt, \
                 k.tile("xst", [P, 3, 16], F32) as st, nc.Block() as block:
                U = 16

                @block.tensor
                def _(pe):
                    def scores(u):
                        h, qb = u // 4, u % 4
                        if u >= 2:
                            pe.wait_ge(ex.sem, ex(u - 1))
                        for c in range(2):
                            mm = pe.matmul(k.ps[:, u % 2, 0:MEM], q_[:, 2 * h + c, qb * P:(qb + 1) * P],
                                           km[:, 2 * h + c, :], start=(c == 0), stop=(c == 1))
                        mm.then_inc(sc.sem, 1)

                    def turn(u):
                        pe.wait_ge(wt.sem, wt(u + 1))
                        if u >= 2:
                            pe.wait_ge(te.sem, te(u - 1))
                        for mb in range(2):
                            mm = pe.transpose(k.ps[:, 2 + u % 2, mb * P:(mb + 1) * P], p[:, u % 4, mb * P:(mb + 1) * P], k.ident)
                        mm.then_inc(tr.sem, 1)

                    def values(h):
                        pe.wait_ge(te.sem, te(4 * h + 4))
                        for db in range(2):
                            if h >= 1:
                                pe.wait_ge(oe.sem, oe(2 * h + db - 1))
                            for mb in range(2):
                                mm = pe.matmul(k.ps[:, 4 + db, :], vt[:, mb, h * 256 + db * P:h * 256 + (db + 1) * P],
                                               pt[:, h % 2, mb, :], start=(mb == 0), stop=(mb == 1))
                            mm.then_inc(po.sem, 1)
                    scores(0)
                    scores(1)
                    for u in range(U):
                        if u + 2 < U:
                            scores(u + 2)
                        turn(u)
                        if u % 4 == 0 and u:
                            values(u // 4 - 1)
                    values(3)

                @block.vector
                def _(v):
                    def out(n):
                        v.wait_ge(po.sem, po(n + 1))
                        v.tensor_copy(o_[:, n, :], k.ps[:, 4 + n % 2, :]).then_inc(oe.sem, 1)

                    def maximum(u):
                        v.wait_ge(sc.sem, sc(u + 1))
                        v.tensor_reduce(st[:, 0, u:u + 1], k.ps[:, u % 2, 0:MEM], AX.X, ALU.max, negate=True
                                        ).then_inc(mx.sem, 1)
                    maximum(0)
                    for u in range(U):
                        if u + 1 < U:
                            maximum(u + 1)
                        v.wait_ge(ex.sem, ex(u + 1))
                        v.reciprocal(st[:, 2, u:u + 1], st[:, 1, u:u + 1]).then_inc(rc.sem, 1)
                        v.wait_ge(rc.sem, rc(u + 1))
                        v.tensor_scalar(p[:, u % 4, :], p[:, u % 4, :], st[:, 2, u:u + 1], None, ALU.mult).then_inc(wt.sem, 1)
                        if u % 4 == 1 and u > 4:
                            out(2 * (u // 4 - 1))
                            out(2 * (u // 4 - 1) + 1)
                    out(6)
                    out(7)

                @block.scalar
                def _(act):
                    def exp(u):
                        act.wait_ge(mx.sem, mx(u + 1))
                        if u >= 4:
                            act.wait_ge(tr.sem, tr(u - 3))
                        act.activation(p[:, u % 4, :], k.ps[:, u % 2, 0:MEM], ACT.Exp, bias=st[:, 0, u:u + 1],
                                       accum_out=st[:, 1, u:u + 1]).then_inc(ex.sem, 1)

                    def take(u):
                        h, qb = u // 4, u % 4
                        act.wait_ge(tr.sem, tr(u + 1))
                        if h >= 2:
                            act.wait_ge(po.sem, po(2 * (h - 1)))
                        act.activation(pt[:, h % 2, :, qb * P:(qb + 1) * P],
                                       k.ps[:, 2 + u % 2, 0:MEM].rearrange("p (m t) -> p m t", m=2), ACT.Copy
                                       ).then_inc(te.sem, 1)
                    exp(0)
                    for u in range(U):
                        if u + 1 < U:
                            exp(u + 1)
                        take(u)
            for s in (sc, mx, ex, rc, wt, tr, te):
                s.base += U
            po.base += 8
            oe.base += 8
            with ExitStack() as st:
                os_ = Split(st, k, "os", KD, T)
                split_tiles(k, o_, os_, KD)
                residual(k, KD, os_)



def conformer(k, a):
    nc = k.nc
    used, free, sig_r, dg, padz = k.sig("chunk_used", "bank_free", "sigmoid_made", "diagonals", "zeroed")
    V_TAPS = TAPS - PE_TAPS
    with k.tile("conv_y", [P, KD, T], F32) as y:
        with k.tile("conv_u", [P, KD, T + TAPS - 1], F32) as u, \
             k.tile("conv_dg", [P, 2, PE_TAPS, P], F32) as diag, k.tile("conv_s", [P, 2, T], F32) as sg:
            def act(e, i, j):
                if j % 2 == 0:
                    return
                f = 2 * i + j // 2
                e.wait_ge(used.sem, used(2 * f + 2))
                if f >= 2:
                    e.wait_ge(free.sem, free(2 * (f - 1) + RING))
                e.activation(sg[:, f % 2, :], k.ps[:, j, :], ACT.Sigmoid, bias=k.vec("cb_in", 8 + f)).then_inc(sig_r.sem, 1)

            def vector(e, i, j):
                if j % 2 == 0:
                    return
                f = 2 * i + j // 2
                e.wait_ge(sig_r.sem, sig_r(f + 1))
                e.scalar_tensor_tensor(u[:, f, TAPS - 1:], k.ps[:, j - 1, :], k.vec("cb_in", f), sg[:, f % 2, :],
                                       ALU.add, ALU.mult).then_inc(free.sem, 2)

            with ExitStack() as st:
                h = st.enter_context(k.tile("h", [P, KD, T], F32))
                hs = Split(st, k, "h", KD, T)
                linear(k, 2 * KD, KD, hs, act=act, vector=vector, unroll=True, feed=Norm(k, "mix1", hs, h))
            sig_r.base += KD
            tp, ac, ye = k.sig("taps_summed", "taps_added", "conv_taken")
            with nc.Block() as block:
                @block.gpsimd
                def _(g):
                    g.memset(u[:, :, 0:TAPS - 1], 0.0).then_inc(padz.sem, 1)
                    for m in range(KD):
                        if m >= 2:
                            g.wait_ge(tp.sem, tp(m - 1))
                        for t in range(PE_TAPS):
                            c = VEC["cdw"] + TAPS * m + t
                            g.tensor_scalar(diag[:, m % 2, t, :], k.ident, k.vecs[:, c:c + 1], None, ALU.mult
                                            ).then_inc(dg.sem, 1)

                @block.tensor
                def _(pe):
                    pe.wait_ge(padz.sem, padz(1))
                    for m in range(KD):
                        if m >= 4:
                            pe.wait_ge(ye.sem, ye(m - 3))
                        for t in range(PE_TAPS):
                            pe.wait_ge(dg.sem, dg(m * PE_TAPS + t + 1))
                            mm = pe.matmul(k.ps[:, m % 4, :], diag[:, m % 2, t, :], u[:, m, t:t + T], start=(t == 0),
                                           stop=(t == PE_TAPS - 1))
                        mm.then_inc(tp.sem, 1)

                @block.vector
                def _(v):
                    n = 0
                    for pair in range(KD // 2):
                        v.wait_ge(tp.sem, tp(2 * pair + 2))
                        for t in range(PE_TAPS, TAPS):
                            for m in (2 * pair, 2 * pair + 1):
                                if t > PE_TAPS:
                                    v.wait_ge(ac.sem, ac(n - 1))
                                c = VEC["cdw"] + TAPS * m + t
                                v.scalar_tensor_tensor(k.ps[:, m % 4, :], u[:, m, t:t + T], k.vecs[:, c:c + 1],
                                                       k.ps[:, m % 4, :], ALU.mult, ALU.add).then_inc(ac.sem, 1)
                                n += 1

                @block.scalar
                def _(act):
                    for m in range(KD):
                        act.wait_ge(ac.sem, ac((m // 2) * 2 * V_TAPS + 2 * V_TAPS - (1 - m % 2)))
                        act.activation(y[:, m, :], k.ps[:, m % 4, :], ACT.Identity, bias=k.vec("cdw_b", m)).then_inc(ye.sem, 1)
            padz.base += 1
            dg.base += KD * PE_TAPS
            tp.base += KD
            ac.base += KD * V_TAPS
            ye.base += KD
        me, ce, sq, va, rt, iv, n1, n2 = k.sig("gn_mean", "gn_centred", "gn_squared", "gn_var", "gn_root", "gn_inverse",
                                               "gn_scaled", "gn_shifted")
        with k.tile("ln_sq", [P, KD, T], F32) as sqt, k.tile("ln_rt", [P, T], F32) as rtt, \
             nc.Block() as block:
            @block.tensor
            def _(pe):
                for m in range(KD):
                    mm = pe.matmul(k.ps[:, 4, :], k.ones[:, :], y[:, m, :], start=(m == 0), stop=(m == KD - 1))
                mm.then_inc(me.sem, 1)
                for m in range(KD):
                    pe.wait_ge(sq.sem, sq(m + 1))
                    mm = pe.matmul(k.ps[:, 5, :], k.ones[:, :], sqt[:, m, :], start=(m == 0), stop=(m == KD - 1))
                mm.then_inc(va.sem, 1)

            @block.vector
            def _(v):
                v.wait_ge(me.sem, me(1))
                for m in range(KD):
                    v.scalar_tensor_tensor(y[:, m, :], k.ps[:, 4, :], -1.0 / D, y[:, m, :], ALU.mult, ALU.add
                                           ).then_inc(ce.sem, 1)
                v.wait_ge(rt.sem, rt(1))
                v.reciprocal(k.ps[:, 6, :], rtt[:, :]).then_inc(iv.sem, 1)
                v.wait_ge(iv.sem, iv(1))
                for m in range(KD):
                    v.scalar_tensor_tensor(y[:, m, :], y[:, m, :], k.vec("cln_g", m), k.ps[:, 6, :], ALU.mult, ALU.mult
                                           ).then_inc(n1.sem, 1)

            @block.scalar
            def _(act):
                for m in range(KD):
                    act.wait_ge(ce.sem, ce(m + 1))
                    act.activation(sqt[:, m, :], y[:, m, :], ACT.Square).then_inc(sq.sem, 1)
                act.wait_ge(va.sem, va(1))
                act.activation(rtt[:, :], k.ps[:, 5, :], ACT.Sqrt, scale=1.0 / D, bias=k.bias[1e-5]).then_inc(rt.sem, 1)
                for m in range(KD):
                    act.wait_ge(n1.sem, n1(m + 1))
                    act.activation(y[:, m, :], y[:, m, :], ACT.Silu, bias=k.vec("cln_b", m)).then_inc(n2.sem, 1)
        me.base += 1
        va.base += 1
        rt.base += 1
        iv.base += 1
        for s in (ce, sq, n1, n2):
            s.base += KD
        with ExitStack() as st:
            ys = Split(st, k, "ys", KD, T)
            split_tiles(k, y, ys, KD)
            residual(k, KD, ys, bias="cb_out")


def conv_ffn(k, layer):
    nc = k.nc
    used, free, ub_r, cv, silu, hi, lo, padz = k.sig(
        "chunk_used", "bank_free", "ffn_copied", "ffn_conv", "ffn_silu", "hidden_hi", "hidden_lo", "zeroed")
    w0 = VEC[f"fdw{layer}"]
    with ExitStack() as st:
        h = st.enter_context(k.tile("h", [P, KD, T], F32))
        hs = Split(st, k, "h", KD, T)
        a_ = Split(st, k, "ffn_a", FFN_PARTS[0], T)
        ub = st.enter_context(k.tile("ffn_u", [P, 4, T + 2], F32))
        sg = st.enter_context(k.tile("ffn_s", [P, 2, T], F32))
        tmp = st.enter_context(k.tile("ffn_t", [P, 2, T], F32))
        with nc.Block() as block:
            @block.gpsimd
            def _(g):
                g.memset(ub[:, :, 0:2], 0.0).then_inc(padz.sem, 1)
        padz.base += 1
        before = 0
        for part, FT in enumerate(FFN_PARTS):
            def act(e, i, j):
                m, f = 4 * i + j, 2 * i + j // 2
                e.wait_ge(used.sem, used(m + 1))
                if m >= 4:
                    e.wait_ge(cv.sem, cv(6 * ((m - 4) // 2) + 5 + m % 2))
                e.activation(ub[:, j, 2:T + 2], k.ps[:, j, :], ACT.Copy).then_inc(ub_r.sem, 1)
                if j % 2:
                    e.wait_ge(cv.sem, cv(6 * f + 6))
                    e.activation(sg[:, f % 2, :], k.ps[:, j - 1, :], ACT.Silu).then_inc(silu.sem, 1)
                    e.wait_ge(free.sem, free(2 * f + 2 + RING))
                    e.activation(a_.hi[:, f, :], tmp[:, f % 2, :], ACT.Copy).then_inc(hi.sem, 1)

            def vector(e, i, j):
                if j % 2 == 0:
                    return
                f = 2 * i + j // 2
                for t in (2, 1, 0):
                    for jj in range(2):
                        m = 2 * f + jj
                        bank = k.ps[:, m % 4, :]
                        c = w0 + 3 * (2 * before + m) + t
                        col = k.vecs[:, c:c + 1]
                        if t == 2:
                            e.wait_ge(ub_r.sem, ub_r(m + 1))
                            e.tensor_scalar(bank, bank, col, None, ALU.mult).then_inc(cv.sem, 1)
                        else:
                            e.wait_ge(cv.sem, cv(6 * f + 2 * (2 - t) + jj - 1))
                            e.scalar_tensor_tensor(bank, ub[:, m % 4, t:t + T], col, bank, ALU.mult, ALU.add
                                                   ).then_inc(cv.sem, 1)
                e.wait_ge(silu.sem, silu(f + 1))
                e.tensor_tensor(tmp[:, f % 2, :], sg[:, f % 2, :], k.ps[:, j, :], ALU.mult).then_inc(free.sem, 2)
                e.wait_ge(hi.sem, hi(f + 1))
                e.tensor_tensor(a_.lo[:, f, :], tmp[:, f % 2, :], as_float(a_.hi[:, f, :]), ALU.subtract).then_inc(lo.sem, 1)
            linear(k, 2 * FT, KD, hs, act=act, vector=vector, unroll=True,
                   feed=None if part else Norm(k, f"ffn{layer}", hs, h))
            ub_r.base += 2 * FT
            cv.base += 6 * FT
            for s in (silu, hi, lo):
                s.base += FT
            residual(k, FT, a_, per=2, squares=(part == 1))
            before += FT


def final_norm(k):
    summed, root, inverse, normed = k.sig("summed", "root", "inverse", "normed")
    with k.nc.Block() as block:
        @block.tensor
        def _(pe):
            pe.matmul(k.ps[:, 4, :], k.ones[:, :], k.squares[:, :], start=True, stop=True).then_inc(summed.sem, 1)

        @block.scalar
        def _(act):
            act.wait_ge(summed.sem, summed(1))
            act.activation(k.root[:, :], k.ps[:, 4, :], ACT.Sqrt, scale=1.0 / D, bias=k.bias[1e-6]).then_inc(root.sem, 1)

        @block.vector
        def _(v):
            v.wait_ge(root.sem, root(1))
            v.reciprocal(k.root[:, :], k.root[:, :]).then_inc(inverse.sem, 1)
            v.wait_ge(inverse.sem, inverse(1))
            for m in range(KD):
                v.scalar_tensor_tensor(k.x[:, m, :], k.x[:, m, :], k.vec("final", m), k.root[:, :],
                                       ALU.mult, ALU.mult).then_inc(normed.sem, 1)
    for s, c in ((summed, 1), (root, 1), (inverse, 1), (normed, KD)):
        s.base += c


def second_block(k, a, stop):
    first = START if START else 2
    if first < 3:
        rwkv(k, a, None)
    if stop == 3:
        return
    with ExitStack() as ring:
        open_ring(k, ring, k.n_chunks - k.chunk)
        if first < 4:
            cross_attention(k, a, 0)
        if stop == 4:
            return
        if first < 5:
            conv_ffn(k, 0)
        if stop == 5:
            return
        if first < 6:
            conformer(k, a)
        if stop == 6:
            return
        if first < 7:
            cross_attention(k, a, 1)
        if stop == 7:
            return
        conv_ffn(k, 1)
        if stop == 8:
            return
        final_norm(k)
        close_ring(k)



def build(nc, a, out, stop=None):
    k = Core(nc)
    k.wall = a["wall"]
    k.n_chunks = a["wall"].shape[0]
    k.x = nc.alloc_sbuf_tensor("x_stream", [P, KD, T], F32)
    k.squares = nc.alloc_sbuf_tensor("squares", [P, T], F32)
    k.root = nc.alloc_sbuf_tensor("root", [P, T], F32)
    k.vecs = nc.alloc_sbuf_tensor("vecs", [P, N_VEC], F32)
    k.consts = nc.alloc_sbuf_tensor("consts", [P, N_KEEP], F32)
    k.ones = nc.alloc_sbuf_tensor("ones", [P, P], F32)
    k.negones = nc.alloc_sbuf_tensor("negones", [P, P], F32)
    k.eps = nc.alloc_sbuf_tensor("eps", [P, 8], F32)
    k.ps = nc.alloc_psum_tensor("ps", [P, 8, 512], F32)
    k.ident = k.cst("ident", 128)
    k.blockones = k.cst("blockones", 128)
    k.negtri = k.cst("negtri", 128)
    if START:
        c0 = {2: 96, 3: 128, 4: 160, 5: 160 + 76, 6: 160 + 76 + 24, 7: 160 + 76 + 24 + 32}[START]
        k.wall = a["wall"][c0:]
        k.n_chunks -= c0
    load_everything(k, a)
    if not START:
        with ExitStack() as ring:
            open_ring(k, ring, N_PROJ + KD + 64)
            first_block(k, a, stop)
            if stop != 1:
                close_ring(k)
    if stop not in (1, 2):
        second_block(k, a, stop)
    stored = k.sig("stored")
    with nc.Block() as block:
        @block.sync
        def _(sp):
            sp.dma_start(out, k.x[:, :, :]).then_inc(stored.sem, 16)
            sp.wait_ge(stored.sem, stored(16))


def chunks(w):
    K, M = w.shape
    per = -(-K // 1024)
    full = np.zeros((per * 1024, M), w.dtype)
    full[:K] = w
    return np.ascontiguousarray(full.reshape(per, 8, P, M // P, P).transpose(3, 0, 2, 1, 4)).reshape(-1, P, 1024)


def interleave(w, pairs):
    K = w.shape[0]
    return w.reshape(K, 2, pairs, P).transpose(0, 2, 1, 3).reshape(K, -1)


def layout(i):
    c = lambda *s: np.arange(*s)
    w_in = np.asarray(i["w_in"])[0]
    q0, kv0, g0, d0, s0 = 0, 256, 640, 652, 1804
    kv = lambda n: c(kv0 + 64 * n, kv0 + 64 * n + 64)
    cols = np.concatenate([c(0, 256), kv(0), kv(1), kv(2), kv(2), kv(4), kv(4), kv(3), kv(5), c(d0, s0), c(s0, s0 + 1152)])
    n = {m: np.asarray(v) for m, v in i.items()}
    fw = lambda l: interleave(n["ffn_w_in_2"][l], F2 // P)
    cut = FFN_PARTS[0] * P
    ffn = lambda l: [fw(l)[:, :2 * cut], n["ffn_w_out_2"][l][:cut], fw(l)[:, 2 * cut:], n["ffn_w_out_2"][l][cut:]]
    wall = np.concatenate([chunks(w) for w in [
        w_in[:, cols], n["w_out"][0],
        n["w_up"][0][:, :F1 // 2], n["w_down"][0][:F1 // 2], n["w_up"][0][:, F1 // 2:], n["w_down"][0][F1 // 2:],
        n["rwkv_w_r_2"][0], n["rwkv_w_k_2"][0], n["rwkv_w_v_2"][0], n["rwkv_w_o_2"][0],
        n["xattn_w_kv_2"][0], n["xattn_w_q_2"][0], n["xattn_w_o_2"][0], *ffn(0),
        interleave(n["conv_w_in_2"][0], 8), n["conv_w_out_2"][0],
        n["xattn_w_kv_2"][1], n["xattn_w_q_2"][1], n["xattn_w_o_2"][1], *ffn(1)]])
    col = lambda v: v.reshape(-1, P).T
    fdw = lambda l: n["ffn_dw_2"][l].reshape(3, 2, F2 // P, P).transpose(3, 2, 1, 0).reshape(P, -1)
    gains = np.concatenate([n["qk_gain_nsa"][0], n["qk_gain_dil"][0]])
    vecs = {"norm_mix": col(n["norm_mix"][0]), "norm_mlp": col(n["norm_mlp"][0]), "mem_norm": col(n["mem_norm_g_2"]),
            "mix0": col(n["norm_mix_g_2"][0]), "mix1": col(n["norm_mix_g_2"][1]),
            "xattn0": col(n["norm_xattn_g_2"][0]), "xattn1": col(n["norm_xattn_g_2"][1]),
            "ffn0": col(n["norm_ffn_g_2"][0]), "ffn1": col(n["norm_ffn_g_2"][1]), "final": col(n["final_norm_g_2"]),
            "mu": col(n["rwkv_mu_2"][0]), "w0": col(n["rwkv_w0_2"][0]), "a0": col(n["rwkv_a0_2"][0]),
            "k_k": col(n["rwkv_k_k_2"][0]), "k_a": col(n["rwkv_k_a_2"][0]), "r_k": col(n["rwkv_r_k_2"][0]),
            "ln_g": col(n["rwkv_ln_g_2"][0]), "ln_b": col(n["rwkv_ln_b_2"][0]), "cb_in": col(n["conv_b_in_2"][0]),
            "cdw": n["conv_dw_2"][0].reshape(TAPS, 8, P).transpose(2, 1, 0).reshape(P, -1),
            "cdw_b": col(n["conv_dw_b_2"][0]), "cln_g": col(n["conv_ln_g_2"][0]), "cln_b": col(n["conv_ln_b_2"][0]),
            "cb_out": col(n["conv_b_out_2"][0]), "fdw0": fdw(0), "fdw1": fdw(1),
            "gains": np.concatenate([gains, gains], axis=1).T}
    act = lambda x: np.ascontiguousarray(x.T.reshape(KD, P, -1).transpose(1, 0, 2))
    lora_a = np.concatenate([n["rwkv_w1_2"][0], n["rwkv_a1_2"][0], n["rwkv_g1_2"][0]], axis=1)
    lora_b = np.zeros((4, P, D), lora_a.dtype)
    lora_b[0, :64], lora_b[1, :64] = n["rwkv_w2_2"][0], n["rwkv_a2_2"][0]
    lora_b[2], lora_b[3, :32] = n["rwkv_g2_2"][0][:P], n["rwkv_g2_2"][0][P:]
    w2 = n["cmp_w2"][0]
    return {
        "x": act(n["x"][0]), "mem": act(n["mem_2"][0]), "wall": wall,
        "vecs": np.ascontiguousarray(np.concatenate([vecs[m] for m, _ in VEC_SIZES], axis=1)),
        "consts": constants(),
        "w_gate": np.ascontiguousarray(w_in[:, g0:d0].reshape(KD, P, 12).transpose(1, 0, 2)),
        "cmp_w1": np.ascontiguousarray(n["cmp_w1"][0].reshape(2, 32, 64, 128).transpose(0, 2, 1, 3)).reshape(P, 32, 128),
        "cmp_w2": np.ascontiguousarray(np.concatenate([w2[0], w2[0], w2[1]], axis=1)),
        "cmp_pe": np.ascontiguousarray(n["cmp_pe"][0].transpose(0, 2, 1)).reshape(P, 32),
        "lora_a": np.ascontiguousarray(lora_a.reshape(KD, P, 288).transpose(1, 0, 2)),
        "lora_b": np.ascontiguousarray(lora_b.transpose(1, 0, 2)),
    }


def constants():
    p = np.arange(P)[:, None]
    q = np.arange(P)[None]
    c = {}
    c["ident"] = (p == q)
    c["blockones"] = (p // 64 == q // 64)
    c["negtri"] = -1.0 * (p >= q)
    c["m4"] = np.concatenate([p < q, p <= q, p < q, p <= q], axis=1)
    c["levels"] = np.concatenate([((p // b) % 2 == 0) & (q // b == p // b + 1) for b in (1, 2, 4, 8, 16, 32, 64)], axis=1)
    far = (p + 3 * P) - np.arange(T)[None]
    ok = [far >= 0, (far >= 0) & (far <= 128), (far >= 0) & (far % 4 == 0), (far >= 0) & (far % 16 == 0)]
    c["dist"] = np.concatenate([np.where(m, -1.0 * far, NEG) for m in ok], axis=1)
    far = (np.arange(NB)[None, :, None] * P + np.arange(P)[:, None, None]) - (16 * np.arange(32)[None, None] + 31)
    c["dist_cmp"] = np.where(far >= 0, -1.0 * far, NEG).reshape(P, -1)
    c["valid"] = (p >= 31)
    return np.ascontiguousarray(np.concatenate([c[m].astype(np.float32) for m, _ in CONST_SIZES], axis=1))


def kernel(**inputs):
    import concourse.bacc as _bacc
    from concourse.bass_utils import run_bass_kernel_spmd as _run

    nc = _bacc.Bacc("TRN2", target_bir_lowering=False, num_devices=1)
    arrays, args = {}, {}
    for name, v in layout(inputs).items():
        arrays[f"in_{name}"] = v
        args[name] = nc.dram_tensor(f"in_{name}", v.shape, mybir.dt.from_np(v.dtype), kind="ExternalInput").ap()
    out = nc.dram_tensor("out_y", [P, KD, T], F32, kind="ExternalOutput").ap()
    build(nc, args, out)
    r = _run(nc, [arrays], core_ids=[0])
    y = r.results[0]["out_y"]
    return np.ascontiguousarray(y.transpose(2, 1, 0)).reshape(1, T, D)
```

```python
from contextlib import ExitStack

import numpy as np
import concourse.bass as bass
from concourse import mybir

F32 = mybir.dt.float32
F32R = mybir.dt.float32r
ACT = mybir.ActivationFunctionType
ALU = mybir.AluOpType
AX = mybir.AxisListType

P = 128
T = 512
D = 1024
KD = D // P
HD = 64
NB = T // P
MEM = 256
RING = 4
AHEAD = 2
N_CMP = 31
SLOPES = [float(2.0 ** (-8.0 * i / 10)) for i in range(1, 11)]
DECAY = float(np.exp(-0.5))
NEG = -1e30

T_Q, T_CMP, T_KSEL, T_KWIN, T_V, T_DQ, T_DK, T_DV, T_SQ, T_SK, T_SV = 0, 2, 3, 4, 5, 6, 9, 12, 15, 18, 21
N_PROJ = 24
V_TILES = [T_V, T_DV, T_DV + 1, T_DV + 2, T_SV, T_SV + 1, T_SV + 2]

START = 0
F1 = 4096
F2 = 2816
FFN_PARTS = (12, 10)
TAPS = 31
PE_TAPS = 13

VEC_SIZES = [("norm_mix", 8), ("norm_mlp", 8), ("mem_norm", 8), ("mix0", 8), ("mix1", 8),
             ("xattn0", 8), ("xattn1", 8), ("ffn0", 8), ("ffn1", 8), ("final", 8), ("mu", 48),
             ("w0", 8), ("a0", 8), ("k_k", 8), ("k_a", 8), ("r_k", 8), ("ln_g", 8), ("ln_b", 8),
             ("cb_in", 16), ("cdw", 8 * TAPS), ("cdw_b", 8), ("cln_g", 8), ("cln_b", 8), ("cb_out", 8),
             ("fdw0", 44 * 3), ("fdw1", 44 * 3), ("gains", 6)]
VEC = {}
_at = 0
for _n, _s in VEC_SIZES:
    VEC[_n] = _at
    _at += _s
N_VEC = _at

CONST_SIZES = [("ident", 128), ("blockones", 128), ("negtri", 128), ("m4", 512), ("levels", 7 * 128),
               ("dist", 4 * 512), ("dist_cmp", 4 * 32), ("valid", 1)]
CST = {}
_at = 0
for _n, _s in CONST_SIZES:
    CST[_n] = _at
    _at += _s
N_CONST = _at
N_KEEP = CST["dist"]


class Signal:

    def __init__(self, nc, name):
        self.sem = nc.alloc_semaphore(name)
        self.base = 0

    def __call__(self, n):
        return self.base + n


class Core:

    def __init__(self, nc):
        self.nc = nc
        self.signals = {}
        self.tiles = 0
        self.chunk = 0
        self.first = self.limit = 0

    def tile(self, name, shape, dtype):
        self.tiles += 1
        return self.nc.sbuf_tensor(f"{name}_{self.tiles}", shape, dtype)

    def sig(self, *names):
        for n in names:
            if n not in self.signals:
                self.signals[n] = Signal(self.nc, n)
        out = [self.signals[n] for n in names]
        return out if len(out) > 1 else out[0]

    def slots(self):
        return [self.sig(f"slot{j}_loaded") for j in range(RING)]

    def vec(self, name, i):
        c = VEC[name] + i
        return self.vecs[:, c:c + 1]

    def cst(self, name, w):
        return self.consts[:, CST[name]:CST[name] + w]


class Split:

    def __init__(self, stack, k, name, *shape):
        self.hi = stack.enter_context(k.tile(f"{name}_hi", [P, *shape], F32R))
        self.lo = stack.enter_context(k.tile(f"{name}_lo", [P, *shape], F32R))


def as_float(t):
    return t.bitcast(F32)


def load_everything(k, a):
    loaded, made, free, used, sq, ac = k.sig("loaded", "made", "bank_free", "chunk_used", "squared", "squares_added")
    with k.tile("sq0", [P, KD, T], F32) as sqt, k.nc.Block() as block:
        @block.sync
        def _(sp):
            sp.dma_start(k.x[:, :, :], a["x"]).then_inc(loaded.sem, 16)

        @block.scalar
        def _(act):
            act.dma_start(k.vecs[:, :], a["vecs"]).then_inc(loaded.sem, 16)
            act.dma_start(k.consts[:, :], a["consts"][:, 0:N_KEEP]).then_inc(loaded.sem, 16)
            act.wait_ge(loaded.sem, loaded(48))
            for m in range(KD):
                act.activation(sqt[:, m, :], k.x[:, m, :], ACT.Square).then_inc(sq.sem, 1)

        @block.vector
        def _(v):
            v.memset(k.ones[:, :], 1.0).then_inc(made.sem, 1)
            v.memset(k.negones[:, :], -1.0).then_inc(made.sem, 1)
            for n, value in enumerate([1e-6, 64e-6, 64e-5, 1e-5, 1.0]):
                v.memset(k.eps[:, n:n + 1], value).then_inc(made.sem, 1)
            v.wait_ge(made.sem, made(7))
            v.sem_inc(free.sem, RING)
            v.sem_inc(used.sem, RING)
            v.wait_ge(sq.sem, sq(2))
            v.tensor_tensor(k.squares[:, :], sqt[:, 0, :], sqt[:, 1, :], ALU.add).then_inc(ac.sem, 1)
            for m in range(2, KD):
                v.wait_ge(sq.sem, sq(m + 1))
                v.wait_ge(ac.sem, ac(m - 1))
                v.tensor_tensor(k.squares[:, :], k.squares[:, :], sqt[:, m, :], ALU.add).then_inc(ac.sem, 1)
    loaded.base += 48
    made.base += 7
    sq.base += KD
    ac.base += KD - 1
    used.base += RING
    k.bias = {1e-6: k.eps[:, 0:1], 64e-6: k.eps[:, 1:2], 64e-5: k.eps[:, 2:3], 1e-5: k.eps[:, 3:4], 1.0: k.eps[:, 4:5]}


def split_weights_hi(k, act, n, value):
    used, hi_r = k.sig("chunk_used", "weights_hi")
    act.wait_ge(k.slots()[n % RING].sem, value)
    act.activation(k.w.hi[:, n % RING, :], k.raw[:, n % RING, :], ACT.Copy).then_inc(hi_r.sem, 1)


def open_ring(k, stack, n_chunks):
    k.raw = stack.enter_context(k.tile("raw", [P, RING, 1024], F32))
    k.w = Split(stack, k, "w", RING, 1024)
    k.first, k.limit = k.chunk, k.chunk + n_chunks
    hi_r, lo_r = k.sig("weights_hi", "weights_lo")
    slots = k.slots()
    with k.nc.Block() as block:
        @block.sync
        def _(sp):
            for n in range(RING + AHEAD):
                if n >= RING:
                    sp.wait_ge(lo_r.sem, lo_r(n - RING + 1))
                sp.dma_start(k.raw[:, n % RING, :], k.wall[k.first + n]).then_inc(slots[n % RING].sem, 16)

        @block.scalar
        def _(act):
            for n in range(AHEAD):
                act.wait_ge(slots[n].sem, slots[n](16))
                act.activation(k.w.hi[:, n, :], k.raw[:, n, :], ACT.Copy).then_inc(hi_r.sem, 1)

        @block.gpsimd
        def _(g):
            for n in range(AHEAD):
                g.wait_ge(hi_r.sem, hi_r(n + 1))
                g.tensor_tensor(k.w.lo[:, n, :], k.raw[:, n, :], as_float(k.w.hi[:, n, :]), ALU.subtract
                                ).then_inc(lo_r.sem, 1)


def close_ring(k):
    for s in k.slots():
        s.base += 16 * ((k.limit - k.first) // RING)


def passes(e, n, first, last):
    a = 1 if first else 0
    b = max(n - 1, a) if last else n
    yield from range(a)
    if b - a == 1:
        yield a
    elif b > a:
        with e.Fori(a, b) as i:
            yield i
    yield from range(b, n)


def linear(k, m_tiles, kt, src, act=None, vector=None, pool=None, width=T, feed=None, unroll=False):
    nc = k.nc
    used, free, hi_r, lo_r, fed = k.sig("chunk_used", "bank_free", "weights_hi", "weights_lo", "fed")
    slots = k.slots()
    per = -(-kt // 8)
    n_groups, N = m_tiles // 4, m_tiles * per
    c0 = k.chunk - k.first
    n_split = min(N, k.limit - k.chunk - AHEAD)
    n_load = min(N, k.limit - k.chunk - AHEAD - RING)
    ending = n_split < N

    def sums(pe, bank, n, q, c, first, last):
        t = 8 * c + q
        w = (n % RING, slice(q * P, (q + 1) * P))
        hi, lo = k.w.hi[:, w[0], w[1]], k.w.lo[:, w[0], w[1]]
        pe.matmul(bank, hi, src.hi[:, t, 0:width], start=first, stop=False)
        pe.matmul(bank, hi, src.lo[:, t, 0:width], start=False, stop=False)
        return pe.matmul(bank, lo, src.hi[:, t, 0:width], start=False, stop=last)

    with nc.Block() as block:
        @block.sync
        def _(sp):
            ahead = AHEAD + RING

            def load(i, j):
                sp.wait_ge(lo_r.sem, lo_r(i * RING + (j + 1 + AHEAD)))
                s = (j + ahead) % RING
                at = k.chunk + j + ahead
                source = k.wall[at + i * RING] if isinstance(i, int) else \
                    k.wall[bass.ds(i * RING + at, 1)].rearrange("o p n -> (o p) n")
                sp.dma_start(k.raw[:, s, :], source).then_inc(slots[s].sem, 16)
            if n_load >= RING:
                for i in passes(sp, n_load // RING, False, False):
                    for j in range(RING):
                        load(i, j)
            for j in range(max(n_load, 0) % RING):
                load(n_load // RING, j)

        @block.tensor
        def _(pe):
            if feed is not None:
                feed.tensor(pe)
            for i in passes(pe, n_groups, feed is not None, False):
                if isinstance(i, int) and i == 0 and feed is not None:
                    assert per == 1
                    for q in range(kt):
                        pe.wait_ge(fed.sem, fed(q + 1))
                        for j in range(4):
                            if q == 0:
                                pe.wait_ge(lo_r.sem, lo_r(j + 1))
                                pe.wait_ge(free.sem, free(j + 1))
                            mm = sums(pe, k.ps[:, j, 0:width], j, q, 0, q == 0, q == kt - 1)
                            if q == kt - 1:
                                mm.then_inc(used.sem, 1)
                    continue
                for j in range(4):
                    pe.wait_ge(free.sem, free(i * 4 + (j + 1)))
                    for c in range(per):
                        n = j * per + c
                        pe.wait_ge(lo_r.sem, lo_r(i * (4 * per) + (n + 1)))
                        for q in range(min(kt - 8 * c, 8)):
                            mm = sums(pe, k.ps[:, j, 0:width], n, q, c, c == 0 and q == 0, 8 * c + q == kt - 1)
                        mm.then_inc(used.sem, 1)

        def splitter(e, step):
            def run(i, j):
                for c in range(per):
                    n = j * per + c
                    if isinstance(i, int) and i * 4 * per + n >= n_split:
                        continue
                    step(i, n)
            return run

        @block.scalar
        def _(e):
            def step(i, n):
                s = (n + AHEAD) % RING
                e.wait_ge(slots[s].sem, (i * per + (c0 // RING + (n + AHEAD) // RING + 1)) * 16 + slots[s].base)
                e.wait_ge(used.sem, used(i * (4 * per) + (n + 1 + AHEAD - RING)))
                e.activation(k.w.hi[:, s, :], k.raw[:, s, :], ACT.Copy).then_inc(hi_r.sem, 1)
            run = splitter(e, step)
            if feed is not None:
                run(0, 0)
                run(0, 1)
                feed.scalar(e)
            for i in (range(n_groups) if unroll else passes(e, n_groups, feed is not None, ending)):
                for j in range(4):
                    if not (feed is not None and isinstance(i, int) and i == 0 and j < 2):
                        run(i, j)
                    if act is not None:
                        act(e, i, j)

        @block.gpsimd
        def _(e):
            def step(i, n):
                s = (n + AHEAD) % RING
                e.wait_ge(hi_r.sem, hi_r(i * (4 * per) + (n + 1 + AHEAD)))
                e.tensor_tensor(k.w.lo[:, s, :], k.raw[:, s, :], as_float(k.w.hi[:, s, :]), ALU.subtract
                                ).then_inc(lo_r.sem, 1)
            run = splitter(e, step)
            if feed is not None:
                run(0, 0)
                run(0, 1)
                feed.gpsimd(e)
            for i in (range(n_groups) if unroll else passes(e, n_groups, feed is not None, ending)):
                for j in range(4):
                    if not (feed is not None and isinstance(i, int) and i == 0 and j < 2):
                        run(i, j)
                    if pool is not None:
                        pool(e, i, j)

        @block.vector
        def _(e):
            if feed is not None:
                feed.vector(e)
            if vector is not None:
                for i in (range(n_groups) if unroll else passes(e, n_groups, False, False)):
                    for j in range(4):
                        vector(e, i, j)
    k.chunk += N
    for s in (used, hi_r, lo_r):
        s.base += N
    free.base += m_tiles
    if feed is not None:
        feed.done()
        fed.base += kt


def dyn(t, m):
    if isinstance(m, int):
        return t[:, m, :]
    return t[:, bass.ds(m, 1), :].rearrange("p o n -> p (o n)")


def copy_out(k, out, scale=1.0, width=T):
    used, free = k.sig("chunk_used", "bank_free")

    def act(e, i, j):
        e.wait_ge(used.sem, used(i * 4 + (j + 1)))
        e.activation(dyn(out, i * 4 + j)[:, 0:width], k.ps[:, j, 0:width], ACT.Copy, scale=scale).then_inc(free.sem, 1)
    return act


def residual(k, kt, src, per=1, bias=None, squares=True):
    used, free, added, sq, ac = k.sig("chunk_used", "bank_free", "added", "squared", "squares_added")
    with k.tile("sqr", [P, 2, T], F32) as sqt:
        def vector(e, i, j):
            m = 4 * i + j
            e.wait_ge(used.sem, used((m + 1) * per))
            if bias is None:
                ins = e.tensor_tensor(k.x[:, m, :], k.x[:, m, :], k.ps[:, j, :], ALU.add)
            else:
                ins = e.scalar_tensor_tensor(k.x[:, m, :], k.x[:, m, :], k.vec(bias, m), k.ps[:, j, :], ALU.add, ALU.add)
            ins.then_inc(free.sem, 1)
            if squares:
                e.sem_inc(added.sem, 1)

        def act(e, i, j):
            m = 4 * i + j
            e.wait_ge(free.sem, free(m + 1 + RING))
            if m >= 2:
                e.wait_ge(ac.sem, ac(m - 1))
            e.activation(sqt[:, m % 2, :], k.x[:, m, :], ACT.Square).then_inc(sq.sem, 1)

        def pool(e, i, j):
            m = 4 * i + j
            e.wait_ge(sq.sem, sq(m + 1))
            if m == 0:
                e.tensor_copy(k.squares[:, :], sqt[:, 0, :]).then_inc(ac.sem, 1)
            else:
                e.wait_ge(ac.sem, ac(m))
                e.tensor_tensor(k.squares[:, :], k.squares[:, :], sqt[:, m % 2, :], ALU.add).then_inc(ac.sem, 1)
        squares_ = squares
        linear(k, KD, kt, src, vector=vector, act=act if squares_ else None, pool=pool if squares_ else None, unroll=True)
    if squares:
        added.base += KD
        sq.base += KD
        ac.base += KD


class Norm:

    def __init__(self, k, gain, dst, whole):
        self.k, self.gain, self.dst, self.whole = k, gain, dst, whole

    def tensor(self, pe):
        k = self.k
        pe.matmul(k.ps[:, 4, :], k.ones[:, :], k.squares[:, :], start=True, stop=True).then_inc(k.sig("summed").sem, 1)

    def scalar(self, act):
        k = self.k
        summed, root, whole_r, hi = k.sig("summed", "root", "normed", "fed_hi")
        act.wait_ge(summed.sem, summed(1))
        act.activation(k.root[:, :], k.ps[:, 4, :], ACT.Sqrt, scale=1.0 / D, bias=k.bias[1e-6]).then_inc(root.sem, 1)
        for m in range(KD):
            act.wait_ge(whole_r.sem, whole_r(m + 1))
            act.activation(self.dst.hi[:, m, :], self.whole[:, m, :], ACT.Copy).then_inc(hi.sem, 1)

    def vector(self, v):
        k = self.k
        root, inverse, whole_r, hi, fed = k.sig("root", "inverse", "normed", "fed_hi", "fed")
        v.wait_ge(root.sem, root(1))
        v.reciprocal(k.root[:, :], k.root[:, :]).then_inc(inverse.sem, 1)
        v.wait_ge(inverse.sem, inverse(1))

        def rest(m):
            v.wait_ge(hi.sem, hi(m + 1))
            v.tensor_tensor(self.dst.lo[:, m, :], self.whole[:, m, :], as_float(self.dst.hi[:, m, :]), ALU.subtract
                            ).then_inc(fed.sem, 1)
        for m in range(KD):
            v.scalar_tensor_tensor(self.whole[:, m, :], k.x[:, m, :], k.vec(self.gain, m), k.root[:, :],
                                   ALU.mult, ALU.mult).then_inc(whole_r.sem, 1)
            if m:
                rest(m - 1)
        rest(KD - 1)

    def gpsimd(self, g):
        pass

    def done(self):
        for n, c in (("summed", 1), ("root", 1), ("inverse", 1), ("normed", KD), ("fed_hi", KD)):
            self.k.sig(n).base += c


class Parts:

    def __init__(self, k, whole, dst, n):
        self.k, self.whole, self.dst, self.n = k, whole, dst, n

    def tensor(self, pe):
        pass

    def scalar(self, act):
        hi = self.k.sig("fed_hi")
        for m in range(self.n):
            act.activation(self.dst.hi[:, m, :], self.whole[:, m, :], ACT.Copy).then_inc(hi.sem, 1)

    def vector(self, v):
        hi, fed = self.k.sig("fed_hi", "fed")
        for m in range(self.n):
            v.wait_ge(hi.sem, hi(m + 1))
            v.tensor_tensor(self.dst.lo[:, m, :], self.whole[:, m, :], as_float(self.dst.hi[:, m, :]), ALU.subtract
                            ).then_inc(fed.sem, 1)

    def gpsimd(self, g):
        pass

    def done(self):
        self.k.sig("fed_hi").base += self.n


class Mix:

    def __init__(self, k, h, xx, xm, dst, i):
        self.k, self.h, self.xx, self.xm, self.dst, self.i = k, h, xx, xm, dst, i

    def tensor(self, pe):
        pass

    def scalar(self, act):
        whole_r, hi = self.k.sig("normed", "fed_hi")
        for m in range(KD):
            act.wait_ge(whole_r.sem, whole_r(m + 1))
            act.activation(self.dst.hi[:, m, :], self.xm[:, m % 4, :], ACT.Copy).then_inc(hi.sem, 1)

    def vector(self, v):
        k = self.k
        whole_r, hi, fed = k.sig("normed", "fed_hi", "fed")

        def rest(m):
            v.wait_ge(hi.sem, hi(m + 1))
            v.tensor_tensor(self.dst.lo[:, m, :], self.xm[:, m % 4, :], as_float(self.dst.hi[:, m, :]), ALU.subtract
                            ).then_inc(fed.sem, 1)
        for m in range(KD):
            if m >= 4:
                v.wait_ge(fed.sem, fed(m - 3))
            v.scalar_tensor_tensor(self.xm[:, m % 4, :], self.xx[:, m, :], k.vec("mu", 8 * self.i + m), self.h[:, m, :],
                                   ALU.mult, ALU.add).then_inc(whole_r.sem, 1)
            if m:
                rest(m - 1)
        rest(KD - 1)

    def gpsimd(self, g):
        pass

    def done(self):
        for n in ("normed", "fed_hi"):
            self.k.sig(n).base += KD



def gates_of(k, wg, h, gates_w, gates, valid):
    wgl, gs, gt, gv = k.sig("gate_w_loaded", "gate_sums", "gates_made", "gates_masked")
    with k.nc.Block() as block:
        @block.sync
        def _(sp):
            sp.dma_start(gates_w[:, :, :], wg).then_inc(wgl.sem, 16)

        @block.tensor
        def _(pe):
            pe.wait_ge(wgl.sem, wgl(16))
            for b in range(NB):
                for m in range(KD):
                    mm = pe.matmul(k.ps[:, 4, b * 16:b * 16 + 12], h[:, m, b * P:(b + 1) * P], gates_w[:, m, :],
                                   start=(m == 0), stop=(m == KD - 1))
            mm.then_inc(gs.sem, 1)

        @block.scalar
        def _(act):
            act.wait_ge(gs.sem, gs(1))
            act.activation(gates[:, :, :], k.ps[:, 4, 0:64].rearrange("p (b g) -> p b g", b=NB)[:, :, 0:12],
                           ACT.Sigmoid).then_inc(gt.sem, 1)

        @block.vector
        def _(v):
            v.wait_ge(gt.sem, gt(1))
            v.tensor_scalar(gates[:, 0, 0:12:3], gates[:, 0, 0:12:3], valid, None, ALU.mult).then_inc(gv.sem, 1)
    wgl.base += 16
    gs.base += 1
    gt.base += 1
    gv.base += 1


def values_by_token(k, pr, vt):
    tr, te = k.sig("transposed", "transposed_out")
    with k.nc.Block() as block:
        @block.tensor
        def _(pe):
            for n, tile in enumerate(V_TILES):
                if n >= 4:
                    pe.wait_ge(te.sem, te(n - 3))
                for b in range(NB):
                    mm = pe.transpose(k.ps[:, 4 + n % 4, b * P:(b + 1) * P], pr[:, tile, b * P:(b + 1) * P], k.ident)
                mm.then_inc(tr.sem, 1)

        @block.scalar
        def _(act):
            for n in range(len(V_TILES)):
                act.wait_ge(tr.sem, tr(n + 1))
                act.activation(vt[:, :, n, :], k.ps[:, 4 + n % 4, :].rearrange("p (b d) -> p b d", b=NB), ACT.Copy
                               ).then_inc(te.sem, 1)
    tr.base += len(V_TILES)
    te.base += len(V_TILES)


def head_norms(k, pr):
    tiles = [(T_Q, 0, True), (T_Q + 1, 0, True), (T_KSEL, 2, False), (T_KWIN, 3, False)]
    tiles += [(T_DQ + i, 4, True) for i in range(3)] + [(T_DK + i, 5, False) for i in range(3)]
    sq_r, ss_r, rt_r, inv_r, nr, qs = k.sig("squared", "summed", "root", "inverse", "normed", "q_scaled")
    n = len(tiles)
    with k.tile("hn_sq", [P, 2, T], F32) as sq, k.tile("hn_rt", [P, 2, T], F32) as rt, \
         k.nc.Block() as block:
        @block.scalar
        def _(act):
            def square(t):
                if t >= 2:
                    act.wait_ge(ss_r.sem, ss_r(t - 1))
                act.activation(sq[:, t % 2, :], pr[:, tiles[t][0], :], ACT.Square).then_inc(sq_r.sem, 1)
            square(0)
            for t in range(n):
                if t + 1 < n:
                    square(t + 1)
                act.wait_ge(ss_r.sem, ss_r(t + 1))
                if t >= 2:
                    act.wait_ge(inv_r.sem, inv_r(t - 1))
                q = tiles[t][2]
                act.activation(rt[:, t % 2, :], k.ps[:, t % 2, :], ACT.Sqrt, scale=1.0 if q else 1.0 / HD,
                               bias=k.bias[64e-6 if q else 1e-6]).then_inc(rt_r.sem, 1)

        @block.tensor
        def _(pe):
            for t in range(n):
                pe.wait_ge(sq_r.sem, sq_r(t + 1))
                if t >= 2:
                    pe.wait_ge(rt_r.sem, rt_r(t - 1))
                pe.matmul(k.ps[:, t % 2, :], k.blockones, sq[:, t % 2, :], start=True, stop=True).then_inc(ss_r.sem, 1)

        @block.vector
        def _(v):
            for t in range(n):
                v.wait_ge(rt_r.sem, rt_r(t + 1))
                if t >= 2:
                    v.wait_ge(nr.sem, nr(t - 1))
                v.reciprocal(k.ps[:, 4 + t % 2, :], rt[:, t % 2, :]).then_inc(inv_r.sem, 1)
                v.wait_ge(inv_r.sem, inv_r(t + 1))
                v.scalar_tensor_tensor(pr[:, tiles[t][0], :], pr[:, tiles[t][0], :], k.vec("gains", tiles[t][1]),
                                       k.ps[:, 4 + t % 2, :], ALU.mult, ALU.mult).then_inc(nr.sem, 1)

        @block.gpsimd
        def _(g):
            for i in range(3):
                g.tensor_scalar(pr[:, T_SQ + i, :], pr[:, T_SQ + i, :], 0.125, None, ALU.mult).then_inc(qs.sem, 1)
    sq_r.base += n
    ss_r.base += n
    rt_r.base += n
    inv_r.base += n
    nr.base += n
    qs.base += 3


def compress(k, pr, w1_in, w2_in, pe_in, kc, vc):
    ld, raw_r, hs, ge, out_r, c1, c2, c3, c4, c5 = k.sig(
        "cmp_loaded", "cmp_raw", "cmp_hidden", "cmp_gelu", "cmp_out", "cmp_sq", "cmp_ss", "cmp_rt", "cmp_inv", "cmp_done")
    nc = k.nc
    with k.tile("cw1", [P, 32, 128], F32) as w1, k.tile("cw2", [P, 192], F32) as w2, \
         k.tile("cpe", [P, 32], F32) as pos, k.tile("craw", [P, 32, N_CMP], F32) as raw, \
         k.tile("chid", [P, 2, N_CMP], F32) as hid, k.tile("ck", [P, 4, 32], F32) as tmp, \
         nc.Block() as block:
        @block.sync
        def _(sp):
            sp.dma_start(pos[:, :], pe_in).then_inc(ld.sem, 16)
            sp.dma_start(w1[:, :, :], w1_in).then_inc(ld.sem, 16)
            sp.dma_start(w2[:, :], w2_in).then_inc(ld.sem, 16)

        @block.vector
        def _(v):
            v.wait_ge(ld.sem, ld(48))
            kv = pr[:, T_CMP, :].rearrange("p (n j) -> p j n", j=16)
            for half in range(2):
                v.tensor_tensor(raw[:, 16 * half:16 * half + 16, :], kv[:, :, half:half + N_CMP],
                                pos[:, 16 * half:16 * half + 16].unsqueeze(2).to_broadcast([P, 16, N_CMP]),
                                ALU.add).then_inc(raw_r.sem, 1)
            v.wait_ge(out_r.sem, out_r(2))
            v.wait_ge(c1.sem, c1(1))
            v.tensor_copy(tmp[:, 0, 0:N_CMP], k.ps[:, 2, 0:N_CMP]).then_inc(c5.sem, 1)
            v.tensor_copy(vc[0:N_CMP, :], k.ps[0:N_CMP, 3, 0:64]).then_inc(c5.sem, 1)
            v.wait_ge(c3.sem, c3(1))
            v.reciprocal(tmp[:, 3, 0:N_CMP], tmp[:, 2, 0:N_CMP]).then_inc(c4.sem, 1)
            v.wait_ge(c4.sem, c4(1))
            v.scalar_tensor_tensor(kc[:, 0:N_CMP], tmp[:, 0, 0:N_CMP], k.vec("gains", 1), tmp[:, 3, 0:N_CMP],
                                   ALU.mult, ALU.mult).then_inc(c5.sem, 1)

        @block.tensor
        def _(pe):
            pe.wait_ge(raw_r.sem, raw_r(2))
            pe.wait_ge(ld.sem, ld(48))
            for c in range(2):
                o = 64 * c
                for j in range(32):
                    mm = pe.matmul(k.ps[:, c, 0:N_CMP], w1[o:o + 64, j, :], raw[o:o + 64, j, :],
                                   start=(j == 0), stop=(j == 31))
                mm.then_inc(hs.sem, 1)
            pe.wait_ge(ge.sem, ge(2))
            pe.matmul(k.ps[:, 2, 0:N_CMP], w2[:, 0:128], hid[:, 0, :], start=True, stop=True).then_inc(out_r.sem, 1)
            pe.matmul(k.ps[0:N_CMP, 3, 0:64], hid[:, 1, :], w2[:, 128:192], start=True, stop=True).then_inc(out_r.sem, 1)
            pe.wait_ge(c1.sem, c1(1))
            pe.matmul(k.ps[:, 4, 0:N_CMP], k.blockones, tmp[:, 1, 0:N_CMP], start=True, stop=True).then_inc(c2.sem, 1)

        @block.scalar
        def _(act):
            for c in range(2):
                act.wait_ge(hs.sem, hs(c + 1))
                act.activation(hid[:, c, :], k.ps[:, c, 0:N_CMP], ACT.Gelu_apprx_tanh).then_inc(ge.sem, 1)
            act.wait_ge(out_r.sem, out_r(1))
            act.activation(tmp[:, 1, 0:N_CMP], k.ps[:, 2, 0:N_CMP], ACT.Square).then_inc(c1.sem, 1)
            act.wait_ge(c2.sem, c2(1))
            act.activation(tmp[:, 2, 0:N_CMP], k.ps[:, 4, 0:N_CMP], ACT.Sqrt, scale=1.0 / HD, bias=k.bias[1e-6]
                           ).then_inc(c3.sem, 1)
    ld.base += 48
    raw_r.base += 2
    hs.base += 2
    ge.base += 2
    out_r.base += 2
    c1.base += 1
    c2.base += 1
    c3.base += 1
    c4.base += 1
    c5.base += 3


def softmax_mixers(k, pr, vt, gates, dist, dist_cmp, kc, vc, cat):
    nc = k.nc
    units = []
    for h in range(4):
        for b, key in ((0, None), (1, T_KSEL), (2, T_KWIN)):
            units.append((T_Q + h // 2, h % 2, key, (0, 64 * (b == 2)), 0, SLOPES[6 + h]))
    for j in range(2):
        for g in range(3):
            units.append((T_DQ + g, j, T_DK + g, (1 + g, 64 * j), 1 + g, SLOPES[2 * g + j]))
    U = len(units)
    sc, bi, mx, ex, wt, scaled, tr, pt_r, pv, oe, sm, mg = k.sig(
        "scores", "biased", "maxima", "exps", "weights", "scaled", "transposed", "transposed_out", "pv_done",
        "mixer_out", "small_steps", "merged_exps")
    with k.tile("sm_p", [P, U, T], F32) as p, k.tile("sm_pt", [P, 3, T], F32) as pt, \
         k.tile("sm_st", [P, 6, 32], F32) as st, nc.Block() as block:
        nm, l, w, e, nmm = st[:, 0, :], st[:, 1, :], st[:, 2, :], st[:, 3, :], st[:, 4, :]
        el = st[:, 5, :]

        def width(u, qb):
            return N_CMP if units[u][2] is None else (qb + 1) * P

        @block.tensor
        def _(pe):
            for qb in range(NB):
                for u, (qt, half, key, _, _, _) in enumerate(units):
                    g = qb * U + u
                    o, w_ = 64 * half, width(u, qb)
                    if g >= 4:
                        pe.wait_ge(bi.sem, bi(g - 3))
                    keys = kc[o:o + 64, 0:w_] if key is None else pr[o:o + 64, key, 0:w_]
                    pe.matmul(k.ps[:, g % 4, 0:w_], pr[o:o + 64, qt, qb * P:(qb + 1) * P], keys,
                              start=True, stop=True).then_inc(sc.sem, 1)

                def turn(u):
                    g = qb * U + u
                    w_ = width(u, qb)
                    pe.wait_ge(scaled.sem, scaled(g + 1))
                    if g >= 2:
                        pe.wait_ge(pt_r.sem, pt_r(g - 1))
                    for b in range(-(-w_ // P)):
                        r = min(P, w_ - b * P)
                        mm = pe.transpose(k.ps[0:r, 4 + g % 2, b * P:(b + 1) * P], p[:, u, b * P:b * P + r], k.ident)
                    mm.then_inc(tr.sem, 1)

                def values(u):
                    g = qb * U + u
                    _, half, key, (vtile, vcol), _, _ = units[u]
                    w_, o = width(u, qb), 64 * half
                    head = u // 3
                    out = 3 * qb + head // 2
                    if u % 3 == 0 and out >= 2:
                        pe.wait_ge(oe.sem, oe(out - 1))
                    pe.wait_ge(pt_r.sem, pt_r(g + 1))
                    nblk = -(-w_ // P)
                    for b in range(nblk):
                        r = min(P, w_ - b * P)
                        val = vc[0:r, :] if key is None else vt[:, b, vtile, vcol:vcol + 64]
                        mm = pe.matmul(k.ps[o:o + 64, 6 + out % 2, 0:P], val, pt[0:r, g % 3, b * P:(b + 1) * P],
                                       start=(u % 3 == 0 and b == 0), stop=(u % 3 == 2 and b == nblk - 1))
                    mm.then_inc(pv.sem, 1)

                turn(0)
                for u in range(U):
                    if u + 1 < U:
                        turn(u + 1)
                    values(u)

        @block.vector
        def _(v):
            steps = 0
            for qb in range(NB):
                def bias(u):
                    g = qb * U + u
                    w_ = width(u, qb)
                    table, slope = units[u][4], units[u][5]
                    d = dist_cmp[:, qb, 0:w_] if units[u][2] is None else dist[:, table, T - w_:T]
                    v.wait_ge(sc.sem, sc(g + 1))
                    if qb >= 1:
                        v.wait_ge(tr.sem, tr(g - U + 1))
                    v.scalar_tensor_tensor(p[:, u, 0:w_], d, slope, k.ps[:, g % 4, 0:w_], ALU.mult, ALU.add
                                           ).then_inc(bi.sem, 1)

                def maximum(u):
                    g = qb * U + u
                    v.wait_ge(bi.sem, bi(g + 1))
                    if qb >= 1 and u == 0:
                        v.wait_ge(scaled.sem, scaled(g))
                    v.tensor_reduce(nm[:, u:u + 1], p[:, u, 0:width(u, qb)], AX.X, ALU.max, negate=True
                                    ).then_inc(mx.sem, 1)
                bias(0)
                for u in range(U):
                    if u + 1 < U:
                        bias(u + 1)
                    maximum(u)
                v.wait_ge(mx.sem, mx((qb + 1) * U))
                v.tensor_reduce(nmm[:, 0:2], nm[:, 12:18].rearrange("p (a b) -> p a b", a=2), AX.X, ALU.min
                                ).then_inc(sm.sem, 1)
                v.wait_ge(ex.sem, ex((qb + 1) * U))
                v.reciprocal(el[:, 0:12], l[:, 0:12]).then_inc(sm.sem, 1)
                v.wait_ge(mg.sem, mg(2 * (qb + 1)))
                v.tensor_tensor(el[:, 12:18], e[:, 0:6], l[:, 12:18], ALU.mult).then_inc(sm.sem, 1)
                v.wait_ge(sm.sem, sm(6 * qb + 3))
                v.tensor_tensor(w[:, 0:12], el[:, 0:12], gates[:, qb, :], ALU.mult).then_inc(wt.sem, 1)
                v.tensor_reduce(nmm[:, 2:4], el[:, 12:18].rearrange("p (a b) -> p a b", a=2), AX.X, ALU.add
                                ).then_inc(sm.sem, 1)
                v.wait_ge(sm.sem, sm(6 * qb + 4))
                v.reciprocal(nmm[:, 4:6], nmm[:, 2:4]).then_inc(sm.sem, 1)
                v.wait_ge(sm.sem, sm(6 * qb + 5))
                v.tensor_tensor(w[:, 12:18].rearrange("p (a b) -> p a b", a=2),
                                e[:, 0:6].rearrange("p (a b) -> p a b", a=2),
                                nmm[:, 4:6].unsqueeze(2).to_broadcast([P, 2, 3]), ALU.mult).then_inc(wt.sem, 1)
                v.sem_inc(sm.sem, 1)
                for i in range(3):
                    v.wait_ge(pv.sem, pv(qb * U + 6 * (i + 1)))
                    v.tensor_copy(cat[:, i, qb * P:(qb + 1) * P], k.ps[:, 6 + (3 * qb + i) % 2, 0:P]).then_inc(oe.sem, 1)

        @block.scalar
        def _(act):
            for qb in range(NB):
                for u in range(U):
                    g = qb * U + u
                    act.wait_ge(mx.sem, mx(g + 1))
                    act.activation(p[:, u, 0:width(u, qb)], p[:, u, 0:width(u, qb)], ACT.Exp, bias=nm[:, u:u + 1],
                                   accum_out=l[:, u:u + 1]).then_inc(ex.sem, 1)
                act.wait_ge(sm.sem, sm(6 * qb + 1))
                for j in range(2):
                    act.activation(e[:, 3 * j:3 * j + 3], nm[:, 12 + 3 * j:15 + 3 * j], ACT.Exp, scale=-1.0,
                                   bias=nmm[:, j:j + 1]).then_inc(mg.sem, 1)
                for u in range(U):
                    g = qb * U + u
                    w_ = width(u, qb)
                    act.wait_ge(tr.sem, tr(g + 1))
                    if g >= 3:
                        act.wait_ge(pv.sem, pv(g - 2))
                    r, c = (w_, P) if units[u][2] is None else (P, w_)
                    act.activation(pt[0:r, g % 3, 0:c], k.ps[0:r, 4 + g % 2, 0:c], ACT.Copy).then_inc(pt_r.sem, 1)

        @block.gpsimd
        def _(gp):
            for qb in range(NB):
                gp.wait_ge(wt.sem, wt(2 * (qb + 1)))
                for u in range(U):
                    gp.tensor_scalar(p[:, u, 0:width(u, qb)], p[:, u, 0:width(u, qb)], w[:, u:u + 1], None, ALU.mult
                                     ).then_inc(scaled.sem, 1)
    for s in (sc, bi, mx, ex, scaled, tr, pt_r, pv):
        s.base += NB * U
    wt.base += 2 * NB
    oe.base += 3 * NB
    sm.base += 6 * NB
    mg.base += 2 * NB


def stick_breaking(k, pr, vt, cat):
    nc = k.nc
    H = 6
    units = [(h, kb) for h in range(H) for kb in (3, 2, 1, 0)]
    z_r, chain, ln_r, sp_raw, sp_r, l_r, at_raw, at_r, o_r, oe = k.sig(
        "z_ready", "softplus_steps", "softplus_log", "softplus_raw", "softplus_ready", "log_weights", "weights_raw",
        "weights_ready", "sb_out", "sb_out_taken")
    n = len(units)
    with k.tile("sb_sp", [P, 8, T], F32) as sp_t, k.tile("sb_at", [P, 8, T], F32) as at, \
         k.tile("sb_t", [P, 2, T], F32) as t1, nc.Block() as block:
        @block.tensor
        def _(pe):
            def z(u):
                h, kb = units[u]
                o, w = 64 * (h % 2), T - kb * P
                if u >= 4:
                    pe.wait_ge(at_raw.sem, at_raw(u - 3))
                pe.matmul(k.ps[:, u % 4, 0:w], pr[o:o + 64, T_SK + h // 2, kb * P:(kb + 1) * P],
                          pr[o:o + 64, T_SQ + h // 2, kb * P:T], start=True, stop=False,
                          skip_group_check=True).then_inc(z_r.sem, 1)

            def accumulate(u):
                h, kb = units[u]
                pe.wait_ge(sp_r.sem, sp_r(u + 1))
                mm = pe.matmul(k.ps[:, u % 4, 0:T - kb * P], k.negtri, sp_t[:, u % 8, 0:T - kb * P],
                               start=False, stop=(kb == 3), skip_group_check=True)
                for later in range(kb + 1, 4):
                    mm = pe.matmul(k.ps[:, u % 4, (later - kb) * P:T - kb * P], k.negones[:, :],
                                   sp_t[:, (4 * h + 3 - later) % 8, 0:T - later * P], start=False,
                                   stop=(later == 3), skip_group_check=True)
                mm.then_inc(l_r.sem, 1)

            def values(h):
                o = 64 * (h % 2)
                pe.wait_ge(at_r.sem, at_r(4 * h + 4))
                if h >= 2:
                    pe.wait_ge(oe.sem, oe(h - 1))
                for kb in range(4):
                    mm = pe.matmul(k.ps[o:o + 64, 4 + h % 2, kb * P:T], vt[:, kb, 4 + h // 2, o:o + 64],
                                   at[:, (4 * h + 3 - kb) % 8, 0:T - kb * P], start=(kb == 0), stop=(kb == 3),
                                   skip_group_check=True)
                mm.then_inc(o_r.sem, 1)

            z(0)
            for u in range(n):
                if u + 1 < n:
                    z(u + 1)
                accumulate(u)
                if u % 4 == 0 and u > 0:
                    values(u // 4 - 1)
            values(H - 1)

        @block.scalar
        def _(act):
            def softplus(u):
                w = T - units[u][1] * P
                act.wait_ge(z_r.sem, z_r(u + 1))
                if u >= 2:
                    act.wait_ge(sp_raw.sem, sp_raw(u - 1))
                act.activation(t1[:, u % 2, 0:w], k.ps[:, u % 4, 0:w], ACT.Abs).then_inc(chain.sem, 1)
                act.wait_ge(chain.sem, chain(2 * u + 1))
                act.activation(t1[:, u % 2, 0:w], t1[:, u % 2, 0:w], ACT.Exp, scale=-1.0).then_inc(chain.sem, 1)
                act.wait_ge(chain.sem, chain(2 * u + 2))
                act.activation(t1[:, u % 2, 0:w], t1[:, u % 2, 0:w], ACT.Ln, bias=k.bias[1.0]).then_inc(ln_r.sem, 1)

            def weights(u):
                h, kb = units[u]
                w = T - kb * P
                act.wait_ge(l_r.sem, l_r(u + 1))
                if h >= 2:
                    act.wait_ge(o_r.sem, o_r(h - 1))
                act.activation(at[:, u % 8, 0:w], k.ps[:, u % 4, 0:w], ACT.Exp).then_inc(at_raw.sem, 1)

            softplus(0)
            for u in range(n):
                if u + 1 < n:
                    softplus(u + 1)
                weights(u)

        @block.vector
        def _(v):
            def out(h):
                o = 64 * (h % 2)
                v.wait_ge(o_r.sem, o_r(h + 1))
                v.tensor_copy(cat[o:o + 64, 3 + h // 2, :], k.ps[o:o + 64, 4 + h % 2, :]).then_inc(oe.sem, 1)

            for u in range(n):
                h, kb = units[u]
                w = T - kb * P
                v.wait_ge(ln_r.sem, ln_r(u + 1))
                if h >= 2:
                    v.wait_ge(l_r.sem, l_r(4 * (h - 1)))
                v.scalar_tensor_tensor(sp_t[:, u % 8, 0:w], k.ps[:, u % 4, 0:w], 0.0, t1[:, u % 2, 0:w],
                                       ALU.max, ALU.add).then_inc(sp_raw.sem, 1)
                if u % 4 == 1 and u > 4:
                    out(u // 4 - 1)
            out(H - 1)

        @block.gpsimd
        def _(g):
            def strict(t):
                return g.affine_select(t, t, [[1, P]], ALU.is_ge, 0.0, base=-1, channel_multiplier=-1)

            g.wait_ge(sp_raw.sem, sp_raw(1))
            strict(sp_t[:, 0, 0:P]).then_inc(sp_r.sem, 1)
            for u in range(n):
                if u + 1 < n:
                    g.wait_ge(sp_raw.sem, sp_raw(u + 2))
                    strict(sp_t[:, (u + 1) % 8, 0:P]).then_inc(sp_r.sem, 1)
                g.wait_ge(at_raw.sem, at_raw(u + 1))
                strict(at[:, u % 8, 0:P]).then_inc(at_r.sem, 1)
    for s in (z_r, ln_r, sp_raw, sp_r, l_r, at_raw, at_r):
        s.base += n
    chain.base += 2 * n
    o_r.base += H
    oe.base += H


def first_block(k, a, stop):
    nc = k.nc
    with ExitStack() as outer:
        tile = lambda st, name, *shape: st.enter_context(k.tile(name, [P, *shape], F32))
        cat = tile(outer, "cat", 6, T)
        with ExitStack() as mixers:
            pr = tile(mixers, "proj", N_PROJ, T)
            far = tile(mixers, "dist", N_CONST - N_KEEP)
            gates = tile(mixers, "gates", NB, 12)
            kc = tile(mixers, "kc", 32)
            vc = tile(mixers, "vc", 64)
            dist = far[:, 0:2048].rearrange("p (a t) -> p a t", a=4)
            dist_cmp = far[:, 2048:2048 + 128].rearrange("p (a t) -> p a t", a=4)
            with ExitStack() as st:
                h = tile(st, "h", KD, T)
                gw = tile(st, "gates_w", KD, 12)
                with ExitStack() as st2:
                    hs = Split(st2, k, "h", KD, T)
                    far_loaded = k.sig("distances_loaded")
                    out = copy_out(k, pr)

                    def act(e, i, j):
                        if isinstance(i, int) and i == 0 and j == 0:
                            e.dma_start(far[:, :], a["consts"][:, N_KEEP:N_CONST]).then_inc(far_loaded.sem, 16)
                        out(e, i, j)
                    linear(k, N_PROJ, KD, hs, act=act, feed=Norm(k, "norm_mix", hs, h))
                gates_of_valid = far[:, 2176:2177]
                with nc.Block() as block:
                    @block.vector
                    def _(v):
                        v.wait_ge(far_loaded.sem, far_loaded(16))
                gates_of(k, a["w_gate"], h, gw, gates, gates_of_valid)
            vt = tile(mixers, "values", NB, 7, P)
            values_by_token(k, pr, vt)
            head_norms(k, pr)
            compress(k, pr, a["cmp_w1"], a["cmp_w2"], a["cmp_pe"], kc, vc)
            stick_breaking(k, pr, vt, cat)
            softmax_mixers(k, pr, vt, gates, dist, dist_cmp, kc, vc, cat)
        cs = Split(outer, k, "cat", 6, T)
        split_tiles(k, cat, cs, 6)
        residual(k, 6, cs)
    if stop == 1:
        return
    mlp(k)


def split_tiles(k, whole, dst, n):
    hi, lo = k.sig("fed_hi", "fed_lo")
    with k.nc.Block() as block:
        @block.scalar
        def _(act):
            for m in range(n):
                act.activation(dst.hi[:, m, :], whole[:, m, :], ACT.Copy).then_inc(hi.sem, 1)

        @block.vector
        def _(v):
            for m in range(n):
                v.wait_ge(hi.sem, hi(m + 1))
                v.tensor_tensor(dst.lo[:, m, :], whole[:, m, :], as_float(dst.hi[:, m, :]), ALU.subtract).then_inc(lo.sem, 1)
    hi.base += n
    lo.base += n


def mlp(k):
    used, free, relued, whole_r, hi, lo = k.sig("chunk_used", "bank_free", "relued", "hidden_whole", "hidden_hi", "hidden_lo")
    half = F1 // P // 2
    with ExitStack() as st:
        hs = Split(st, k, "h", KD, T)
        h = st.enter_context(k.tile("h", [P, KD, T], F32))
        hid = Split(st, k, "hidden", half, T)
        rl = st.enter_context(k.tile("relu", [P, 2, T], F32))
        sq = st.enter_context(k.tile("relu2", [P, 2, T], F32))

        def act(e, i, j):
            e.wait_ge(used.sem, used(i * 4 + (j + 1)))
            e.wait_ge(free.sem, free(i * 4 + (j + RING - 1)))
            e.activation(rl[:, j % 2, :], k.ps[:, j, :], ACT.Relu).then_inc(relued.sem, 1)
            e.wait_ge(relued.sem, relued(i * 4 + (j + 1)))
            e.activation(dyn(hid.hi, i * 4 + j), rl[:, j % 2, :], ACT.Square).then_inc(hi.sem, 1)

        def vector(e, i, j):
            e.wait_ge(relued.sem, relued(i * 4 + (j + 1)))
            e.tensor_tensor(sq[:, j % 2, :], rl[:, j % 2, :], k.ps[:, j, :], ALU.mult).then_inc(free.sem, 1)
            e.wait_ge(free.sem, free(i * 4 + (j + 1 + RING)))
            e.wait_ge(hi.sem, hi(i * 4 + (j + 1)))
            e.tensor_tensor(dyn(hid.lo, i * 4 + j), sq[:, j % 2, :], as_float(dyn(hid.hi, i * 4 + j)), ALU.subtract
                            ).then_inc(lo.sem, 1)
        for n in range(2):
            linear(k, half, KD, hs, act=act, vector=vector, feed=None if n else Norm(k, "norm_mlp", hs, h))
            for s in (relued, hi, lo):
                s.base += half
            residual(k, half, hid, per=2, squares=(n == 1))



def time_mix_inputs(k, a, r, kk, vv, inner_w, inner_a, inner_g):
    nc = k.nc
    summed, root, inverse, normed, shifted, ld, mixed, sums, inner_r, xu = k.sig(
        "summed", "root", "inverse", "normed", "shifted", "lora_loaded", "mixed", "lora_sums", "lora_inner", "mix_used")
    with ExitStack() as st:
        tile = lambda name, *shape: st.enter_context(k.tile(name, [P, *shape], F32))
        h, xx, xm = tile("h", KD, T), tile("xx", KD, T), tile("xm", 4, T)
        with nc.Block() as block:
            @block.tensor
            def _(pe):
                pe.matmul(k.ps[:, 4, :], k.ones[:, :], k.squares[:, :], start=True, stop=True).then_inc(summed.sem, 1)

            @block.scalar
            def _(act):
                act.wait_ge(summed.sem, summed(1))
                act.activation(k.root[:, :], k.ps[:, 4, :], ACT.Sqrt, scale=1.0 / D, bias=k.bias[1e-6]).then_inc(root.sem, 1)

            @block.vector
            def _(v):
                v.wait_ge(root.sem, root(1))
                v.reciprocal(k.root[:, :], k.root[:, :]).then_inc(inverse.sem, 1)
                v.wait_ge(inverse.sem, inverse(1))
                for m in range(KD):
                    v.scalar_tensor_tensor(h[:, m, :], k.x[:, m, :], k.vec("mix0", m), k.root[:, :],
                                           ALU.mult, ALU.mult).then_inc(normed.sem, 1)
                for m in range(KD):
                    v.wait_ge(normed.sem, normed(m + 1))
                    v.tensor_tensor(xx[:, m, 1:T], h[:, m, 0:T - 1], h[:, m, 1:T], ALU.subtract).then_inc(shifted.sem, 1)
                v.tensor_scalar(xx[:, :, 0:1], h[:, :, 0:1], -1.0, None, ALU.mult).then_inc(shifted.sem, 1)
        for s, c in ((summed, 1), (root, 1), (inverse, 1), (normed, KD), (shifted, KD + 1)):
            s.base += c
        with ExitStack() as st2:
            xs = Split(st2, k, "xs", KD, T)
            for i, out in ((0, r), (2, kk), (3, vv)):
                linear(k, KD, KD, xs, act=copy_out(k, out), feed=Mix(k, h, xx, xm, xs, i))
        with k.tile("lora_a", [P, KD, 288], F32) as wa, nc.Block() as block:
            parts = [(1, 4, 0, 64), (4, 5, 64, 64), (5, 6, 128, P), (5, 7, 256, 32)]

            @block.sync
            def _(sp):
                sp.dma_start(wa[:, :, :], a["lora_a"]).then_inc(ld.sem, 16)

            @block.vector
            def _(v):
                for n, i in enumerate((1, 4, 5)):
                    for m in range(KD):
                        t = n * KD + m
                        if t >= 4:
                            v.wait_ge(xu.sem, xu(t - 3))
                        v.scalar_tensor_tensor(xm[:, t % 4, :], xx[:, m, :], k.vec("mu", 8 * i + m), h[:, m, :],
                                               ALU.mult, ALU.add).then_inc(mixed.sem, 1)

            @block.tensor
            def _(pe):
                pe.wait_ge(ld.sem, ld(16))
                for n, i in enumerate((1, 4, 5)):
                    for m in range(KD):
                        t = n * KD + m
                        pe.wait_ge(mixed.sem, mixed(t + 1))
                        for mu, bank, c, w in parts:
                            if mu == i:
                                mm = pe.matmul(k.ps[0:w, bank, :], wa[:, m, c:c + w], xm[:, t % 4, :], start=(m == 0),
                                               stop=(m == KD - 1))
                        mm.then_inc(xu.sem, 1)

            @block.scalar
            def _(act):
                act.wait_ge(xu.sem, xu(KD))
                act.activation(inner_w[0:64, :], k.ps[0:64, 4, :], ACT.Tanh).then_inc(inner_r.sem, 1)
                act.wait_ge(xu.sem, xu(2 * KD))
                act.activation(inner_a[0:64, :], k.ps[0:64, 5, :], ACT.Copy).then_inc(inner_r.sem, 1)
                act.wait_ge(xu.sem, xu(3 * KD))
                act.activation(inner_g[:, 0, :], k.ps[:, 6, :], ACT.Sigmoid).then_inc(inner_r.sem, 1)
                act.activation(inner_g[0:32, 1, :], k.ps[0:32, 7, :], ACT.Sigmoid).then_inc(inner_r.sem, 1)
        ld.base += 16
        mixed.base += 3 * KD
        xu.base += 3 * KD
        inner_r.base += 4


def low_rank_outputs(k, a, inner_w, inner_a, sg, aa):
    ld, s2, t2 = k.sig("lora_loaded", "lora_out", "lora_taken")
    with k.tile("lora_b", [P, 2, D], F32) as wb, k.nc.Block() as block:
        @block.sync
        def _(sp):
            sp.dma_start(wb[0:64, :, :], a["lora_b"][0:64, 0:2, :]).then_inc(ld.sem, 16)

        @block.tensor
        def _(pe):
            pe.wait_ge(ld.sem, ld(16))
            for n, src in enumerate((inner_w, inner_a)):
                for m in range(KD):
                    t = n * KD + m
                    if t >= 4:
                        pe.wait_ge(t2.sem, t2(t - 3))
                    pe.matmul(k.ps[:, 4 + t % 4, :], wb[0:64, n, m * P:(m + 1) * P], src[0:64, :], start=True, stop=True
                              ).then_inc(s2.sem, 1)

        @block.scalar
        def _(act):
            for n, (dst, bias) in enumerate(((sg, "w0"), (aa, "a0"))):
                for m in range(KD):
                    t = n * KD + m
                    act.wait_ge(s2.sem, s2(t + 1))
                    act.activation(dst[:, m, :], k.ps[:, 4 + t % 4, :], ACT.Sigmoid, bias=k.vec(bias, m)).then_inc(t2.sem, 1)
    ld.base += 16
    s2.base += 2 * KD
    t2.base += 2 * KD


class Pairs:

    C = NB
    MID = 64

    def __init__(self, k, stack, r, kk, vv, sg, aa):
        self.k, self.r, self.kk, self.vv, self.sg, self.aa = k, r, kk, vv, sg, aa
        sb = lambda name, *shape: stack.enter_context(k.tile(f"pair_{name}", [P, *shape], F32))
        self.kkn, self.kn, self.ba, self.t0, self.t1 = (sb(n, T) for n in ("kkn", "kn", "ba", "t0", "t1"))
        self.L, self.Em = sb("L", NB, P + 1), sb("Em", NB, P)
        self.AR, self.B, self.K = sb("AR", 2, NB, 2 * P), sb("B", NB, P), sb("K", NB, P)
        self.AT, self.BT, self.KT, self.VT = (sb(n, NB, P) for n in ("AT", "BT", "KT", "VT"))
        self.M, self.T, self.Tt, self.U, self.Mo = sb("M", 8, T), sb("T", 8, P), sb("Tt", 8, P), sb("U", 8, P), sb("Mo", 2, 8, P)
        self.X, self.H, self.G = sb("X", NB, P), sb("H", NB, P), sb("G", NB, P)
        self.S, self.Ss, self.Spc, self.SA = sb("S", P), sb("Ss", 2, P), sb("Spc", P), sb("SA", 2, P)
        self.sm = sb("sm", 2, 20)

    def bank(self, n):
        return self.k.ps[:, n, :].rearrange("p (u t) -> p u t", u=4)


    def vectors_vector(self, v, p, step):
        k, s = self.k, self.k.sig("vec_vector")
        ts, ta = self.k.sig("vec_tensor", "vec_scalar")
        L, sm = self.L, self.sm[:, p % 2, :]
        AR = self.AR[:, p % 2]
        R_, K_, V_, S_, A_ = (t[:, p, :] for t in (self.r, self.kk, self.vv, self.sg, self.aa))
        cut = lambda t: t.rearrange("p (c t) -> p c t", c=NB)
        if step == 0:
            v.tensor_scalar(self.kkn[:, :], K_, k.vec("k_k", p), None, ALU.mult).then_inc(s.sem, 1)
            v.tensor_scalar(self.t0[:, :], A_, -1.0, k.vec("k_a", p), ALU.add, ALU.mult).then_inc(s.sem, 1)
            for i in range(NB):
                v.tensor_tensor_scan(L[:, i, 1:P + 1], k.ones[:, :], S_[:, i * P:(i + 1) * P], 0.0, ALU.mult, ALU.add
                                     ).then_inc(s.sem, 1)
        if step == 1:
            v.wait_ge(s.sem, s(6))
            v.scalar_tensor_tensor(self.kn[:, :], self.t0[:, :], 1.0, K_, ALU.add, ALU.mult).then_inc(s.sem, 1)
            v.tensor_scalar(sm[:, 0:4], L[:, :, self.MID], DECAY, None, ALU.mult).then_inc(s.sem, 1)
            v.tensor_scalar(sm[:, 4:8], L[:, :, self.MID], -DECAY, None, ALU.mult).then_inc(s.sem, 1)
            v.wait_ge(s.sem, s(7))
            v.scalar_tensor_tensor(self.t0[:, :], R_, k.vec("r_k", p), self.kn[:, :], ALU.mult, ALU.mult).then_inc(s.sem, 1)
        if step == 2:
            v.wait_ge(ta.sem, ta(2))
            v.tensor_scalar(self.t1[:, :], self.t1[:, :], 1e-12, None, ALU.max).then_inc(s.sem, 1)
            v.wait_ge(s.sem, s(11))
            v.reciprocal(self.t1[:, :], self.t1[:, :]).then_inc(s.sem, 1)
        if step == 3:
            v.wait_ge(s.sem, s(12))
            v.tensor_tensor(self.kkn[:, :], self.kkn[:, :], self.t1[:, :], ALU.mult).then_inc(s.sem, 1)
            v.wait_ge(ts.sem, ts(2))
            v.wait_ge(s.sem, s(13))
            v.tensor_tensor(self.ba[:, :], self.kkn[:, :], A_, ALU.mult).then_inc(s.sem, 1)
            v.tensor_tensor(K_, V_, k.ps[:, 7, :], ALU.mult).then_inc(s.sem, 1)
        if step == 4:
            v.wait_ge(ta.sem, ta(12))
            v.scalar_tensor_tensor(AR[:, :, 0:P], cut(self.kkn[:, :]), -1.0, L[:, :, 0:P], ALU.mult, ALU.mult
                                   ).then_inc(s.sem, 1)
            v.tensor_tensor(AR[:, :, P:2 * P], cut(R_), L[:, :, 1:P + 1], ALU.mult).then_inc(s.sem, 1)
            v.wait_ge(s.sem, s(14))
            v.tensor_tensor(self.B[:, :, :], cut(self.ba[:, :]), self.Em[:, :, :], ALU.mult).then_inc(s.sem, 1)
            v.tensor_tensor(self.K[:, :, :], cut(self.kn[:, :]), self.Em[:, :, :], ALU.mult).then_inc(s.sem, 1)

    def vectors_scalar(self, act, p, step):
        k, s = self.k, self.k.sig("vec_scalar")
        ts, tv, z = self.k.sig("vec_tensor", "vec_vector", "zeroed")
        L, sm = self.L, self.sm[:, p % 2, :]
        if step == 0:
            act.wait_ge(tv.sem, tv(1))
            act.activation(self.t1[:, :], self.kkn[:, :], ACT.Square).then_inc(s.sem, 1)
        if step == 1:
            act.wait_ge(ts.sem, ts(1))
            act.activation(self.t1[:, :], k.ps[:, 6, :], ACT.Sqrt).then_inc(s.sem, 1)
        if step == 2:
            act.wait_ge(tv.sem, tv(9))
            act.activation(sm[:, 8:12], L[:, :, self.MID], ACT.Exp, scale=-DECAY).then_inc(s.sem, 1)
            act.activation(sm[:, 12:16], L[:, :, P], ACT.Exp, scale=-DECAY).then_inc(s.sem, 1)
            for i in range(NB):
                act.activation(self.Em[:, i, :], L[:, i, 1:P + 1], ACT.Exp, scale=DECAY, bias=sm[:, 4 + i:5 + i]
                               ).then_inc(s.sem, 1)
        if step == 3:
            act.wait_ge(z.sem, z(1))
            act.wait_ge(s.sem, s(8))
            for i in range(NB):
                act.activation(L[:, i, :], L[:, i, :], ACT.Exp, scale=-DECAY, bias=sm[:, i:i + 1]).then_inc(s.sem, 1)
            act.wait_ge(s.sem, s(12))
            act.activation(sm[:, 16:20], L[:, :, P], ACT.Copy).then_inc(s.sem, 1)

    def vectors_tensor(self, pe, p, step):
        k, s = self.k, self.k.sig("vec_tensor")
        ta, tv = self.k.sig("vec_scalar", "vec_vector")
        if step == 0:
            pe.wait_ge(ta.sem, ta(1))
            pe.matmul(k.ps[:, 6, :], k.blockones, self.t1[:, :], start=True, stop=True).then_inc(s.sem, 1)
        if step == 1:
            pe.wait_ge(tv.sem, tv(10))
            pe.matmul(k.ps[:, 7, :], k.blockones, self.t0[:, :], start=True, stop=True).then_inc(s.sem, 1)

    def vectors_pool(self, g, p):
        g.memset(self.L[:, :, 0:1], 0.0).then_inc(self.k.sig("zeroed").sem, 1)


    def products_tensor(self, pe, p):
        k = self.k
        tv, tok, tokc, pr, prm, i1, t0, yc = k.sig("vec_vector", "by_token", "by_token_taken", "products", "masked",
                                                   "single_inverse", "single_turned", "y_taken")
        AR = self.AR[:, p % 2]
        pe.wait_ge(tv.sem, tv(19))
        for n, src in enumerate((lambda i: AR[:, i, 0:P], lambda i: self.B[:, i, :], lambda i: self.K[:, i, :],
                                 lambda i: self.vv[:, p, i * P:(i + 1) * P])):
            for i in range(NB):
                mm = pe.transpose(self.bank(n)[:, i, :], src(i), k.ident)
            mm.then_inc(tok.sem, 1)
        for q in range(8):
            i, o = q // 2, 64 * (q % 2)
            if q >= 2:
                pe.wait_ge(prm.sem, prm(q - 1))
            pe.matmul(k.ps[:, 4 + q % 2, 0:256], self.B[o:o + 64, i, :], AR[o:o + 64, i, :], start=True, stop=True)
            pe.matmul(k.ps[:, 4 + q % 2, 256:512], self.K[o:o + 64, i, :], AR[o:o + 64, i, :], start=True, stop=True
                      ).then_inc(pr.sem, 1)
        for b in range(2):
            pe.wait_ge(i1.sem, i1(b + 1))
            if p:
                pe.wait_ge(yc.sem, yc(4))
            for q in range(4):
                mm = pe.transpose(self.bank(6 + b)[:, q, :], self.Tt[:, 4 * b + q, :], k.ident)
            mm.then_inc(t0.sem, 1)

    def products_scalar(self, act, p):
        k = self.k
        tok, tokc, t0, t0c = k.sig("by_token", "by_token_taken", "single_turned", "single_taken")
        for n, dst in enumerate((self.AT, self.BT, self.KT, self.VT)):
            act.wait_ge(tok.sem, tok(n + 1))
            act.activation(dst[:, :, :], self.bank(n), ACT.Copy).then_inc(tokc.sem, 1)
        for b in range(2):
            act.wait_ge(t0.sem, t0(b + 1))
            act.activation(self.T[:, 4 * b:4 * b + 4, :], self.bank(6 + b), ACT.Copy).then_inc(t0c.sem, 1)

    def products_vector(self, v, p):
        k = self.k
        pr, prm, i0, i1 = k.sig("products", "masked", "single_coupled", "single_inverse")
        for q in range(8):
            v.wait_ge(pr.sem, pr(q + 1))
            v.tensor_tensor(self.M[:, q, :], k.ps[:, 4 + q % 2, :], k.cst("m4", 512), ALU.mult).then_inc(prm.sem, 1)
        mask = k.consts[:, CST["levels"]:CST["levels"] + P].unsqueeze(1).to_broadcast([P, 4, P])
        ident = k.ident.unsqueeze(1).to_broadcast([P, 4, P])
        for b in range(2):
            u = self.Tt[:, 4 * b:4 * b + 4, :]
            v.wait_ge(prm.sem, prm(4 * b + 4))
            v.tensor_tensor(u, self.M[:, 4 * b:4 * b + 4, 0:P], mask, ALU.mult).then_inc(i0.sem, 1)
            v.wait_ge(i0.sem, i0(b + 1))
            v.tensor_tensor(u, u, ident, ALU.add).then_inc(i1.sem, 1)

    def advance_products(self):
        for n, c in (("by_token", 4), ("by_token_taken", 4), ("products", 8), ("masked", 8), ("single_coupled", 2),
                     ("single_inverse", 2), ("single_turned", 2), ("single_taken", 2)):
            self.k.sig(n).base += c

    def advance_vectors(self):
        for n, c in (("vec_vector", 19), ("vec_scalar", 13), ("vec_tensor", 2), ("zeroed", 1)):
            self.k.sig(n).base += c

    def first(self):
        with self.k.nc.Block() as block:
            @block.vector
            def _(v):
                for t in (self.S, self.Spc):
                    v.memset(t[:, :], 0.0).then_inc(self.k.sig("made").sem, 1)
                for step in range(5):
                    self.vectors_vector(v, 0, step)
                self.products_vector(v, 0)

            @block.scalar
            def _(act):
                for step in range(4):
                    self.vectors_scalar(act, 0, step)
                self.products_scalar(act, 0)

            @block.tensor
            def _(pe):
                for step in range(2):
                    self.vectors_tensor(pe, 0, step)
                self.products_tensor(pe, 0)

            @block.gpsimd
            def _(g):
                self.vectors_pool(g, 0)
        self.k.sig("made").base += 2
        self.advance_vectors()
        self.advance_products()

    def pair(self, p):
        k = self.k
        more = p + 1 < KD
        mo, ur, uc, gr, gtr, tu, ttu = k.sig("coupling", "mo_t", "mo_t_taken", "t_mo_t", "t_mo_t_turned", "t_joined",
                                             "t_turned_joined")
        xr, xc, hr, hc, gs, gc = k.sig("ak_v", "ak_v_taken", "h_sums", "h_taken", "g_sums", "g_taken")
        sar, sat, snr, st, ss, yr, yc = k.sig("sa_sums", "sa_made", "state_sums", "state_made", "state_scaled", "y_sums",
                                              "y_taken")
        tv = k.sig("vec_vector")
        AR, sm = self.AR[:, p % 2], self.sm[:, p % 2, :]
        M, Tm, Tt, U, Mo = self.M, self.T, self.Tt, self.U, self.Mo
        units = lambda t, b: t[:, 4 * b:4 * b + 4, 0:P]
        LV = 6

        with k.nc.Block() as block:
            @block.gpsimd
            def _(g):
                for l in range(1, LV + 1):
                    for b in range(2):
                        if l >= 3:
                            g.wait_ge(ur.sem, ur(2 * (l - 3) + b + 1))
                        c = CST["levels"] + l * P
                        g.tensor_tensor(Mo[:, l % 2, 4 * b:4 * b + 4, :], units(M, b),
                                        k.consts[:, c:c + P].unsqueeze(1).to_broadcast([P, 4, P]), ALU.mult
                                        ).then_inc(mo.sem, 1)
                    if l == 2 and more:
                        self.vectors_pool(g, p + 1)

            @block.tensor
            def _(pe):
                for q in range(8):
                    mm = pe.matmul(self.bank(6 + q // 4)[:, q % 4, :], M[:, q, 256:384], self.VT[:, q // 2, :],
                                   start=True, stop=True)
                    if q % 4 == 3:
                        mm.then_inc(xr.sem, 1)
                for l in range(1, LV + 1):
                    for b in range(2):
                        pe.wait_ge(mo.sem, mo(2 * (l - 1) + b + 1))
                        if l > 1:
                            pe.wait_ge(tu.sem, tu(2 * (l - 2) + b + 1))
                        for q in range(4):
                            mm = pe.matmul(self.bank(3 * b)[:, q, :], Mo[:, l % 2, 4 * b + q, :], Tm[:, 4 * b + q, :],
                                           start=True, stop=True)
                        mm.then_inc(ur.sem, 1)
                    for b in range(2):
                        pe.wait_ge(uc.sem, uc(2 * (l - 1) + b + 1))
                        if l > 1:
                            pe.wait_ge(ttu.sem, ttu(2 * (l - 2) + b + 1))
                        if l < LV:
                            for q in range(4):
                                mm = pe.matmul(self.bank(1 + 3 * b)[:, q, :], Tt[:, 4 * b + q, :], U[:, 4 * b + q, :],
                                               start=True, stop=True)
                            mm.then_inc(gr.sem, 1)
                        for q in range(4):
                            mm = pe.matmul(self.bank(2 + 3 * b)[:, q, :], U[:, 4 * b + q, :], Tt[:, 4 * b + q, :],
                                           start=True, stop=True)
                        mm.then_inc(gtr.sem, 1)
                    if more and l == 2:
                        pe.wait_ge(xc.sem, xc(4))
                        self.vectors_tensor(pe, p + 1, 0)
                    if more and l == 3:
                        self.vectors_tensor(pe, p + 1, 1)
                pe.wait_ge(xc.sem, xc(4))
                for b in range(2):
                    pe.wait_ge(ttu.sem, ttu(2 * (LV - 1) + b + 1))
                    for q in range(4 * b, 4 * b + 4):
                        mm = pe.matmul(self.bank(b)[:, q % 4, :], Tt[:, q, :], self.X[:, q // 2, :], start=True, stop=True)
                    mm.then_inc(hr.sem, 1)
                for q in range(8):
                    i, o = q // 2, 64 * (q % 2)
                    mm = pe.matmul(k.ps[o:o + 64, 3, i * P:(i + 1) * P], self.AT[:, i, o:o + 64], Tt[:, q, :],
                                   start=True, stop=True)
                mm.then_inc(gs.sem, 1)

                def output(i):
                    if i >= 2:
                        pe.wait_ge(yc.sem, yc(i - 1))
                    elif more:
                        pe.wait_ge(tv.sem, tv(15))
                    y = k.ps[:, 6 + i % 2, 0:P]
                    pe.wait_ge(ss.sem, ss(2 * i + 1))
                    pe.matmul(y, self.Ss[:, i % 2, :], AR[:, i, P:2 * P], start=True, stop=False, skip_group_check=True)
                    for hh in range(2):
                        o, q = 64 * hh, 2 * i + hh
                        yo = k.ps[o:o + 64, 6 + i % 2, 0:P]
                        pe.matmul(yo, self.VT[:, i, o:o + 64], M[:, q, 384:512], start=False, stop=False,
                                  skip_group_check=True)
                        mm = pe.matmul(yo, self.SA[:, i % 2, o:o + 64], M[:, q, P:2 * P], start=False, stop=(hh == 1),
                                       skip_group_check=True)
                    mm.then_inc(yr.sem, 1)

                pe.wait_ge(gc.sem, gc(4))
                for i in range(NB):
                    pe.wait_ge(st.sem, st(2 * i + 2))
                    pe.matmul(k.ps[:, 4, 0:P], self.G[:, i, :], self.S[:, :], start=True, stop=True).then_inc(sar.sem, 1)
                    if i < NB - 1:
                        pe.matmul(k.ps[:, 5, 0:P], self.KT[:, i, :], self.VT[:, i, :], start=True, stop=False)
                        pe.wait_ge(sat.sem, sat(i + 1))
                        pe.matmul(k.ps[:, 5, 0:P], self.BT[:, i, :], self.SA[:, i % 2, :], start=False, stop=True
                                  ).then_inc(snr.sem, 1)
                    else:
                        pe.wait_ge(sat.sem, sat(i + 1))
                    output(i)
                if more:
                    self.products_tensor(pe, p + 1)

            @block.scalar
            def _(act):
                def halves(dst, bank, b, done):
                    t = k.ps[:, bank, :].rearrange("p (i h d) -> p i h d", i=2, h=2)
                    for hh in range(2):
                        act.activation(dst[:, 2 * b:2 * b + 2, 64 * hh:64 * hh + 64], t[:, :, hh, 64 * hh:64 * hh + 64],
                                       ACT.Copy).then_inc(done.sem, 1)
                for l in range(1, LV + 1):
                    for b in range(2):
                        act.wait_ge(ur.sem, ur(2 * (l - 1) + b + 1))
                        act.activation(units(U, b), self.bank(3 * b), ACT.Copy).then_inc(uc.sem, 1)
                    if l == 1:
                        for b in range(2):
                            act.wait_ge(xr.sem, xr(b + 1))
                            halves(self.X, 6 + b, b, xc)
                    if more and l < 5:
                        self.vectors_scalar(act, p + 1, l - 1)
                for b in range(2):
                    act.wait_ge(hr.sem, hr(b + 1))
                    halves(self.H, b, b, hc)
                act.wait_ge(gs.sem, gs(1))
                for i in range(NB):
                    act.activation(self.G[:, i, :], k.ps[:, 3, i * P:(i + 1) * P], ACT.Copy, scale=sm[:, 8 + i:9 + i]
                                   ).then_inc(gc.sem, 1)
                for i in range(NB):
                    act.wait_ge(yr.sem, yr(i + 1))
                    act.activation(self.r[:, p, i * P:(i + 1) * P], k.ps[:, 6 + i % 2, 0:P], ACT.Copy).then_inc(yc.sem, 1)
                if more:
                    self.products_scalar(act, p + 1)

            @block.vector
            def _(v):
                if more:
                    self.vectors_vector(v, p + 1, 0)
                for l in range(1, LV + 1):
                    for b in range(2):
                        if l < LV:
                            v.wait_ge(gr.sem, gr(2 * (l - 1) + b + 1))
                            v.tensor_tensor(units(Tm, b), units(Tm, b), self.bank(1 + 3 * b), ALU.add).then_inc(tu.sem, 1)
                        v.wait_ge(gtr.sem, gtr(2 * (l - 1) + b + 1))
                        v.tensor_tensor(units(Tt, b), units(Tt, b), self.bank(2 + 3 * b), ALU.add).then_inc(ttu.sem, 1)
                    if more and l < 5:
                        self.vectors_vector(v, p + 1, l)
                v.memset(self.S[:, :], 0.0).then_inc(st.sem, 2)
                v.wait_ge(hc.sem, hc(4))
                for i in range(NB):
                    v.wait_ge(st.sem, st(2 * i + 2))
                    v.tensor_scalar(self.Ss[:, i % 2, :], self.S[:, :], sm[:, 8 + i:9 + i], None, ALU.mult).then_inc(ss.sem, 1)
                    v.tensor_scalar(self.Spc[:, :], self.S[:, :], sm[:, 12 + i:13 + i], None, ALU.mult).then_inc(ss.sem, 1)
                    v.wait_ge(sar.sem, sar(i + 1))
                    v.tensor_tensor(self.SA[:, i % 2, :], k.ps[:, 4, 0:P], self.H[:, i, :], ALU.add).then_inc(sat.sem, 1)
                    if i < NB - 1:
                        v.wait_ge(snr.sem, snr(i + 1))
                        v.wait_ge(ss.sem, ss(2 * i + 2))
                        for hh in range(2):
                            o = slice(64 * hh, 64 * hh + 64)
                            v.scalar_tensor_tensor(self.S[o, o], k.ps[o, 5, o], sm[o, 16 + i:17 + i], self.Spc[o, o],
                                                   ALU.mult, ALU.add).then_inc(st.sem, 1)
                if more:
                    self.products_vector(v, p + 1)
        for s, c in ((mo, 12), (ur, 12), (uc, 12), (gr, 10), (gtr, 12), (tu, 10), (ttu, 12), (xr, 2), (xc, 4), (hr, 2),
                     (hc, 4), (gs, 1), (gc, 4), (sar, 4), (sat, 4), (snr, 3), (st, 8), (ss, 8), (yr, 4), (yc, 4)):
            s.base += c
        if more:
            self.advance_vectors()
            self.advance_products()


def group_norm_and_gate(k, a, y, bonus, inner, z):
    nc = k.nc
    ld, go = k.sig("lora_loaded", "lora_out")
    me, ce, sq, va, rt, iv, n1, n2, nd = k.sig("gn_mean", "gn_centred", "gn_squared", "gn_var", "gn_root", "gn_inverse",
                                                "gn_scaled", "gn_shifted", "gn_done")
    with k.tile("gwb", [P, 2, D], F32) as wb, k.tile("gsq", [P, 2, T], F32) as sqt, \
         k.tile("grt", [P, 2, T], F32) as rtt, nc.Block() as block:
        @block.sync
        def _(sp):
            sp.dma_start(wb[:, :, :], a["lora_b"][:, 2:4, :]).then_inc(ld.sem, 16)

        @block.vector
        def _(v):
            for m in range(KD):
                v.wait_ge(me.sem, me(m + 1))
                v.scalar_tensor_tensor(y[:, m, :], k.ps[:, m % 2, :], -1.0 / 64, y[:, m, :], ALU.mult, ALU.add
                                       ).then_inc(ce.sem, 1)
                v.wait_ge(rt.sem, rt(m + 1))
                v.reciprocal(k.ps[:, 4, :], rtt[:, m % 2, :]).then_inc(iv.sem, 1)
                v.wait_ge(iv.sem, iv(m + 1))
                v.scalar_tensor_tensor(y[:, m, :], y[:, m, :], k.vec("ln_g", m), k.ps[:, 4, :], ALU.mult, ALU.mult
                                       ).then_inc(n1.sem, 1)
                v.wait_ge(n1.sem, n1(m + 1))
                v.scalar_tensor_tensor(y[:, m, :], y[:, m, :], k.vec("ln_b", m), bonus[:, m, :], ALU.add, ALU.add
                                       ).then_inc(n2.sem, 1)
                v.wait_ge(n2.sem, n2(m + 1))
                v.wait_ge(go.sem, go(m + 1))
                v.tensor_tensor(z[:, m, :], y[:, m, :], k.ps[:, 5 + m % 2, :], ALU.mult).then_inc(nd.sem, 1)

        @block.tensor
        def _(pe):
            pe.wait_ge(ld.sem, ld(16))

            def mean(m):
                if m >= 2:
                    pe.wait_ge(ce.sem, ce(m - 1))
                pe.matmul(k.ps[:, m % 2, :], k.blockones, y[:, m, :], start=True, stop=True).then_inc(me.sem, 1)
            mean(0)
            for m in range(KD):
                if m + 1 < KD:
                    mean(m + 1)
                if m >= 2:
                    pe.wait_ge(nd.sem, nd(m - 1))
                pe.matmul(k.ps[:, 5 + m % 2, :], wb[:, 0, m * P:(m + 1) * P], inner[:, 0, :], start=True, stop=False)
                pe.matmul(k.ps[:, 5 + m % 2, :], wb[0:32, 1, m * P:(m + 1) * P], inner[0:32, 1, :], start=False, stop=True
                          ).then_inc(go.sem, 1)
                pe.wait_ge(sq.sem, sq(m + 1))
                if m >= 2:
                    pe.wait_ge(rt.sem, rt(m - 1))
                pe.matmul(k.ps[:, 2 + m % 2, :], k.blockones, sqt[:, m % 2, :], start=True, stop=True).then_inc(va.sem, 1)

        @block.scalar
        def _(act):
            for m in range(KD):
                act.wait_ge(ce.sem, ce(m + 1))
                if m >= 2:
                    act.wait_ge(va.sem, va(m - 1))
                act.activation(sqt[:, m % 2, :], y[:, m, :], ACT.Square).then_inc(sq.sem, 1)
                act.wait_ge(va.sem, va(m + 1))
                if m >= 2:
                    act.wait_ge(iv.sem, iv(m - 1))
                act.activation(rtt[:, m % 2, :], k.ps[:, 2 + m % 2, :], ACT.Sqrt, scale=1.0 / 64, bias=k.bias[64e-5]
                               ).then_inc(rt.sem, 1)
    ld.base += 16
    for s in (me, ce, sq, va, rt, iv, n1, n2, nd, go):
        s.base += KD


def rwkv(k, a, ring):
    nc = k.nc
    with ExitStack() as outer:
        tile = lambda st, name, *shape: st.enter_context(k.tile(name, [P, *shape], F32))
        r, kk, vv = (tile(outer, n, KD, T) for n in ("r", "kk", "vv"))
        inner_g, inner_w, inner_a = tile(outer, "inner_g", 2, T), tile(outer, "inner_w", T), tile(outer, "inner_a", T)
        with ExitStack() as first:
            open_ring(k, first, 3 * KD)
            time_mix_inputs(k, a, r, kk, vv, inner_w, inner_a, inner_g)
            close_ring(k)
        with ExitStack() as stack:
            sg, aa = tile(stack, "sg", KD, T), tile(stack, "aa", KD, T)
            low_rank_outputs(k, a, inner_w, inner_a, sg, aa)
            pairs = Pairs(k, stack, r, kk, vv, sg, aa)
            pairs.first()
            for p in range(KD):
                pairs.pair(p)
        with ExitStack() as last:
            z = tile(last, "z", KD, T)
            group_norm_and_gate(k, a, r, kk, inner_g, z)
            open_ring(k, last, KD)
            zs = Split(last, k, "z", KD, T)
            split_tiles(k, z, zs, KD)
            residual(k, KD, zs)
            close_ring(k)



def norm_memory(k, mem):
    squared, summed, root, inverse, normed = k.sig("squared", "summed", "root", "inverse", "normed")
    with k.tile("sqm", [P, KD, MEM], F32) as sq, k.nc.Block() as block:
        @block.scalar
        def _(act):
            for m in range(KD):
                act.activation(sq[:, m, :], mem[:, m, :], ACT.Square).then_inc(squared.sem, 1)
            act.wait_ge(summed.sem, summed(1))
            act.activation(k.root[:, 0:MEM], k.ps[:, 4, 0:MEM], ACT.Sqrt, scale=1.0 / D, bias=k.bias[1e-6]
                           ).then_inc(root.sem, 1)

        @block.tensor
        def _(pe):
            for m in range(KD):
                pe.wait_ge(squared.sem, squared(m + 1))
                mm = pe.matmul(k.ps[:, 4, 0:MEM], k.ones[:, :], sq[:, m, :], start=(m == 0), stop=(m == KD - 1))
            mm.then_inc(summed.sem, 1)

        @block.vector
        def _(v):
            v.wait_ge(root.sem, root(1))
            v.reciprocal(k.root[:, 0:MEM], k.root[:, 0:MEM]).then_inc(inverse.sem, 1)
            v.wait_ge(inverse.sem, inverse(1))
            for m in range(KD):
                v.scalar_tensor_tensor(mem[:, m, :], mem[:, m, :], k.vec("mem_norm", m), k.root[:, 0:MEM],
                                       ALU.mult, ALU.mult).then_inc(normed.sem, 1)
    for s, c in ((squared, KD), (summed, 1), (root, 1), (inverse, 1), (normed, KD)):
        s.base += c


def cross_attention(k, a, layer):
    nc = k.nc
    ml = k.sig("memory_loaded")
    with k.tile("km", [P, KD, MEM], F32) as km, k.tile("vt", [P, 2, D], F32) as vt:
        with k.tile("mem", [P, KD, MEM], F32) as mem, k.tile("kvm", [P, 2 * KD, MEM], F32) as kv:
            with nc.Block() as block:
                @block.sync
                def _(sp):
                    sp.dma_start(mem[:, :, :], a["mem"]).then_inc(ml.sem, 16)
                    sp.wait_ge(ml.sem, ml(16))
            ml.base += 16
            norm_memory(k, mem)
            with ExitStack() as st:
                ms = Split(st, k, "ms", KD, MEM)
                linear(k, 2 * KD, KD, ms, act=copy_out(k, kv, width=MEM), width=MEM, feed=Parts(k, mem, ms, KD))
            tr, te, kc = k.sig("transposed", "transposed_out", "keys_copied")
            with nc.Block() as block:
                @block.tensor
                def _(pe):
                    for n in range(4):
                        mb, half = n % 2, n // 2
                        for q in range(4):
                            mm = pe.transpose(k.ps[:, n, q * P:(q + 1) * P], kv[:, KD + 4 * half + q, mb * P:(mb + 1) * P], k.ident)
                        mm.then_inc(tr.sem, 1)

                @block.scalar
                def _(act):
                    for n in range(4):
                        act.wait_ge(tr.sem, tr(n + 1))
                        act.activation(vt[:, n % 2, (n // 2) * 512:(n // 2) * 512 + 512], k.ps[:, n, :], ACT.Copy
                                       ).then_inc(te.sem, 1)

                @block.gpsimd
                def _(g):
                    g.tensor_copy(km[:, :, :], kv[:, 0:KD, :]).then_inc(kc.sem, 1)
            tr.base += 4
            te.base += 4
            kc.base += 1
        with k.tile("q", [P, KD, T], F32) as q_, k.tile("o", [P, KD, T], F32) as o_:
            with ExitStack() as st:
                h = st.enter_context(k.tile("h", [P, KD, T], F32))
                hs = Split(st, k, "h", KD, T)
                linear(k, KD, KD, hs, act=copy_out(k, q_, scale=1.0 / 16), feed=Norm(k, f"xattn{layer}", hs, h))
            sc, mx, ex, rc, wt, tr, te, po, oe = k.sig("scores", "maxima", "exps", "sums_inverted", "scaled", "transposed",
                                                       "transposed_out", "pv_done", "mixer_out")
            with k.tile("xp", [P, 4, MEM], F32) as p, k.tile("xpt", [P, 2, 2, T], F32) as pt, \
                 k.tile("xst", [P, 3, 16], F32) as st, nc.Block() as block:
                U = 16

                @block.tensor
                def _(pe):
                    def scores(u):
                        h, qb = u // 4, u % 4
                        if u >= 2:
                            pe.wait_ge(ex.sem, ex(u - 1))
                        for c in range(2):
                            mm = pe.matmul(k.ps[:, u % 2, 0:MEM], q_[:, 2 * h + c, qb * P:(qb + 1) * P],
                                           km[:, 2 * h + c, :], start=(c == 0), stop=(c == 1))
                        mm.then_inc(sc.sem, 1)

                    def turn(u):
                        pe.wait_ge(wt.sem, wt(u + 1))
                        if u >= 2:
                            pe.wait_ge(te.sem, te(u - 1))
                        for mb in range(2):
                            mm = pe.transpose(k.ps[:, 2 + u % 2, mb * P:(mb + 1) * P], p[:, u % 4, mb * P:(mb + 1) * P], k.ident)
                        mm.then_inc(tr.sem, 1)

                    def values(h):
                        pe.wait_ge(te.sem, te(4 * h + 4))
                        for db in range(2):
                            if h >= 1:
                                pe.wait_ge(oe.sem, oe(2 * h + db - 1))
                            for mb in range(2):
                                mm = pe.matmul(k.ps[:, 4 + db, :], vt[:, mb, h * 256 + db * P:h * 256 + (db + 1) * P],
                                               pt[:, h % 2, mb, :], start=(mb == 0), stop=(mb == 1))
                            mm.then_inc(po.sem, 1)
                    scores(0)
                    scores(1)
                    for u in range(U):
                        if u + 2 < U:
                            scores(u + 2)
                        turn(u)
                        if u % 4 == 0 and u:
                            values(u // 4 - 1)
                    values(3)

                @block.vector
                def _(v):
                    def out(n):
                        v.wait_ge(po.sem, po(n + 1))
                        v.tensor_copy(o_[:, n, :], k.ps[:, 4 + n % 2, :]).then_inc(oe.sem, 1)

                    def maximum(u):
                        v.wait_ge(sc.sem, sc(u + 1))
                        v.tensor_reduce(st[:, 0, u:u + 1], k.ps[:, u % 2, 0:MEM], AX.X, ALU.max, negate=True
                                        ).then_inc(mx.sem, 1)
                    maximum(0)
                    for u in range(U):
                        if u + 1 < U:
                            maximum(u + 1)
                        v.wait_ge(ex.sem, ex(u + 1))
                        v.reciprocal(st[:, 2, u:u + 1], st[:, 1, u:u + 1]).then_inc(rc.sem, 1)
                        v.wait_ge(rc.sem, rc(u + 1))
                        v.tensor_scalar(p[:, u % 4, :], p[:, u % 4, :], st[:, 2, u:u + 1], None, ALU.mult).then_inc(wt.sem, 1)
                        if u % 4 == 1 and u > 4:
                            out(2 * (u // 4 - 1))
                            out(2 * (u // 4 - 1) + 1)
                    out(6)
                    out(7)

                @block.scalar
                def _(act):
                    def exp(u):
                        act.wait_ge(mx.sem, mx(u + 1))
                        if u >= 4:
                            act.wait_ge(tr.sem, tr(u - 3))
                        act.activation(p[:, u % 4, :], k.ps[:, u % 2, 0:MEM], ACT.Exp, bias=st[:, 0, u:u + 1],
                                       accum_out=st[:, 1, u:u + 1]).then_inc(ex.sem, 1)

                    def take(u):
                        h, qb = u // 4, u % 4
                        act.wait_ge(tr.sem, tr(u + 1))
                        if h >= 2:
                            act.wait_ge(po.sem, po(2 * (h - 1)))
                        act.activation(pt[:, h % 2, :, qb * P:(qb + 1) * P],
                                       k.ps[:, 2 + u % 2, 0:MEM].rearrange("p (m t) -> p m t", m=2), ACT.Copy
                                       ).then_inc(te.sem, 1)
                    exp(0)
                    for u in range(U):
                        if u + 1 < U:
                            exp(u + 1)
                        take(u)
            for s in (sc, mx, ex, rc, wt, tr, te):
                s.base += U
            po.base += 8
            oe.base += 8
            with ExitStack() as st:
                os_ = Split(st, k, "os", KD, T)
                split_tiles(k, o_, os_, KD)
                residual(k, KD, os_)



def conformer(k, a):
    nc = k.nc
    used, free, sig_r, dg, padz = k.sig("chunk_used", "bank_free", "sigmoid_made", "diagonals", "zeroed")
    V_TAPS = TAPS - PE_TAPS
    with k.tile("conv_y", [P, KD, T], F32) as y:
        with k.tile("conv_u", [P, KD, T + TAPS - 1], F32) as u, \
             k.tile("conv_dg", [P, 2, PE_TAPS, P], F32) as diag, k.tile("conv_s", [P, 2, T], F32) as sg:
            def act(e, i, j):
                if j % 2 == 0:
                    return
                f = 2 * i + j // 2
                e.wait_ge(used.sem, used(2 * f + 2))
                if f >= 2:
                    e.wait_ge(free.sem, free(2 * (f - 1) + RING))
                e.activation(sg[:, f % 2, :], k.ps[:, j, :], ACT.Sigmoid, bias=k.vec("cb_in", 8 + f)).then_inc(sig_r.sem, 1)

            def vector(e, i, j):
                if j % 2 == 0:
                    return
                f = 2 * i + j // 2
                e.wait_ge(sig_r.sem, sig_r(f + 1))
                e.scalar_tensor_tensor(u[:, f, TAPS - 1:], k.ps[:, j - 1, :], k.vec("cb_in", f), sg[:, f % 2, :],
                                       ALU.add, ALU.mult).then_inc(free.sem, 2)

            with ExitStack() as st:
                h = st.enter_context(k.tile("h", [P, KD, T], F32))
                hs = Split(st, k, "h", KD, T)
                linear(k, 2 * KD, KD, hs, act=act, vector=vector, unroll=True, feed=Norm(k, "mix1", hs, h))
            sig_r.base += KD
            tp, ac, ye = k.sig("taps_summed", "taps_added", "conv_taken")
            with nc.Block() as block:
                @block.gpsimd
                def _(g):
                    g.memset(u[:, :, 0:TAPS - 1], 0.0).then_inc(padz.sem, 1)
                    for m in range(KD):
                        if m >= 2:
                            g.wait_ge(tp.sem, tp(m - 1))
                        for t in range(PE_TAPS):
                            c = VEC["cdw"] + TAPS * m + t
                            g.tensor_scalar(diag[:, m % 2, t, :], k.ident, k.vecs[:, c:c + 1], None, ALU.mult
                                            ).then_inc(dg.sem, 1)

                @block.tensor
                def _(pe):
                    pe.wait_ge(padz.sem, padz(1))
                    for m in range(KD):
                        if m >= 4:
                            pe.wait_ge(ye.sem, ye(m - 3))
                        for t in range(PE_TAPS):
                            pe.wait_ge(dg.sem, dg(m * PE_TAPS + t + 1))
                            mm = pe.matmul(k.ps[:, m % 4, :], diag[:, m % 2, t, :], u[:, m, t:t + T], start=(t == 0),
                                           stop=(t == PE_TAPS - 1))
                        mm.then_inc(tp.sem, 1)

                @block.vector
                def _(v):
                    n = 0
                    for pair in range(KD // 2):
                        v.wait_ge(tp.sem, tp(2 * pair + 2))
                        for t in range(PE_TAPS, TAPS):
                            for m in (2 * pair, 2 * pair + 1):
                                if t > PE_TAPS:
                                    v.wait_ge(ac.sem, ac(n - 1))
                                c = VEC["cdw"] + TAPS * m + t
                                v.scalar_tensor_tensor(k.ps[:, m % 4, :], u[:, m, t:t + T], k.vecs[:, c:c + 1],
                                                       k.ps[:, m % 4, :], ALU.mult, ALU.add).then_inc(ac.sem, 1)
                                n += 1

                @block.scalar
                def _(act):
                    for m in range(KD):
                        act.wait_ge(ac.sem, ac((m // 2) * 2 * V_TAPS + 2 * V_TAPS - (1 - m % 2)))
                        act.activation(y[:, m, :], k.ps[:, m % 4, :], ACT.Identity, bias=k.vec("cdw_b", m)).then_inc(ye.sem, 1)
            padz.base += 1
            dg.base += KD * PE_TAPS
            tp.base += KD
            ac.base += KD * V_TAPS
            ye.base += KD
        me, ce, sq, va, rt, iv, n1, n2 = k.sig("gn_mean", "gn_centred", "gn_squared", "gn_var", "gn_root", "gn_inverse",
                                               "gn_scaled", "gn_shifted")
        with k.tile("ln_sq", [P, KD, T], F32) as sqt, k.tile("ln_rt", [P, T], F32) as rtt, \
             nc.Block() as block:
            @block.tensor
            def _(pe):
                for m in range(KD):
                    mm = pe.matmul(k.ps[:, 4, :], k.ones[:, :], y[:, m, :], start=(m == 0), stop=(m == KD - 1))
                mm.then_inc(me.sem, 1)
                for m in range(KD):
                    pe.wait_ge(sq.sem, sq(m + 1))
                    mm = pe.matmul(k.ps[:, 5, :], k.ones[:, :], sqt[:, m, :], start=(m == 0), stop=(m == KD - 1))
                mm.then_inc(va.sem, 1)

            @block.vector
            def _(v):
                v.wait_ge(me.sem, me(1))
                for m in range(KD):
                    v.scalar_tensor_tensor(y[:, m, :], k.ps[:, 4, :], -1.0 / D, y[:, m, :], ALU.mult, ALU.add
                                           ).then_inc(ce.sem, 1)
                v.wait_ge(rt.sem, rt(1))
                v.reciprocal(k.ps[:, 6, :], rtt[:, :]).then_inc(iv.sem, 1)
                v.wait_ge(iv.sem, iv(1))
                for m in range(KD):
                    v.scalar_tensor_tensor(y[:, m, :], y[:, m, :], k.vec("cln_g", m), k.ps[:, 6, :], ALU.mult, ALU.mult
                                           ).then_inc(n1.sem, 1)

            @block.scalar
            def _(act):
                for m in range(KD):
                    act.wait_ge(ce.sem, ce(m + 1))
                    act.activation(sqt[:, m, :], y[:, m, :], ACT.Square).then_inc(sq.sem, 1)
                act.wait_ge(va.sem, va(1))
                act.activation(rtt[:, :], k.ps[:, 5, :], ACT.Sqrt, scale=1.0 / D, bias=k.bias[1e-5]).then_inc(rt.sem, 1)
                for m in range(KD):
                    act.wait_ge(n1.sem, n1(m + 1))
                    act.activation(y[:, m, :], y[:, m, :], ACT.Silu, bias=k.vec("cln_b", m)).then_inc(n2.sem, 1)
        me.base += 1
        va.base += 1
        rt.base += 1
        iv.base += 1
        for s in (ce, sq, n1, n2):
            s.base += KD
        with ExitStack() as st:
            ys = Split(st, k, "ys", KD, T)
            split_tiles(k, y, ys, KD)
            residual(k, KD, ys, bias="cb_out")


def conv_ffn(k, layer):
    nc = k.nc
    used, free, ub_r, cv, silu, hi, lo, padz = k.sig(
        "chunk_used", "bank_free", "ffn_copied", "ffn_conv", "ffn_silu", "hidden_hi", "hidden_lo", "zeroed")
    w0 = VEC[f"fdw{layer}"]
    with ExitStack() as st:
        h = st.enter_context(k.tile("h", [P, KD, T], F32))
        hs = Split(st, k, "h", KD, T)
        a_ = Split(st, k, "ffn_a", FFN_PARTS[0], T)
        ub = st.enter_context(k.tile("ffn_u", [P, 4, T + 2], F32))
        sg = st.enter_context(k.tile("ffn_s", [P, 2, T], F32))
        tmp = st.enter_context(k.tile("ffn_t", [P, 2, T], F32))
        with nc.Block() as block:
            @block.gpsimd
            def _(g):
                g.memset(ub[:, :, 0:2], 0.0).then_inc(padz.sem, 1)
        padz.base += 1
        before = 0
        for part, FT in enumerate(FFN_PARTS):
            def act(e, i, j):
                m, f = 4 * i + j, 2 * i + j // 2
                e.wait_ge(used.sem, used(m + 1))
                if m >= 4:
                    e.wait_ge(cv.sem, cv(6 * ((m - 4) // 2) + 5 + m % 2))
                e.activation(ub[:, j, 2:T + 2], k.ps[:, j, :], ACT.Copy).then_inc(ub_r.sem, 1)
                if j % 2:
                    e.wait_ge(cv.sem, cv(6 * f + 6))
                    e.activation(sg[:, f % 2, :], k.ps[:, j - 1, :], ACT.Silu).then_inc(silu.sem, 1)
                    e.wait_ge(free.sem, free(2 * f + 2 + RING))
                    e.activation(a_.hi[:, f, :], tmp[:, f % 2, :], ACT.Copy).then_inc(hi.sem, 1)

            def vector(e, i, j):
                if j % 2 == 0:
                    return
                f = 2 * i + j // 2
                for t in (2, 1, 0):
                    for jj in range(2):
                        m = 2 * f + jj
                        bank = k.ps[:, m % 4, :]
                        c = w0 + 3 * (2 * before + m) + t
                        col = k.vecs[:, c:c + 1]
                        if t == 2:
                            e.wait_ge(ub_r.sem, ub_r(m + 1))
                            e.tensor_scalar(bank, bank, col, None, ALU.mult).then_inc(cv.sem, 1)
                        else:
                            e.wait_ge(cv.sem, cv(6 * f + 2 * (2 - t) + jj - 1))
                            e.scalar_tensor_tensor(bank, ub[:, m % 4, t:t + T], col, bank, ALU.mult, ALU.add
                                                   ).then_inc(cv.sem, 1)
                e.wait_ge(silu.sem, silu(f + 1))
                e.tensor_tensor(tmp[:, f % 2, :], sg[:, f % 2, :], k.ps[:, j, :], ALU.mult).then_inc(free.sem, 2)
                e.wait_ge(hi.sem, hi(f + 1))
                e.tensor_tensor(a_.lo[:, f, :], tmp[:, f % 2, :], as_float(a_.hi[:, f, :]), ALU.subtract).then_inc(lo.sem, 1)
            linear(k, 2 * FT, KD, hs, act=act, vector=vector, unroll=True,
                   feed=None if part else Norm(k, f"ffn{layer}", hs, h))
            ub_r.base += 2 * FT
            cv.base += 6 * FT
            for s in (silu, hi, lo):
                s.base += FT
            residual(k, FT, a_, per=2, squares=(part == 1))
            before += FT


def final_norm(k):
    summed, root, inverse, normed = k.sig("summed", "root", "inverse", "normed")
    with k.nc.Block() as block:
        @block.tensor
        def _(pe):
            pe.matmul(k.ps[:, 4, :], k.ones[:, :], k.squares[:, :], start=True, stop=True).then_inc(summed.sem, 1)

        @block.scalar
        def _(act):
            act.wait_ge(summed.sem, summed(1))
            act.activation(k.root[:, :], k.ps[:, 4, :], ACT.Sqrt, scale=1.0 / D, bias=k.bias[1e-6]).then_inc(root.sem, 1)

        @block.vector
        def _(v):
            v.wait_ge(root.sem, root(1))
            v.reciprocal(k.root[:, :], k.root[:, :]).then_inc(inverse.sem, 1)
            v.wait_ge(inverse.sem, inverse(1))
            for m in range(KD):
                v.scalar_tensor_tensor(k.x[:, m, :], k.x[:, m, :], k.vec("final", m), k.root[:, :],
                                       ALU.mult, ALU.mult).then_inc(normed.sem, 1)
    for s, c in ((summed, 1), (root, 1), (inverse, 1), (normed, KD)):
        s.base += c


def second_block(k, a, stop):
    first = START if START else 2
    if first < 3:
        rwkv(k, a, None)
    if stop == 3:
        return
    with ExitStack() as ring:
        open_ring(k, ring, k.n_chunks - k.chunk)
        if first < 4:
            cross_attention(k, a, 0)
        if stop == 4:
            return
        if first < 5:
            conv_ffn(k, 0)
        if stop == 5:
            return
        if first < 6:
            conformer(k, a)
        if stop == 6:
            return
        if first < 7:
            cross_attention(k, a, 1)
        if stop == 7:
            return
        conv_ffn(k, 1)
        if stop == 8:
            return
        final_norm(k)
        close_ring(k)



def build(nc, a, out, stop=None):
    k = Core(nc)
    k.wall = a["wall"]
    k.n_chunks = a["wall"].shape[0]
    k.x = nc.alloc_sbuf_tensor("x_stream", [P, KD, T], F32)
    k.squares = nc.alloc_sbuf_tensor("squares", [P, T], F32)
    k.root = nc.alloc_sbuf_tensor("root", [P, T], F32)
    k.vecs = nc.alloc_sbuf_tensor("vecs", [P, N_VEC], F32)
    k.consts = nc.alloc_sbuf_tensor("consts", [P, N_KEEP], F32)
    k.ones = nc.alloc_sbuf_tensor("ones", [P, P], F32)
    k.negones = nc.alloc_sbuf_tensor("negones", [P, P], F32)
    k.eps = nc.alloc_sbuf_tensor("eps", [P, 8], F32)
    k.ps = nc.alloc_psum_tensor("ps", [P, 8, 512], F32)
    k.ident = k.cst("ident", 128)
    k.blockones = k.cst("blockones", 128)
    k.negtri = k.cst("negtri", 128)
    if START:
        c0 = {2: 96, 3: 128, 4: 160, 5: 160 + 76, 6: 160 + 76 + 24, 7: 160 + 76 + 24 + 32}[START]
        k.wall = a["wall"][c0:]
        k.n_chunks -= c0
    load_everything(k, a)
    if not START:
        with ExitStack() as ring:
            open_ring(k, ring, N_PROJ + KD + 64)
            first_block(k, a, stop)
            if stop != 1:
                close_ring(k)
    if stop not in (1, 2):
        second_block(k, a, stop)
    stored = k.sig("stored")
    with nc.Block() as block:
        @block.sync
        def _(sp):
            sp.dma_start(out, k.x[:, :, :]).then_inc(stored.sem, 16)
            sp.wait_ge(stored.sem, stored(16))


def chunks(w):
    K, M = w.shape
    per = -(-K // 1024)
    full = np.zeros((per * 1024, M), w.dtype)
    full[:K] = w
    return np.ascontiguousarray(full.reshape(per, 8, P, M // P, P).transpose(3, 0, 2, 1, 4)).reshape(-1, P, 1024)


def interleave(w, pairs):
    K = w.shape[0]
    return w.reshape(K, 2, pairs, P).transpose(0, 2, 1, 3).reshape(K, -1)


def layout(i):
    c = lambda *s: np.arange(*s)
    w_in = np.asarray(i["w_in"])[0]
    q0, kv0, g0, d0, s0 = 0, 256, 640, 652, 1804
    kv = lambda n: c(kv0 + 64 * n, kv0 + 64 * n + 64)
    cols = np.concatenate([c(0, 256), kv(0), kv(1), kv(2), kv(2), kv(4), kv(4), kv(3), kv(5), c(d0, s0), c(s0, s0 + 1152)])
    n = {m: np.asarray(v) for m, v in i.items()}
    fw = lambda l: interleave(n["ffn_w_in_2"][l], F2 // P)
    cut = FFN_PARTS[0] * P
    ffn = lambda l: [fw(l)[:, :2 * cut], n["ffn_w_out_2"][l][:cut], fw(l)[:, 2 * cut:], n["ffn_w_out_2"][l][cut:]]
    wall = np.concatenate([chunks(w) for w in [
        w_in[:, cols], n["w_out"][0],
        n["w_up"][0][:, :F1 // 2], n["w_down"][0][:F1 // 2], n["w_up"][0][:, F1 // 2:], n["w_down"][0][F1 // 2:],
        n["rwkv_w_r_2"][0], n["rwkv_w_k_2"][0], n["rwkv_w_v_2"][0], n["rwkv_w_o_2"][0],
        n["xattn_w_kv_2"][0], n["xattn_w_q_2"][0], n["xattn_w_o_2"][0], *ffn(0),
        interleave(n["conv_w_in_2"][0], 8), n["conv_w_out_2"][0],
        n["xattn_w_kv_2"][1], n["xattn_w_q_2"][1], n["xattn_w_o_2"][1], *ffn(1)]])
    col = lambda v: v.reshape(-1, P).T
    fdw = lambda l: n["ffn_dw_2"][l].reshape(3, 2, F2 // P, P).transpose(3, 2, 1, 0).reshape(P, -1)
    gains = np.concatenate([n["qk_gain_nsa"][0], n["qk_gain_dil"][0]])
    vecs = {"norm_mix": col(n["norm_mix"][0]), "norm_mlp": col(n["norm_mlp"][0]), "mem_norm": col(n["mem_norm_g_2"]),
            "mix0": col(n["norm_mix_g_2"][0]), "mix1": col(n["norm_mix_g_2"][1]),
            "xattn0": col(n["norm_xattn_g_2"][0]), "xattn1": col(n["norm_xattn_g_2"][1]),
            "ffn0": col(n["norm_ffn_g_2"][0]), "ffn1": col(n["norm_ffn_g_2"][1]), "final": col(n["final_norm_g_2"]),
            "mu": col(n["rwkv_mu_2"][0]), "w0": col(n["rwkv_w0_2"][0]), "a0": col(n["rwkv_a0_2"][0]),
            "k_k": col(n["rwkv_k_k_2"][0]), "k_a": col(n["rwkv_k_a_2"][0]), "r_k": col(n["rwkv_r_k_2"][0]),
            "ln_g": col(n["rwkv_ln_g_2"][0]), "ln_b": col(n["rwkv_ln_b_2"][0]), "cb_in": col(n["conv_b_in_2"][0]),
            "cdw": n["conv_dw_2"][0].reshape(TAPS, 8, P).transpose(2, 1, 0).reshape(P, -1),
            "cdw_b": col(n["conv_dw_b_2"][0]), "cln_g": col(n["conv_ln_g_2"][0]), "cln_b": col(n["conv_ln_b_2"][0]),
            "cb_out": col(n["conv_b_out_2"][0]), "fdw0": fdw(0), "fdw1": fdw(1),
            "gains": np.concatenate([gains, gains], axis=1).T}
    act = lambda x: np.ascontiguousarray(x.T.reshape(KD, P, -1).transpose(1, 0, 2))
    lora_a = np.concatenate([n["rwkv_w1_2"][0], n["rwkv_a1_2"][0], n["rwkv_g1_2"][0]], axis=1)
    lora_b = np.zeros((4, P, D), lora_a.dtype)
    lora_b[0, :64], lora_b[1, :64] = n["rwkv_w2_2"][0], n["rwkv_a2_2"][0]
    lora_b[2], lora_b[3, :32] = n["rwkv_g2_2"][0][:P], n["rwkv_g2_2"][0][P:]
    w2 = n["cmp_w2"][0]
    return {
        "x": act(n["x"][0]), "mem": act(n["mem_2"][0]), "wall": wall,
        "vecs": np.ascontiguousarray(np.concatenate([vecs[m] for m, _ in VEC_SIZES], axis=1)),
        "consts": constants(),
        "w_gate": np.ascontiguousarray(w_in[:, g0:d0].reshape(KD, P, 12).transpose(1, 0, 2)),
        "cmp_w1": np.ascontiguousarray(n["cmp_w1"][0].reshape(2, 32, 64, 128).transpose(0, 2, 1, 3)).reshape(P, 32, 128),
        "cmp_w2": np.ascontiguousarray(np.concatenate([w2[0], w2[0], w2[1]], axis=1)),
        "cmp_pe": np.ascontiguousarray(n["cmp_pe"][0].transpose(0, 2, 1)).reshape(P, 32),
        "lora_a": np.ascontiguousarray(lora_a.reshape(KD, P, 288).transpose(1, 0, 2)),
        "lora_b": np.ascontiguousarray(lora_b.transpose(1, 0, 2)),
    }


def constants():
    p = np.arange(P)[:, None]
    q = np.arange(P)[None]
    c = {}
    c["ident"] = (p == q)
    c["blockones"] = (p // 64 == q // 64)
    c["negtri"] = -1.0 * (p >= q)
    c["m4"] = np.concatenate([p < q, p <= q, p < q, p <= q], axis=1)
    c["levels"] = np.concatenate([((p // b) % 2 == 0) & (q // b == p // b + 1) for b in (1, 2, 4, 8, 16, 32, 64)], axis=1)
    far = (p + 3 * P) - np.arange(T)[None]
    ok = [far >= 0, (far >= 0) & (far <= 128), (far >= 0) & (far % 4 == 0), (far >= 0) & (far % 16 == 0)]
    c["dist"] = np.concatenate([np.where(m, -1.0 * far, NEG) for m in ok], axis=1)
    far = (np.arange(NB)[None, :, None] * P + np.arange(P)[:, None, None]) - (16 * np.arange(32)[None, None] + 31)
    c["dist_cmp"] = np.where(far >= 0, -1.0 * far, NEG).reshape(P, -1)
    c["valid"] = (p >= 31)
    return np.ascontiguousarray(np.concatenate([c[m].astype(np.float32) for m, _ in CONST_SIZES], axis=1))


def kernel(**inputs):
    import concourse.bacc as _bacc
    from concourse.bass_utils import run_bass_kernel_spmd as _run

    nc = _bacc.Bacc("TRN2", target_bir_lowering=False, num_devices=1)
    arrays, args = {}, {}
    for name, v in layout(inputs).items():
        arrays[f"in_{name}"] = v
        args[name] = nc.dram_tensor(f"in_{name}", v.shape, mybir.dt.from_np(v.dtype), kind="ExternalInput").ap()
    out = nc.dram_tensor("out_y", [P, KD, T], F32, kind="ExternalOutput").ap()
    build(nc, args, out)
    r = _run(nc, [arrays], core_ids=[0])
    y = r.results[0]["out_y"]
    return np.ascontiguousarray(y.transpose(2, 1, 0)).reshape(1, T, D)
```

```python
from contextlib import ExitStack

import numpy as np
import concourse.bass as bass
from concourse import mybir

F32 = mybir.dt.float32
F32R = mybir.dt.float32r
ACT = mybir.ActivationFunctionType
ALU = mybir.AluOpType
AX = mybir.AxisListType

P = 128
T = 512
D = 1024
KD = D // P
HD = 64
NB = T // P
MEM = 256
RING = 4
AHEAD = 2
N_CMP = 31
SLOPES = [float(2.0 ** (-8.0 * i / 10)) for i in range(1, 11)]
DECAY = float(np.exp(-0.5))
NEG = -1e30

T_Q, T_CMP, T_KSEL, T_KWIN, T_V, T_DQ, T_DK, T_DV, T_SQ, T_SK, T_SV = 0, 2, 3, 4, 5, 6, 9, 12, 15, 18, 21
N_PROJ = 24
V_TILES = [T_V, T_DV, T_DV + 1, T_DV + 2, T_SV, T_SV + 1, T_SV + 2]

F1 = 4096
F2 = 2816
FFN_PARTS = (12, 10)
TAPS = 31
PE_TAPS = 13

VEC_SIZES = [("norm_mix", 8), ("norm_mlp", 8), ("mem_norm", 8), ("mix0", 8), ("mix1", 8),
             ("xattn0", 8), ("xattn1", 8), ("ffn0", 8), ("ffn1", 8), ("final", 8), ("mu", 48),
             ("w0", 8), ("a0", 8), ("k_k", 8), ("k_a", 8), ("r_k", 8), ("ln_g", 8), ("ln_b", 8),
             ("cb_in", 16), ("cdw", 8 * TAPS), ("cdw_b", 8), ("cln_g", 8), ("cln_b", 8), ("cb_out", 8),
             ("fdw0", 44 * 3), ("fdw1", 44 * 3), ("gains", 6)]
VEC = {}
_at = 0
for _n, _s in VEC_SIZES:
    VEC[_n] = _at
    _at += _s
N_VEC = _at

HEAD_TILES = 10

CONST_SIZES = [("ident", 128), ("blockones", 128), ("negtri", 128), ("m4", 512), ("levels", 7 * 128),
               ("dist", 4 * 512), ("dist_cmp", 4 * 32), ("valid", 1),
               ("pick", 4 * HEAD_TILES - 2), ("spread", HEAD_TILES * P), ("pick_scale", 1), ("pick_bias", 1)]
CST = {}
_at = 0
for _n, _s in CONST_SIZES:
    CST[_n] = _at
    _at += _s
N_CONST = _at
N_KEEP = CST["dist"]


class Signal:

    def __init__(self, nc, name):
        self.sem = nc.alloc_semaphore(name)
        self.base = 0

    def __call__(self, n):
        return self.base + n


class Core:

    def __init__(self, nc):
        self.nc = nc
        self.signals = {}
        self.tiles = 0
        self.chunk = 0
        self.first = self.limit = 0

    def tile(self, name, shape, dtype):
        self.tiles += 1
        return self.nc.sbuf_tensor(f"{name}_{self.tiles}", shape, dtype)

    def sig(self, *names):
        for n in names:
            if n not in self.signals:
                self.signals[n] = Signal(self.nc, n)
        out = [self.signals[n] for n in names]
        return out if len(out) > 1 else out[0]

    def slots(self):
        return [self.sig(f"slot{j}_loaded") for j in range(RING)]

    def vec(self, name, i):
        c = VEC[name] + i
        return self.vecs[:, c:c + 1]

    def cst(self, name, w):
        return self.consts[:, CST[name]:CST[name] + w]


class Split:

    def __init__(self, stack, k, name, *shape):
        self.hi = stack.enter_context(k.tile(f"{name}_hi", [P, *shape], F32R))
        self.lo = stack.enter_context(k.tile(f"{name}_lo", [P, *shape], F32R))


def as_float(t):
    return t.bitcast(F32)


def load_everything(k, a):
    loaded, made, free, used, sq, ac = k.sig("loaded", "made", "bank_free", "chunk_used", "squared", "squares_added")
    with k.tile("sq0", [P, KD, T], F32) as sqt, k.nc.Block() as block:
        @block.sync
        def _(sp):
            sp.dma_start(k.x[:, :, :], a["x"]).then_inc(loaded.sem, 16)

        @block.scalar
        def _(act):
            act.dma_start(k.vecs[:, :], a["vecs"]).then_inc(loaded.sem, 16)
            act.dma_start(k.consts[:, :], a["consts"][:, 0:N_KEEP]).then_inc(loaded.sem, 16)
            act.wait_ge(loaded.sem, loaded(48))
            for m in range(KD):
                act.activation(sqt[:, m, :], k.x[:, m, :], ACT.Square).then_inc(sq.sem, 1)

        @block.vector
        def _(v):
            v.memset(k.ones[:, :], 1.0).then_inc(made.sem, 1)
            v.memset(k.negones[:, :], -1.0).then_inc(made.sem, 1)
            for n, value in enumerate([1e-6, 64e-6, 64e-5, 1e-5, 1.0]):
                v.memset(k.eps[:, n:n + 1], value).then_inc(made.sem, 1)
            v.wait_ge(made.sem, made(7))
            v.sem_inc(free.sem, RING)
            v.sem_inc(used.sem, RING)
            v.wait_ge(sq.sem, sq(2))
            v.tensor_tensor(k.squares[:, :], sqt[:, 0, :], sqt[:, 1, :], ALU.add).then_inc(ac.sem, 1)
            for m in range(2, KD):
                v.wait_ge(sq.sem, sq(m + 1))
                v.wait_ge(ac.sem, ac(m - 1))
                v.tensor_tensor(k.squares[:, :], k.squares[:, :], sqt[:, m, :], ALU.add).then_inc(ac.sem, 1)
    loaded.base += 48
    made.base += 7
    sq.base += KD
    ac.base += KD - 1
    used.base += RING
    k.bias = {1e-6: k.eps[:, 0:1], 64e-6: k.eps[:, 1:2], 64e-5: k.eps[:, 2:3], 1e-5: k.eps[:, 3:4], 1.0: k.eps[:, 4:5]}


def open_ring(k, stack, n_chunks):
    k.raw = stack.enter_context(k.tile("raw", [P, RING, 1024], F32))
    k.w = Split(stack, k, "w", RING, 1024)
    k.first, k.limit = k.chunk, k.chunk + n_chunks
    hi_r, lo_r = k.sig("weights_hi", "weights_lo")
    slots = k.slots()
    with k.nc.Block() as block:
        @block.sync
        def _(sp):
            for n in range(RING + AHEAD):
                if n >= RING:
                    sp.wait_ge(lo_r.sem, lo_r(n - RING + 1))
                sp.dma_start(k.raw[:, n % RING, :], k.wall[k.first + n]).then_inc(slots[n % RING].sem, 16)

        @block.scalar
        def _(act):
            for n in range(AHEAD):
                act.wait_ge(slots[n].sem, slots[n](16))
                act.activation(k.w.hi[:, n, :], k.raw[:, n, :], ACT.Copy).then_inc(hi_r.sem, 1)

        @block.vector
        def _(g):
            for n in range(AHEAD):
                g.wait_ge(hi_r.sem, hi_r(n + 1))
                g.tensor_tensor(k.w.lo[:, n, :], k.raw[:, n, :], as_float(k.w.hi[:, n, :]), ALU.subtract
                                ).then_inc(lo_r.sem, 1)


def close_ring(k):
    for s in k.slots():
        s.base += 16 * ((k.limit - k.first) // RING)


def passes(e, n, first, last):
    a = 1 if first else 0
    b = max(n - 1, a) if last else n
    yield from range(a)
    if b - a == 1:
        yield a
    elif b > a:
        with e.Fori(a, b) as i:
            yield i
    yield from range(b, n)


def linear(k, m_tiles, kt, src, act=None, vector=None, pool=None, width=T, feed=None, unroll=False, norm=False):
    nc = k.nc
    used, free, hi_r, lo_r, fed = k.sig("chunk_used", "bank_free", "weights_hi", "weights_lo", "fed")
    summed, root, inverse = k.sig("summed", "root", "inverse")
    peel = feed is not None or norm
    slots = k.slots()
    per = -(-kt // 8)
    n_groups, N = m_tiles // 4, m_tiles * per
    c0 = k.chunk - k.first
    n_split = min(N, k.limit - k.chunk - AHEAD)
    n_load = min(N, k.limit - k.chunk - AHEAD - RING)
    ending = n_split < N

    def sums(pe, bank, n, q, c, first, last):
        t = 8 * c + q
        w = (n % RING, slice(q * P, (q + 1) * P))
        hi, lo = k.w.hi[:, w[0], w[1]], k.w.lo[:, w[0], w[1]]
        pe.matmul(bank, hi, src.hi[:, t, 0:width], start=first, stop=False)
        pe.matmul(bank, hi, src.lo[:, t, 0:width], start=False, stop=False)
        return pe.matmul(bank, lo, src.hi[:, t, 0:width], start=False, stop=last)

    with nc.Block() as block:
        @block.sync
        def _(sp):
            ahead = AHEAD + RING

            def load(i, j):
                sp.wait_ge(lo_r.sem, lo_r(i * RING + (j + 1 + AHEAD)))
                s = (j + ahead) % RING
                at = k.chunk + j + ahead
                source = k.wall[at + i * RING] if isinstance(i, int) else \
                    k.wall[bass.ds(i * RING + at, 1)].rearrange("o p n -> (o p) n")
                sp.dma_start(k.raw[:, s, :], source).then_inc(slots[s].sem, 16)
            if n_load >= RING:
                for i in passes(sp, n_load // RING, False, False):
                    for j in range(RING):
                        load(i, j)
            for j in range(max(n_load, 0) % RING):
                load(n_load // RING, j)

        @block.tensor
        def _(pe):
            if feed is not None:
                feed.tensor(pe)
            for i in passes(pe, n_groups, peel, False):
                if isinstance(i, int) and i == 0 and feed is not None:
                    assert per == 1
                    for q in range(kt):
                        pe.wait_ge(fed.sem, fed(q + 1))
                        for j in range(4):
                            if q == 0:
                                pe.wait_ge(lo_r.sem, lo_r(j + 1))
                                pe.wait_ge(free.sem, free(j + 1))
                            mm = sums(pe, k.ps[:, j, 0:width], j, q, 0, q == 0, q == kt - 1)
                            if q == kt - 1:
                                mm.then_inc(used.sem, 1)
                    continue
                for j in range(4):
                    pe.wait_ge(free.sem, free(i * 4 + (j + 1)))
                    for c in range(per):
                        n = j * per + c
                        pe.wait_ge(lo_r.sem, lo_r(i * (4 * per) + (n + 1)))
                        for q in range(min(kt - 8 * c, 8)):
                            mm = sums(pe, k.ps[:, j, 0:width], n, q, c, c == 0 and q == 0, 8 * c + q == kt - 1)
                        mm.then_inc(used.sem, 1)
                    if norm and isinstance(i, int) and i == 0 and j == 0:
                        pe.matmul(k.ps[:, 4, :], k.ones[:, :], k.squares[:, :], start=True, stop=True
                                  ).then_inc(summed.sem, 1)

        def splitter(e, step):
            def run(i, j):
                for c in range(per):
                    n = j * per + c
                    if isinstance(i, int) and i * 4 * per + n >= n_split:
                        continue
                    step(i, n)
            return run

        @block.scalar
        def _(e):
            def step(i, n):
                s = (n + AHEAD) % RING
                e.wait_ge(slots[s].sem, (i * per + (c0 // RING + (n + AHEAD) // RING + 1)) * 16 + slots[s].base)
                e.wait_ge(used.sem, used(i * (4 * per) + (n + 1 + AHEAD - RING)))
                e.activation(k.w.hi[:, s, :], k.raw[:, s, :], ACT.Copy).then_inc(hi_r.sem, 1)
            run = splitter(e, step)
            if feed is not None:
                run(0, 0)
                run(0, 1)
                feed.scalar(e)
            if norm:
                run(0, 0)
                run(0, 1)
                e.wait_ge(summed.sem, summed(1))
                e.activation(k.root[:, :], k.ps[:, 4, :], ACT.Sqrt, scale=1.0 / D, bias=k.bias[1e-6]).then_inc(root.sem, 1)
            for i in (range(n_groups) if unroll else passes(e, n_groups, peel, ending)):
                for j in range(4):
                    if not (peel and isinstance(i, int) and i == 0 and j < 2):
                        run(i, j)
                    if act is not None:
                        act(e, i, j)

        @block.gpsimd
        def _(e):
            def step(i, n):
                s = (n + AHEAD) % RING
                e.wait_ge(hi_r.sem, hi_r(i * (4 * per) + (n + 1 + AHEAD)))
                e.tensor_tensor(k.w.lo[:, s, :], k.raw[:, s, :], as_float(k.w.hi[:, s, :]), ALU.subtract
                                ).then_inc(lo_r.sem, 1)
            run = splitter(e, step)
            if feed is not None:
                run(0, 0)
                run(0, 1)
                feed.gpsimd(e)
            for i in (range(n_groups) if unroll else passes(e, n_groups, feed is not None, ending)):
                for j in range(4):
                    if not (feed is not None and isinstance(i, int) and i == 0 and j < 2):
                        run(i, j)
                    if pool is not None:
                        pool(e, i, j)

        @block.vector
        def _(e):
            if feed is not None:
                feed.vector(e)
            if norm:
                e.wait_ge(root.sem, root(1))
                e.reciprocal(k.root[:, :], k.root[:, :]).then_inc(inverse.sem, 1)
                e.wait_ge(inverse.sem, inverse(1))
            if vector is not None:
                for i in (range(n_groups) if unroll else passes(e, n_groups, False, False)):
                    for j in range(4):
                        vector(e, i, j)
    k.chunk += N
    for s in (used, hi_r, lo_r):
        s.base += N
    free.base += m_tiles
    if norm:
        for s in (summed, root, inverse):
            s.base += 1
    if feed is not None:
        feed.done()
        fed.base += kt


def dyn(t, m):
    if isinstance(m, int):
        return t[:, m, :]
    return t[:, bass.ds(m, 1), :].rearrange("p o n -> p (o n)")


def copy_out(k, out, scale=1.0, width=T):
    used, free = k.sig("chunk_used", "bank_free")

    def act(e, i, j):
        e.wait_ge(used.sem, used(i * 4 + (j + 1)))
        e.activation(dyn(out, i * 4 + j)[:, 0:width], k.ps[:, j, 0:width], ACT.Copy, scale=scale).then_inc(free.sem, 1)
    return act


def residual(k, kt, src, per=1, bias=None, squares=True, gain=None, feed=None, early=None):
    used, free, sq, ac = k.sig("chunk_used", "bank_free", "squared", "squares_added")
    gained, hi_r, lo_r = k.sig("gained", "ahead_hi", "ahead_lo")
    with ExitStack() as st:
        sqt = st.enter_context(k.tile("sqr", [P, 2, T], F32))
        xg = st.enter_context(k.tile("x_gained", [P, 2, T], F32)) if gain else None

        def rest(e, m):
            e.wait_ge(hi_r.sem, hi_r(m + 1))
            e.tensor_tensor(k.ahead.lo[:, m, :], xg[:, m % 2, :], as_float(k.ahead.hi[:, m, :]), ALU.subtract
                            ).then_inc(lo_r.sem, 1)

        def vector(e, i, j):
            m = 4 * i + j
            e.wait_ge(used.sem, used((m + 1) * per))
            if bias is None:
                ins = e.tensor_tensor(k.x[:, m, :], k.x[:, m, :], k.ps[:, j, :], ALU.add)
            else:
                ins = e.scalar_tensor_tensor(k.x[:, m, :], k.x[:, m, :], k.vec(bias, m), k.ps[:, j, :], ALU.add, ALU.add)
            ins.then_inc(free.sem, 1)
            if gain is None:
                return
            e.wait_ge(free.sem, free(m + 1 + RING))
            if m >= 2:
                e.wait_ge(lo_r.sem, lo_r(m - 1))
            e.tensor_scalar(xg[:, m % 2, :], k.x[:, m, :], k.vec(gain, m), None, ALU.mult).then_inc(gained.sem, 1)
            if m:
                rest(e, m - 1)
            if m == KD - 1:
                rest(e, m)

        def act(e, i, j):
            m = 4 * i + j
            if m == 0 and early is not None:
                early(e)
            e.wait_ge(free.sem, free(m + 1 + RING))
            if m >= 2:
                e.wait_ge(ac.sem, ac(m - 1))
            e.activation(sqt[:, m % 2, :], k.x[:, m, :], ACT.Square).then_inc(sq.sem, 1)
            if gain is not None:
                e.wait_ge(gained.sem, gained(m + 1))
                e.activation(k.ahead.hi[:, m, :], xg[:, m % 2, :], ACT.Copy).then_inc(hi_r.sem, 1)

        def pool(e, i, j):
            m = 4 * i + j
            e.wait_ge(sq.sem, sq(m + 1))
            if m == 0:
                e.tensor_copy(k.squares[:, :], sqt[:, 0, :]).then_inc(ac.sem, 1)
            else:
                e.wait_ge(ac.sem, ac(m))
                e.tensor_tensor(k.squares[:, :], k.squares[:, :], sqt[:, m % 2, :], ALU.add).then_inc(ac.sem, 1)
        linear(k, KD, kt, src, vector=vector, act=act if squares else None, pool=pool if squares else None, unroll=True,
               feed=feed)
    if squares:
        sq.base += KD
        ac.base += KD
    if gain is not None:
        for s in (gained, hi_r, lo_r):
            s.base += KD


class Norm:

    def __init__(self, k, gain, dst, whole):
        self.k, self.gain, self.dst, self.whole = k, gain, dst, whole

    def tensor(self, pe):
        k = self.k
        pe.matmul(k.ps[:, 4, :], k.ones[:, :], k.squares[:, :], start=True, stop=True).then_inc(k.sig("summed").sem, 1)

    def scalar(self, act):
        k = self.k
        summed, root, whole_r, hi = k.sig("summed", "root", "normed", "fed_hi")
        act.wait_ge(summed.sem, summed(1))
        act.activation(k.root[:, :], k.ps[:, 4, :], ACT.Sqrt, scale=1.0 / D, bias=k.bias[1e-6]).then_inc(root.sem, 1)
        for m in range(KD):
            act.wait_ge(whole_r.sem, whole_r(m + 1))
            act.activation(self.dst.hi[:, m, :], self.whole[:, m, :], ACT.Copy).then_inc(hi.sem, 1)

    def vector(self, v):
        k = self.k
        root, inverse, whole_r, hi, fed = k.sig("root", "inverse", "normed", "fed_hi", "fed")
        v.wait_ge(root.sem, root(1))
        v.reciprocal(k.root[:, :], k.root[:, :]).then_inc(inverse.sem, 1)
        v.wait_ge(inverse.sem, inverse(1))

        def rest(m):
            v.wait_ge(hi.sem, hi(m + 1))
            v.tensor_tensor(self.dst.lo[:, m, :], self.whole[:, m, :], as_float(self.dst.hi[:, m, :]), ALU.subtract
                            ).then_inc(fed.sem, 1)
        for m in range(KD):
            v.scalar_tensor_tensor(self.whole[:, m, :], k.x[:, m, :], k.vec(self.gain, m), k.root[:, :],
                                   ALU.mult, ALU.mult).then_inc(whole_r.sem, 1)
            if m:
                rest(m - 1)
        rest(KD - 1)

    def gpsimd(self, g):
        pass

    def done(self):
        for n, c in (("summed", 1), ("root", 1), ("inverse", 1), ("normed", KD), ("fed_hi", KD)):
            self.k.sig(n).base += c


class Parts:

    def __init__(self, k, whole, dst, n):
        self.k, self.whole, self.dst, self.n = k, whole, dst, n

    def tensor(self, pe):
        pass

    def scalar(self, act):
        hi = self.k.sig("fed_hi")
        for m in range(self.n):
            act.activation(self.dst.hi[:, m, :], self.whole[:, m, :], ACT.Copy).then_inc(hi.sem, 1)

    def vector(self, v):
        hi, fed = self.k.sig("fed_hi", "fed")
        for m in range(self.n):
            v.wait_ge(hi.sem, hi(m + 1))
            v.tensor_tensor(self.dst.lo[:, m, :], self.whole[:, m, :], as_float(self.dst.hi[:, m, :]), ALU.subtract
                            ).then_inc(fed.sem, 1)

    def gpsimd(self, g):
        pass

    def done(self):
        self.k.sig("fed_hi").base += self.n


class Mix:

    def __init__(self, k, h, xx, xm, dst, i):
        self.k, self.h, self.xx, self.xm, self.dst, self.i = k, h, xx, xm, dst, i

    def tensor(self, pe):
        pass

    def scalar(self, act):
        whole_r, hi = self.k.sig("normed", "fed_hi")
        for m in range(KD):
            act.wait_ge(whole_r.sem, whole_r(m + 1))
            act.activation(self.dst.hi[:, m, :], self.xm[:, m % 4, :], ACT.Copy).then_inc(hi.sem, 1)

    def vector(self, v):
        k = self.k
        whole_r, hi, fed = k.sig("normed", "fed_hi", "fed")

        def rest(m):
            v.wait_ge(hi.sem, hi(m + 1))
            v.tensor_tensor(self.dst.lo[:, m, :], self.xm[:, m % 4, :], as_float(self.dst.hi[:, m, :]), ALU.subtract
                            ).then_inc(fed.sem, 1)
        for m in range(KD):
            if m >= 4:
                v.wait_ge(fed.sem, fed(m - 3))
            v.scalar_tensor_tensor(self.xm[:, m % 4, :], self.xx[:, m, :], k.vec("mu", 8 * self.i + m), self.h[:, m, :],
                                   ALU.mult, ALU.add).then_inc(whole_r.sem, 1)
            if m:
                rest(m - 1)
        rest(KD - 1)

    def gpsimd(self, g):
        pass

    def done(self):
        for n in ("normed", "fed_hi"):
            self.k.sig(n).base += KD



def gates_of(k, h, gates_w, gates, valid):
    wgl, gs, gt, gv = k.sig("gate_w_loaded", "gate_sums", "gates_made", "gates_masked")
    with k.nc.Block() as block:
        @block.tensor
        def _(pe):
            pe.wait_ge(wgl.sem, wgl(16))
            for b in range(NB):
                for m in range(KD):
                    mm = pe.matmul(k.ps[:, 4, b * 16:b * 16 + 12], h[:, m, b * P:(b + 1) * P], gates_w[:, m, :],
                                   start=(m == 0), stop=(m == KD - 1))
            mm.then_inc(gs.sem, 1)

        @block.scalar
        def _(act):
            act.wait_ge(gs.sem, gs(1))
            act.activation(gates[:, :, :], k.ps[:, 4, 0:64].rearrange("p (b g) -> p b g", b=NB)[:, :, 0:12],
                           ACT.Sigmoid).then_inc(gt.sem, 1)

        @block.vector
        def _(v):
            v.wait_ge(gt.sem, gt(1))
            v.tensor_scalar(gates[:, 0, 0:12:3], gates[:, 0, 0:12:3], valid, None, ALU.mult).then_inc(gv.sem, 1)
    wgl.base += 16
    gs.base += 1
    gt.base += 1
    gv.base += 1


def prepare_mixers(k, a, pr, vt, far, kc, vc):
    tiles = [(T_Q, 0), (T_Q + 1, 0)] + [(T_DQ + i, 4) for i in range(3)]
    tiles += [(T_KSEL, 2), (T_KWIN, 3)] + [(T_DK + i, 5) for i in range(3)]
    n, rows = len(tiles), 2 * len(tiles)
    tr, te, sq_r, ss_r, rt_r, inv_r, sp_r, nr, qs = k.sig(
        "transposed", "transposed_out", "squared", "heads_summed", "root", "inverse", "spread", "normed", "q_scaled")
    ld, raw_r, hs, ge, ht, hc, out_r, c1, c2, c3, c4, c5 = k.sig(
        "cmp_loaded", "cmp_raw", "cmp_hidden", "cmp_gelu", "cmp_turned", "cmp_turned_out", "cmp_out", "cmp_sq", "cmp_ss",
        "cmp_rt", "cmp_inv", "cmp_done")
    at = lambda name: CST[name] - N_KEEP
    with k.tile("hn_sq", [P, 2, T], F32) as sq, k.tile("hn_rt", [P, 2, T], F32) as rt, \
         k.tile("cw1", [P, 32, 128], F32) as w1, k.tile("cw2", [P, 192], F32) as w2, \
         k.tile("cpe", [P, 32], F32) as pos, k.tile("craw", [P, 32, N_CMP], F32) as raw, \
         k.tile("chid", [P, 2, 128], F32) as hid, k.tile("chidt", [P, 2, 32], F32) as hid_t, \
         k.tile("ck", [P, 4, 32], F32) as tmp, k.nc.Block() as block:
        @block.sync
        def _(sp):
            sp.dma_start(pos[:, :], a["cmp_pe"]).then_inc(ld.sem, 16)
            sp.dma_start(w1[:, :, :], a["cmp_w1"]).then_inc(ld.sem, 16)
            sp.dma_start(w2[:, :], a["cmp_w2"]).then_inc(ld.sem, 16)

        @block.tensor
        def _(pe):
            def turn(i):
                if i >= 4:
                    pe.wait_ge(te.sem, te(i - 3))
                for b in range(NB):
                    mm = pe.transpose(k.ps[:, 4 + i % 4, b * P:(b + 1) * P], pr[:, V_TILES[i], b * P:(b + 1) * P],
                                      k.ident)
                mm.then_inc(tr.sem, 1)

            for t in range(n):
                if t < len(V_TILES):
                    turn(t)
                pe.wait_ge(sq_r.sem, sq_r(t + 1))
                c = at("pick") + rows - 2 - 2 * t
                pe.matmul(k.ps[0:rows, 0, :], far[:, c:c + rows], sq[:, t % 2, :], start=(t == 0), stop=(t == n - 1)
                          ).then_inc(ss_r.sem, 1)
            pe.wait_ge(raw_r.sem, raw_r(2))
            for c in range(2):
                o = 64 * c
                for j in range(32):
                    mm = pe.matmul(k.ps[0:N_CMP, 1 + c, 0:128], raw[o:o + 64, j, :], w1[o:o + 64, j, :],
                                   start=(j == 0), stop=(j == 31))
                mm.then_inc(hs.sem, 1)
            pe.wait_ge(inv_r.sem, inv_r(1))
            for t in range(n):
                if t < 4:
                    pe.wait_ge(te.sem, te(len(V_TILES)))
                else:
                    pe.wait_ge(nr.sem, nr(t - 3))
                c = at("spread") + t * P
                pe.matmul(k.ps[:, 4 + t % 4, :], far[0:rows, c:c + P], rt[0:rows, 1, :], start=True, stop=True
                          ).then_inc(sp_r.sem, 1)
                if t == 3:
                    pe.wait_ge(ge.sem, ge(2))
                    for c in range(2):
                        mm = pe.transpose(k.ps[:, 3, 64 * c:64 * c + N_CMP], hid[0:N_CMP, c, :], k.ident[0:N_CMP, 0:N_CMP])
                    mm.then_inc(ht.sem, 1)
                if t == 5:
                    pe.wait_ge(hc.sem, hc(1))
                    pe.matmul(k.ps[:, 1, 0:N_CMP], w2[:, 0:128], hid_t[:, 0, 0:N_CMP], start=True, stop=True
                              ).then_inc(out_r.sem, 1)
                    pe.matmul(k.ps[0:N_CMP, 2, 0:64], hid_t[:, 1, 0:N_CMP], w2[:, 128:192], start=True, stop=True
                              ).then_inc(out_r.sem, 1)
                if t == 7:
                    pe.wait_ge(c1.sem, c1(1))
                    pe.matmul(k.ps[:, 3, 0:N_CMP], k.blockones, tmp[:, 1, 0:N_CMP], start=True, stop=True
                              ).then_inc(c2.sem, 1)

        @block.scalar
        def _(act):
            for t in range(n):
                if t >= 2:
                    act.wait_ge(ss_r.sem, ss_r(t - 1))
                act.activation(sq[:, t % 2, :], pr[:, tiles[t][0], :], ACT.Square).then_inc(sq_r.sem, 1)
                if t < len(V_TILES):
                    act.wait_ge(tr.sem, tr(t + 1))
                    act.activation(vt[:, :, t, :], k.ps[:, 4 + t % 4, :].rearrange("p (b d) -> p b d", b=NB), ACT.Copy
                                   ).then_inc(te.sem, 1)
            act.wait_ge(ss_r.sem, ss_r(n))
            scale, bias = (far[0:rows, at(m):at(m) + 1] for m in ("pick_scale", "pick_bias"))
            act.activation(rt[0:rows, 0, :], k.ps[0:rows, 0, :], ACT.Sqrt, scale=scale, bias=bias).then_inc(rt_r.sem, 1)
            for c in range(2):
                act.wait_ge(hs.sem, hs(c + 1))
                act.activation(hid[0:N_CMP, c, :], k.ps[0:N_CMP, 1 + c, 0:128], ACT.Gelu_apprx_tanh).then_inc(ge.sem, 1)
            act.wait_ge(ht.sem, ht(1))
            act.activation(hid_t[:, :, 0:N_CMP], k.ps[:, 3, 0:128].rearrange("p (c n) -> p c n", c=2)[:, :, 0:N_CMP],
                           ACT.Copy).then_inc(hc.sem, 1)
            act.wait_ge(out_r.sem, out_r(1))
            act.activation(tmp[:, 1, 0:N_CMP], k.ps[:, 1, 0:N_CMP], ACT.Square).then_inc(c1.sem, 1)
            act.wait_ge(c2.sem, c2(1))
            act.activation(tmp[:, 2, 0:N_CMP], k.ps[:, 3, 0:N_CMP], ACT.Sqrt, scale=1.0 / HD, bias=k.bias[1e-6]
                           ).then_inc(c3.sem, 1)

        @block.vector
        def _(v):
            v.wait_ge(ld.sem, ld(48))
            kv = pr[:, T_CMP, :].rearrange("p (n j) -> p j n", j=16)
            for half in range(2):
                v.tensor_tensor(raw[:, 16 * half:16 * half + 16, :], kv[:, :, half:half + N_CMP],
                                pos[:, 16 * half:16 * half + 16].unsqueeze(2).to_broadcast([P, 16, N_CMP]),
                                ALU.add).then_inc(raw_r.sem, 1)
            v.wait_ge(rt_r.sem, rt_r(1))
            v.reciprocal(rt[0:rows, 1, :], rt[0:rows, 0, :]).then_inc(inv_r.sem, 1)
            for t in range(n):
                v.wait_ge(sp_r.sem, sp_r(t + 1))
                v.scalar_tensor_tensor(pr[:, tiles[t][0], :], pr[:, tiles[t][0], :], k.vec("gains", tiles[t][1]),
                                       k.ps[:, 4 + t % 4, :], ALU.mult, ALU.mult).then_inc(nr.sem, 1)
                if t == 7:
                    v.wait_ge(c1.sem, c1(1))
                    v.wait_ge(out_r.sem, out_r(2))
                    v.tensor_copy(tmp[:, 0, 0:N_CMP], k.ps[:, 1, 0:N_CMP]).then_inc(c5.sem, 1)
                    v.tensor_copy(vc[0:N_CMP, :], k.ps[0:N_CMP, 2, 0:64]).then_inc(c5.sem, 1)
            v.wait_ge(c3.sem, c3(1))
            v.reciprocal(tmp[:, 3, 0:N_CMP], tmp[:, 2, 0:N_CMP]).then_inc(c4.sem, 1)
            v.wait_ge(c4.sem, c4(1))
            v.scalar_tensor_tensor(kc[:, 0:N_CMP], tmp[:, 0, 0:N_CMP], k.vec("gains", 1), tmp[:, 3, 0:N_CMP],
                                   ALU.mult, ALU.mult).then_inc(c5.sem, 1)

        @block.gpsimd
        def _(g):
            for i in range(3):
                g.tensor_scalar(pr[:, T_SQ + i, :], pr[:, T_SQ + i, :], 0.125, None, ALU.mult).then_inc(qs.sem, 1)
    for s, c in ((tr, len(V_TILES)), (te, len(V_TILES)), (sq_r, n), (ss_r, n), (rt_r, 1), (inv_r, 1), (sp_r, n), (nr, n),
                 (qs, 3), (ld, 48), (raw_r, 2), (hs, 2), (ge, 2), (ht, 1), (hc, 1), (out_r, 2), (c1, 1), (c2, 1), (c3, 1),
                 (c4, 1), (c5, 3)):
        s.base += c


def softmax_mixers(k, pr, vt, gates, dist, dist_cmp, kc, vc, cat):
    nc = k.nc
    units = []
    for h in range(4):
        for b, key in ((0, None), (1, T_KSEL), (2, T_KWIN)):
            units.append((T_Q + h // 2, h % 2, key, (0, 64 * (b == 2)), 0, SLOPES[6 + h]))
    for j in range(2):
        for g in range(3):
            units.append((T_DQ + g, j, T_DK + g, (1 + g, 64 * j), 1 + g, SLOPES[2 * g + j]))
    U = len(units)
    sc, bi, mx, ex, wt, scaled, scaled_v, tr, pt_r, pv, oe, sm, mg = k.sig(
        "scores", "biased", "maxima", "exps", "weights", "scaled_by_pool", "scaled_by_vector", "transposed", "transposed_out", "pv_done",
        "mixer_out", "small_steps", "merged_exps")
    with k.tile("sm_p", [P, U - 4, T - P], F32) as p_even, k.tile("sm_p2", [P, 2, T], F32) as p_odd, k.tile("sm_pc", [P, 2, 4, 32], F32) as p_cmp, \
          k.tile("sm_pt", [P, 3, T], F32) as pt, \
         k.tile("sm_st", [P, 2, 6, 32], F32) as st, nc.Block() as block:
        NM, L, W, E, NMM, EL = range(6)

        def stats(qb, row):
            return st[:, qb % 2, row, :]

        def probs(qb, u):
            if units[u][2] is None:
                return p_cmp[:, qb % 2, u // 3, 0:N_CMP]
            n = u - 1 - u // 3 if u < 12 else u - 4
            if qb % 2 == 0:
                return p_even[:, n, 0:width(u, qb)]
            return pr[:, T_DV + n, 0:width(u, qb)] if T_DV + n < N_PROJ else                 p_odd[:, T_DV + n - N_PROJ, 0:width(u, qb)]

        def width(u, qb):
            return N_CMP if units[u][2] is None else (qb + 1) * P

        @block.tensor
        def _(pe):
            def scores(qb, u):
                g = qb * U + u
                qt, half, key = units[u][:3]
                o, w_ = 64 * half, width(u, qb)
                if g >= 4:
                    pe.wait_ge(bi.sem, bi(g - 3))
                keys = kc[o:o + 64, 0:w_] if key is None else pr[o:o + 64, key, 0:w_]
                pe.matmul(k.ps[:, g % 4, 0:w_], pr[o:o + 64, qt, qb * P:(qb + 1) * P], keys,
                          start=True, stop=True).then_inc(sc.sem, 1)

            def turn(qb, u):
                g = qb * U + u
                w_ = width(u, qb)
                if u % 3 == 2:
                    pe.wait_ge(scaled_v.sem, scaled_v(qb * (U // 3) + u // 3 + 1))
                else:
                    pe.wait_ge(scaled.sem, scaled(qb * (U - U // 3) + u - u // 3 + 1))
                if g >= 2:
                    pe.wait_ge(pt_r.sem, pt_r(g - 1))
                for b in range(-(-w_ // P)):
                    r = min(P, w_ - b * P)
                    mm = pe.transpose(k.ps[0:r, 4 + g % 2, b * P:(b + 1) * P], probs(qb, u)[:, b * P:b * P + r], k.ident)
                mm.then_inc(tr.sem, 1)

            def values(qb, u):
                g = qb * U + u
                _, half, key, (vtile, vcol), _, _ = units[u]
                w_, o = width(u, qb), 64 * half
                out = 3 * qb + u // 6
                if u % 3 == 0 and out >= 2:
                    pe.wait_ge(oe.sem, oe(out - 1))
                pe.wait_ge(pt_r.sem, pt_r(g + 1))
                nblk = -(-w_ // P)
                for b in range(nblk):
                    r = min(P, w_ - b * P)
                    val = vc[0:r, :] if key is None else vt[:, b, vtile, vcol:vcol + 64]
                    mm = pe.matmul(k.ps[o:o + 64, 6 + out % 2, 0:P], val, pt[0:r, g % 3, b * P:(b + 1) * P],
                                   start=(u % 3 == 0 and b == 0), stop=(u % 3 == 2 and b == nblk - 1))
                mm.then_inc(pv.sem, 1)

            for u in range(U):
                scores(0, u)
            for qb in range(NB):
                if qb + 1 < NB:
                    scores(qb + 1, 0)
                    scores(qb + 1, 1)
                turn(qb, 0)
                for u in range(U):
                    if qb + 1 < NB and 2 * u + 3 < U:
                        scores(qb + 1, 2 * u + 2)
                        scores(qb + 1, 2 * u + 3)
                    if u + 1 < U:
                        turn(qb, u + 1)
                    values(qb, u)

        @block.vector
        def _(v):
            def bias(qb, u):
                g = qb * U + u
                w_ = width(u, qb)
                table, slope = units[u][4], units[u][5]
                d = dist_cmp[:, qb, 0:w_] if units[u][2] is None else dist[:, table, T - w_:T]
                v.wait_ge(sc.sem, sc(g + 1))
                if qb >= 2:
                    v.wait_ge(tr.sem, tr(g - 2 * U + 1))
                v.scalar_tensor_tensor(probs(qb, u), d, slope, k.ps[:, g % 4, 0:w_], ALU.mult, ALU.add
                                       ).then_inc(bi.sem, 1)

            def maximum(qb, u):
                g = qb * U + u
                v.wait_ge(bi.sem, bi(g + 1))
                v.tensor_reduce(stats(qb, NM)[:, u:u + 1], probs(qb, u), AX.X, ALU.max, negate=True
                                ).then_inc(mx.sem, 1)

            def weigh(n):
                nm, l, w, e, nmm, el = (stats(n, r) for r in range(6))
                v.wait_ge(mx.sem, mx((n + 1) * U))
                v.tensor_reduce(nmm[:, 0:2], nm[:, 12:18].rearrange("p (a b) -> p a b", a=2), AX.X, ALU.min
                                ).then_inc(sm.sem, 1)
                v.wait_ge(ex.sem, ex((n + 1) * U))
                v.reciprocal(el[:, 0:12], l[:, 0:12]).then_inc(sm.sem, 1)
                v.wait_ge(mg.sem, mg(2 * (n + 1)))
                v.tensor_tensor(el[:, 12:18], e[:, 0:6], l[:, 12:18], ALU.mult).then_inc(sm.sem, 1)
                v.wait_ge(sm.sem, sm(5 * n + 3))
                v.tensor_tensor(w[:, 0:12], el[:, 0:12], gates[:, n, :], ALU.mult).then_inc(wt.sem, 1)
                v.tensor_reduce(nmm[:, 2:4], el[:, 12:18].rearrange("p (a b) -> p a b", a=2), AX.X, ALU.add
                                ).then_inc(sm.sem, 1)
                v.wait_ge(sm.sem, sm(5 * n + 4))
                v.reciprocal(nmm[:, 4:6], nmm[:, 2:4]).then_inc(sm.sem, 1)
                v.wait_ge(sm.sem, sm(5 * n + 5))
                v.tensor_tensor(w[:, 12:18].rearrange("p (a b) -> p a b", a=2),
                                e[:, 0:6].rearrange("p (a b) -> p a b", a=2),
                                nmm[:, 4:6].unsqueeze(2).to_broadcast([P, 2, 3]), ALU.mult).then_inc(wt.sem, 1)

                v.wait_ge(wt.sem, wt(2 * (n + 1)))
                for u in range(2, U, 3):
                    v.tensor_scalar(probs(n, u), probs(n, u), w[:, u:u + 1], None, ALU.mult).then_inc(scaled_v.sem, 1)

            def sums(qb, i):
                v.wait_ge(pv.sem, pv(qb * U + 6 * i + 6))
                v.tensor_copy(cat[:, i, qb * P:(qb + 1) * P], k.ps[:, 6 + (3 * qb + i) % 2, 0:P]).then_inc(oe.sem, 1)

            bias(0, 0)
            for u in range(U):
                if u + 1 < U:
                    bias(0, u + 1)
                maximum(0, u)
            weigh(0)
            for qb in range(NB):
                if qb + 1 < NB:
                    if qb >= 1:
                        v.wait_ge(scaled.sem, scaled(qb * (U - U // 3)))
                        v.wait_ge(scaled_v.sem, scaled_v(qb * (U // 3)))
                    bias(qb + 1, 0)
                for u in range(U):
                    if qb + 1 < NB:
                        for t in (2 * u, 2 * u + 1):
                            if t + 1 < U:
                                bias(qb + 1, t + 1)
                            if t < U:
                                maximum(qb + 1, t)
                    if u in (8, 14):
                        sums(qb, u // 6 - 1)
                    if u == 11 and qb + 1 < NB:
                        weigh(qb + 1)
                sums(qb, 2)

        @block.scalar
        def _(act):
            def exponentials(qb, u):
                g = qb * U + u
                act.wait_ge(mx.sem, mx(g + 1))
                act.activation(probs(qb, u), probs(qb, u), ACT.Exp,
                               bias=stats(qb, NM)[:, u:u + 1], accum_out=stats(qb, L)[:, u:u + 1]).then_inc(ex.sem, 1)

            def merged(qb):
                act.wait_ge(sm.sem, sm(5 * qb + 1))
                for j in range(2):
                    act.activation(stats(qb, E)[:, 3 * j:3 * j + 3], stats(qb, NM)[:, 12 + 3 * j:15 + 3 * j], ACT.Exp,
                                   scale=-1.0, bias=stats(qb, NMM)[:, j:j + 1]).then_inc(mg.sem, 1)

            for u in range(U):
                exponentials(0, u)
            merged(0)
            for qb in range(NB):
                for u in range(U):
                    g = qb * U + u
                    w_ = width(u, qb)
                    act.wait_ge(tr.sem, tr(g + 1))
                    if g >= 3:
                        act.wait_ge(pv.sem, pv(g - 2))
                    r, c = (w_, P) if units[u][2] is None else (P, w_)
                    act.activation(pt[0:r, g % 3, 0:c], k.ps[0:r, 4 + g % 2, 0:c], ACT.Copy).then_inc(pt_r.sem, 1)
                    if qb + 1 < NB:
                        for t in (2 * u - 2, 2 * u - 1):
                            if 0 <= t < U:
                                exponentials(qb + 1, t)
                        if 2 * u - 1 == U + 1:
                            merged(qb + 1)

        @block.gpsimd
        def _(gp):
            for qb in range(NB):
                gp.wait_ge(wt.sem, wt(2 * (qb + 1)))
                for u in range(U):
                    if u % 3 == 2:
                        continue
                    t = probs(qb, u)
                    gp.tensor_scalar(t, t, stats(qb, W)[:, u:u + 1], None, ALU.mult).then_inc(scaled.sem, 1)
    for s in (sc, bi, mx, ex, tr, pt_r, pv):
        s.base += NB * U
    wt.base += 2 * NB
    oe.base += 3 * NB
    sm.base += 5 * NB
    scaled.base += NB * (U - U // 3)
    scaled_v.base += NB * (U // 3)
    mg.base += 2 * NB


def stick_breaking(k, pr, vt, cat):
    nc = k.nc
    H = 6
    units = [(h, kb) for h in range(H) for kb in (3, 2, 1, 0)]
    z_r, chain, ln_r, sp_raw, sp_r, l_r, at_raw, at_r, o_r, oe = k.sig(
        "z_ready", "softplus_steps", "softplus_log", "softplus_raw", "softplus_ready", "log_weights", "weights_raw",
        "weights_ready", "sb_out", "sb_out_taken")
    n = len(units)
    with k.tile("sb_sp", [P, 8, T], F32) as sp_t, k.tile("sb_at", [P, 8, T], F32) as at, \
         k.tile("sb_t", [P, 4, T], F32) as t1, nc.Block() as block:
        def order(h):
            return [4 * h + i for i in ((0, 1, 2, 3) if h == 0 else (1, 2, 3, 0))]

        def place(u):
            return 4 * (u // 4) + order(u // 4).index(u)

        @block.tensor
        def _(pe):
            def z(u):
                h, kb = units[u]
                o, w = 64 * (h % 2), T - kb * P
                if u >= 8:
                    pe.wait_ge(at_raw.sem, at_raw(u - 7))
                    if u % 4 == 0:
                        pe.wait_ge(oe.sem, oe(h - 1))
                pe.matmul(k.ps[:, u % 8, 0:w], pr[o:o + 64, T_SK + h // 2, kb * P:(kb + 1) * P],
                          pr[o:o + 64, T_SQ + h // 2, kb * P:T], start=True, stop=False,
                          skip_group_check=True).then_inc(z_r.sem, 1)

            def accumulate(u):
                h, kb = units[u]
                pe.wait_ge(sp_r.sem, sp_r(u + 1))
                mm = pe.matmul(k.ps[:, u % 8, 0:T - kb * P], k.negtri, sp_t[:, u % 8, 0:T - kb * P],
                               start=False, stop=(kb == 3), skip_group_check=True)
                for later in range(kb + 1, 4):
                    mm = pe.matmul(k.ps[:, u % 8, (later - kb) * P:T - kb * P], k.negones[:, :],
                                   sp_t[:, (4 * h + 3 - later) % 8, 0:T - later * P], start=False,
                                   stop=(later == 3), skip_group_check=True)
                mm.then_inc(l_r.sem, 1)

            def values(h):
                o = 64 * (h % 2)
                pe.wait_ge(at_r.sem, at_r(4 * h + 4))
                for kb in range(4):
                    mm = pe.matmul(k.ps[o:o + 64, 4 * (h % 2), kb * P:T], vt[:, kb, 4 + h // 2, o:o + 64],
                                   at[:, (4 * h + 3 - kb) % 8, 0:T - kb * P], start=(kb == 0), stop=(kb == 3),
                                   skip_group_check=True)
                mm.then_inc(o_r.sem, 1)

            for u in order(0) + order(1):
                z(u)
            for h in range(H):
                for i in range(4):
                    accumulate(4 * h + i)
                if h:
                    values(h - 1)
                if 1 <= h < H - 1:
                    for u in order(h + 1):
                        z(u)
            values(H - 1)

        @block.scalar
        def _(act):
            def exponentials(h):
                for u in order(h):
                    w = T - units[u][1] * P
                    act.wait_ge(z_r.sem, z_r(place(u) + 1))
                    if u >= 4:
                        act.wait_ge(sp_raw.sem, sp_raw(u - 3))
                    act.activation(t1[:, u % 4, 0:w], k.ps[:, u % 8, 0:w], ACT.Abs).then_inc(chain.sem, 1)
                for u in order(h):
                    w = T - units[u][1] * P
                    act.wait_ge(chain.sem, chain(4 * h + place(u) + 1))
                    act.activation(t1[:, u % 4, 0:w], t1[:, u % 4, 0:w], ACT.Exp, scale=-1.0).then_inc(chain.sem, 1)

            def logarithms(h):
                act.wait_ge(chain.sem, chain(8 * h + 8))
                for u in range(4 * h, 4 * h + 4):
                    w = T - units[u][1] * P
                    act.activation(t1[:, u % 4, 0:w], t1[:, u % 4, 0:w], ACT.Ln, bias=k.bias[1.0]).then_inc(ln_r.sem, 1)

            def weights(h):
                for u in range(4 * h, 4 * h + 4):
                    w = T - units[u][1] * P
                    act.wait_ge(l_r.sem, l_r(u + 1))
                    if h >= 2:
                        act.wait_ge(o_r.sem, o_r(h - 1))
                    act.activation(at[:, u % 8, 0:w], k.ps[:, u % 8, 0:w], ACT.Exp).then_inc(at_raw.sem, 1)

            exponentials(0)
            logarithms(0)
            for h in range(H):
                if h + 1 < H:
                    exponentials(h + 1)
                    logarithms(h + 1)
                weights(h)

        @block.vector
        def _(v):
            def softplus(h):
                for u in range(4 * h, 4 * h + 4):
                    w = T - units[u][1] * P
                    v.wait_ge(ln_r.sem, ln_r(u + 1))
                    if h >= 2:
                        v.wait_ge(l_r.sem, l_r(4 * (h - 1)))
                    v.scalar_tensor_tensor(sp_t[:, u % 8, 0:w], k.ps[:, u % 8, 0:w], 0.0, t1[:, u % 4, 0:w],
                                           ALU.max, ALU.add).then_inc(sp_raw.sem, 1)

            softplus(0)
            for h in range(H):
                if h + 1 < H:
                    softplus(h + 1)
                o = 64 * (h % 2)
                v.wait_ge(o_r.sem, o_r(h + 1))
                v.tensor_copy(cat[o:o + 64, 3 + h // 2, :], k.ps[o:o + 64, 4 * (h % 2), :]).then_inc(oe.sem, 1)

        @block.gpsimd
        def _(g):
            def strict(t):
                return g.affine_select(t, t, [[1, P]], ALU.is_ge, 0.0, base=-1, channel_multiplier=-1)

            for u in range(-4, n):
                if u + 4 < n:
                    g.wait_ge(sp_raw.sem, sp_raw(u + 5))
                    strict(sp_t[:, (u + 4) % 8, 0:P]).then_inc(sp_r.sem, 1)
                if u < 0:
                    continue
                g.wait_ge(at_raw.sem, at_raw(u + 1))
                strict(at[:, u % 8, 0:P]).then_inc(at_r.sem, 1)
    for s in (z_r, ln_r, sp_raw, sp_r, l_r, at_raw, at_r):
        s.base += n
    chain.base += 2 * n
    o_r.base += H
    oe.base += H


def first_block(k, a):
    nc = k.nc
    with ExitStack() as outer:
        tile = lambda st, name, *shape: st.enter_context(k.tile(name, [P, *shape], F32))
        cat = tile(outer, "cat", 6, T)
        with ExitStack() as mixers:
            pr = tile(mixers, "proj", N_PROJ, T)
            far = tile(mixers, "dist", N_CONST - N_KEEP)
            gates = tile(mixers, "gates", NB, 12)
            kc = tile(mixers, "kc", 32)
            vc = tile(mixers, "vc", 64)
            dist = far[:, 0:2048].rearrange("p (a t) -> p a t", a=4)
            dist_cmp = far[:, 2048:2048 + 128].rearrange("p (a t) -> p a t", a=4)
            with ExitStack() as st:
                h = tile(st, "h", KD, T)
                gw = tile(st, "gates_w", KD, 12)
                with ExitStack() as st2:
                    hs = Split(st2, k, "h", KD, T)
                    far_loaded = k.sig("distances_loaded")
                    out = copy_out(k, pr)

                    def act(e, i, j):
                        if isinstance(i, int) and i == 0 and j == 0:
                            e.dma_start(far[:, :], a["consts"][:, N_KEEP:N_CONST]).then_inc(far_loaded.sem, 16)
                            e.dma_start(gw[:, :, :], a["w_gate"]).then_inc(k.sig("gate_w_loaded").sem, 16)
                        out(e, i, j)
                    linear(k, N_PROJ, KD, hs, act=act, feed=Norm(k, "norm_mix", hs, h))
                gates_of_valid = far[:, 2176:2177]
                with nc.Block() as block:
                    @block.vector
                    def _(v):
                        v.wait_ge(far_loaded.sem, far_loaded(16))
                gates_of(k, h, gw, gates, gates_of_valid)
            vt = tile(mixers, "values", NB, 7, P)
            prepare_mixers(k, a, pr, vt, far, kc, vc)
            stick_breaking(k, pr, vt, cat)
            softmax_mixers(k, pr, vt, gates, dist, dist_cmp, kc, vc, cat)
        k.ahead = Split(outer, k, "ahead", KD, T)
        hid = Split(outer, k, "hidden", F1 // P // 2, T)
        residual(k, 6, hid, gain="norm_mlp", feed=Parts(k, cat, hid, 6))
        mlp(k, hid)


def mlp(k, hid):
    used, free, whole_r, hi, lo = k.sig("chunk_used", "bank_free", "hidden_whole", "hidden_hi", "hidden_lo")
    half = F1 // P // 2
    with ExitStack() as st:
        rl = st.enter_context(k.tile("relu", [P, 2, T], F32))
        sq = st.enter_context(k.tile("relu2", [P, 2, T], F32))

        def act(e, i, j):
            e.wait_ge(free.sem, free(i * 4 + (j + 1 + RING)))
            e.activation(dyn(hid.hi, i * 4 + j), rl[:, j % 2, :], ACT.Square).then_inc(hi.sem, 1)

        def vector(e, i, j):
            e.wait_ge(used.sem, used(i * 4 + (j + 1)))
            e.wait_ge(hi.sem, hi(i * 4 + (j - 1 + RING)))
            e.wait_ge(lo.sem, lo(i * 4 + (j - 1 + RING)))
            e.scalar_tensor_tensor(rl[:, j % 2, :], k.ps[:, j, :], 0.0, k.root[:, :], ALU.max, ALU.mult
                                   ).then_inc(free.sem, 1)
            e.wait_ge(free.sem, free(i * 4 + (j + 1 + RING)))
            e.tensor_tensor(sq[:, j % 2, :], rl[:, j % 2, :], rl[:, j % 2, :], ALU.mult).then_inc(whole_r.sem, 1)
            e.wait_ge(whole_r.sem, whole_r(i * 4 + (j + 1)))
            e.wait_ge(hi.sem, hi(i * 4 + (j + 1 + RING)))
            e.tensor_tensor(dyn(hid.lo, i * 4 + j), sq[:, j % 2, :], as_float(dyn(hid.hi, i * 4 + j)), ALU.subtract
                            ).then_inc(lo.sem, 1)
        with k.nc.Block() as block:
            @block.vector
            def _(v):
                v.sem_inc(hi.sem, RING)
                v.sem_inc(lo.sem, RING)
        for n in range(2):
            linear(k, half, KD, k.ahead, act=act, vector=vector, norm=(n == 0))
            for s in (whole_r, hi, lo):
                s.base += half
            residual(k, half, hid, per=2, squares=(n == 1))
        for s in (hi, lo):
            s.base += RING



def time_mix_inputs(k, a, r, kk, vv, inner_w, inner_a, inner_g):
    nc = k.nc
    summed, root, inverse, normed, shifted, ld, mixed, sums, inner_r, xu = k.sig(
        "summed", "root", "inverse", "normed", "shifted", "lora_loaded", "mixed", "lora_sums", "lora_inner", "mix_used")
    with ExitStack() as st:
        tile = lambda name, *shape: st.enter_context(k.tile(name, [P, *shape], F32))
        h, xx, xm = tile("h", KD, T), tile("xx", KD, T), tile("xm", 4, T)
        with nc.Block() as block:
            @block.tensor
            def _(pe):
                pe.matmul(k.ps[:, 4, :], k.ones[:, :], k.squares[:, :], start=True, stop=True).then_inc(summed.sem, 1)

            @block.scalar
            def _(act):
                act.wait_ge(summed.sem, summed(1))
                act.activation(k.root[:, :], k.ps[:, 4, :], ACT.Sqrt, scale=1.0 / D, bias=k.bias[1e-6]).then_inc(root.sem, 1)

            @block.vector
            def _(v):
                v.wait_ge(root.sem, root(1))
                v.reciprocal(k.root[:, :], k.root[:, :]).then_inc(inverse.sem, 1)
                v.wait_ge(inverse.sem, inverse(1))
                for m in range(KD):
                    v.scalar_tensor_tensor(h[:, m, :], k.x[:, m, :], k.vec("mix0", m), k.root[:, :],
                                           ALU.mult, ALU.mult).then_inc(normed.sem, 1)
                for m in range(KD):
                    v.wait_ge(normed.sem, normed(m + 1))
                    v.tensor_tensor(xx[:, m, 1:T], h[:, m, 0:T - 1], h[:, m, 1:T], ALU.subtract).then_inc(shifted.sem, 1)
                v.tensor_scalar(xx[:, :, 0:1], h[:, :, 0:1], -1.0, None, ALU.mult).then_inc(shifted.sem, 1)
        for s, c in ((summed, 1), (root, 1), (inverse, 1), (normed, KD), (shifted, KD + 1)):
            s.base += c
        with ExitStack() as st2:
            xs = Split(st2, k, "xs", KD, T)
            for i, out in ((0, r), (2, kk), (3, vv)):
                linear(k, KD, KD, xs, act=copy_out(k, out), feed=Mix(k, h, xx, xm, xs, i))
        with k.tile("lora_a", [P, KD, 288], F32) as wa, nc.Block() as block:
            parts = [(1, 4, 0, 64), (4, 5, 64, 64), (5, 6, 128, P), (5, 7, 256, 32)]

            @block.sync
            def _(sp):
                sp.dma_start(wa[:, :, :], a["lora_a"]).then_inc(ld.sem, 16)

            @block.vector
            def _(v):
                for n, i in enumerate((1, 4, 5)):
                    for m in range(KD):
                        t = n * KD + m
                        if t >= 4:
                            v.wait_ge(xu.sem, xu(t - 3))
                        v.scalar_tensor_tensor(xm[:, t % 4, :], xx[:, m, :], k.vec("mu", 8 * i + m), h[:, m, :],
                                               ALU.mult, ALU.add).then_inc(mixed.sem, 1)

            @block.tensor
            def _(pe):
                pe.wait_ge(ld.sem, ld(16))
                for n, i in enumerate((1, 4, 5)):
                    for m in range(KD):
                        t = n * KD + m
                        pe.wait_ge(mixed.sem, mixed(t + 1))
                        for mu, bank, c, w in parts:
                            if mu == i:
                                mm = pe.matmul(k.ps[0:w, bank, :], wa[:, m, c:c + w], xm[:, t % 4, :], start=(m == 0),
                                               stop=(m == KD - 1))
                        mm.then_inc(xu.sem, 1)

            @block.scalar
            def _(act):
                act.wait_ge(xu.sem, xu(KD))
                act.activation(inner_w[0:64, :], k.ps[0:64, 4, :], ACT.Tanh).then_inc(inner_r.sem, 1)
                act.wait_ge(xu.sem, xu(2 * KD))
                act.activation(inner_a[0:64, :], k.ps[0:64, 5, :], ACT.Copy).then_inc(inner_r.sem, 1)
                act.wait_ge(xu.sem, xu(3 * KD))
                act.activation(inner_g[:, 0, :], k.ps[:, 6, :], ACT.Sigmoid).then_inc(inner_r.sem, 1)
                act.activation(inner_g[0:32, 1, :], k.ps[0:32, 7, :], ACT.Sigmoid).then_inc(inner_r.sem, 1)
        ld.base += 16
        mixed.base += 3 * KD
        xu.base += 3 * KD
        inner_r.base += 4


def low_rank_outputs(k, a, inner_w, inner_a, sg, aa):
    ld, s2, t2 = k.sig("lora_loaded", "lora_out", "lora_taken")
    with k.tile("lora_b", [P, 2, D], F32) as wb, k.nc.Block() as block:
        @block.sync
        def _(sp):
            sp.dma_start(wb[0:64, :, :], a["lora_b"][0:64, 0:2, :]).then_inc(ld.sem, 16)

        @block.tensor
        def _(pe):
            pe.wait_ge(ld.sem, ld(16))
            for n, src in enumerate((inner_w, inner_a)):
                for m in range(KD):
                    t = n * KD + m
                    if t >= 4:
                        pe.wait_ge(t2.sem, t2(t - 3))
                    pe.matmul(k.ps[:, 4 + t % 4, :], wb[0:64, n, m * P:(m + 1) * P], src[0:64, :], start=True, stop=True
                              ).then_inc(s2.sem, 1)

        @block.scalar
        def _(act):
            for n, (dst, bias) in enumerate(((sg, "w0"), (aa, "a0"))):
                for m in range(KD):
                    t = n * KD + m
                    act.wait_ge(s2.sem, s2(t + 1))
                    act.activation(dst[:, m, :], k.ps[:, 4 + t % 4, :], ACT.Sigmoid, bias=k.vec(bias, m)).then_inc(t2.sem, 1)
    ld.base += 16
    s2.base += 2 * KD
    t2.base += 2 * KD


class Pairs:

    C = NB
    MID = 64

    def __init__(self, k, stack, r, kk, vv, sg, aa):
        self.k, self.r, self.kk, self.vv, self.sg, self.aa = k, r, kk, vv, sg, aa
        sb = lambda name, *shape: stack.enter_context(k.tile(f"pair_{name}", [P, *shape], F32))
        self.kkn, self.kn, self.ba, self.t0, self.t1 = (sb(n, T) for n in ("kkn", "kn", "ba", "t0", "t1"))
        self.L, self.Em = sb("L", NB, P + 1), sb("Em", NB, P)
        self.AR, self.B, self.K = sb("AR", 2, NB, 2 * P), sb("B", NB, P), sb("K", NB, P)
        self.AT, self.BT, self.KT, self.VT = (sb(n, NB, P) for n in ("AT", "BT", "KT", "VT"))
        self.M, self.T, self.Tt, self.U, self.Mo = sb("M", 8, T), sb("T", 8, P), sb("Tt", 8, P), sb("U", 8, P), sb("Mo", 2, 8, P)
        self.X, self.H, self.G = sb("X", NB, P), sb("H", NB, P), sb("G", NB, P)
        self.S, self.Ss, self.Spc, self.SA = sb("S", P), sb("Ss", 2, P), sb("Spc", P), sb("SA", 2, P)
        self.sm = sb("sm", 2, 20)

    def bank(self, n):
        return self.k.ps[:, n, :].rearrange("p (u t) -> p u t", u=4)


    def vectors_vector(self, v, p, step):
        k, s = self.k, self.k.sig("vec_vector")
        ts, ta = self.k.sig("vec_tensor", "vec_scalar")
        L, sm = self.L, self.sm[:, p % 2, :]
        AR = self.AR[:, p % 2]
        R_, K_, V_, S_, A_ = (t[:, p, :] for t in (self.r, self.kk, self.vv, self.sg, self.aa))
        cut = lambda t: t.rearrange("p (c t) -> p c t", c=NB)
        if step == 0:
            v.tensor_scalar(self.kkn[:, :], K_, k.vec("k_k", p), None, ALU.mult).then_inc(s.sem, 1)
            v.tensor_scalar(self.t0[:, :], A_, -1.0, k.vec("k_a", p), ALU.add, ALU.mult).then_inc(s.sem, 1)
            for i in range(NB):
                v.tensor_tensor_scan(L[:, i, 1:P + 1], k.ones[:, :], S_[:, i * P:(i + 1) * P], 0.0, ALU.mult, ALU.add
                                     ).then_inc(s.sem, 1)
        if step == 1:
            v.wait_ge(s.sem, s(6))
            v.scalar_tensor_tensor(self.kn[:, :], self.t0[:, :], 1.0, K_, ALU.add, ALU.mult).then_inc(s.sem, 1)
            v.tensor_scalar(sm[:, 0:4], L[:, :, self.MID], DECAY, None, ALU.mult).then_inc(s.sem, 1)
            v.tensor_scalar(sm[:, 4:8], L[:, :, self.MID], -DECAY, None, ALU.mult).then_inc(s.sem, 1)
            v.wait_ge(s.sem, s(7))
            v.scalar_tensor_tensor(self.t0[:, :], R_, k.vec("r_k", p), self.kn[:, :], ALU.mult, ALU.mult).then_inc(s.sem, 1)
        if step == 2:
            v.wait_ge(ta.sem, ta(2))
            v.tensor_scalar(self.t1[:, :], self.t1[:, :], 1e-12, None, ALU.max).then_inc(s.sem, 1)
            v.wait_ge(s.sem, s(11))
            v.reciprocal(self.t1[:, :], self.t1[:, :]).then_inc(s.sem, 1)
        if step == 3:
            v.wait_ge(s.sem, s(12))
            v.tensor_tensor(self.kkn[:, :], self.kkn[:, :], self.t1[:, :], ALU.mult).then_inc(s.sem, 1)
            v.wait_ge(ts.sem, ts(2))
            v.wait_ge(s.sem, s(13))
            v.tensor_tensor(self.ba[:, :], self.kkn[:, :], A_, ALU.mult).then_inc(s.sem, 1)
            v.tensor_tensor(K_, V_, k.ps[:, 7, :], ALU.mult).then_inc(s.sem, 1)
        if step == 4:
            v.wait_ge(ta.sem, ta(12))
            v.scalar_tensor_tensor(AR[:, :, 0:P], cut(self.kkn[:, :]), -1.0, L[:, :, 0:P], ALU.mult, ALU.mult
                                   ).then_inc(s.sem, 1)
            v.tensor_tensor(AR[:, :, P:2 * P], cut(R_), L[:, :, 1:P + 1], ALU.mult).then_inc(s.sem, 1)
            v.wait_ge(s.sem, s(14))
            v.tensor_tensor(self.B[:, :, :], cut(self.ba[:, :]), self.Em[:, :, :], ALU.mult).then_inc(s.sem, 1)
            v.tensor_tensor(self.K[:, :, :], cut(self.kn[:, :]), self.Em[:, :, :], ALU.mult).then_inc(s.sem, 1)

    def vectors_scalar(self, act, p, step):
        k, s = self.k, self.k.sig("vec_scalar")
        ts, tv, z = self.k.sig("vec_tensor", "vec_vector", "zeroed")
        L, sm = self.L, self.sm[:, p % 2, :]
        if step == 0:
            act.wait_ge(tv.sem, tv(1))
            act.activation(self.t1[:, :], self.kkn[:, :], ACT.Square).then_inc(s.sem, 1)
        if step == 1:
            act.wait_ge(ts.sem, ts(1))
            act.activation(self.t1[:, :], k.ps[:, 6, :], ACT.Sqrt).then_inc(s.sem, 1)
        if step == 2:
            act.wait_ge(tv.sem, tv(9))
            act.activation(sm[:, 8:12], L[:, :, self.MID], ACT.Exp, scale=-DECAY).then_inc(s.sem, 1)
            act.activation(sm[:, 12:16], L[:, :, P], ACT.Exp, scale=-DECAY).then_inc(s.sem, 1)
            for i in range(NB):
                act.activation(self.Em[:, i, :], L[:, i, 1:P + 1], ACT.Exp, scale=DECAY, bias=sm[:, 4 + i:5 + i]
                               ).then_inc(s.sem, 1)
        if step == 3:
            act.wait_ge(z.sem, z(1))
            act.wait_ge(s.sem, s(8))
            for i in range(NB):
                act.activation(L[:, i, :], L[:, i, :], ACT.Exp, scale=-DECAY, bias=sm[:, i:i + 1]).then_inc(s.sem, 1)
            act.wait_ge(s.sem, s(12))
            act.activation(sm[:, 16:20], L[:, :, P], ACT.Copy).then_inc(s.sem, 1)

    def vectors_tensor(self, pe, p, step):
        k, s = self.k, self.k.sig("vec_tensor")
        ta, tv = self.k.sig("vec_scalar", "vec_vector")
        if step == 0:
            pe.wait_ge(ta.sem, ta(1))
            pe.matmul(k.ps[:, 6, :], k.blockones, self.t1[:, :], start=True, stop=True).then_inc(s.sem, 1)
        if step == 1:
            pe.wait_ge(tv.sem, tv(10))
            pe.matmul(k.ps[:, 7, :], k.blockones, self.t0[:, :], start=True, stop=True).then_inc(s.sem, 1)

    def vectors_pool(self, g, p):
        g.memset(self.L[:, :, 0:1], 0.0).then_inc(self.k.sig("zeroed").sem, 1)


    def products_tensor(self, pe, p):
        k = self.k
        tv, tok, tokc, pr, prm, i1, t0, yc = k.sig("vec_vector", "by_token", "by_token_taken", "products", "masked",
                                                   "single_inverse", "single_turned", "y_taken")
        AR = self.AR[:, p % 2]
        pe.wait_ge(tv.sem, tv(19))
        for n, src in enumerate((lambda i: AR[:, i, 0:P], lambda i: self.B[:, i, :], lambda i: self.K[:, i, :],
                                 lambda i: self.vv[:, p, i * P:(i + 1) * P])):
            for i in range(NB):
                mm = pe.transpose(self.bank(n)[:, i, :], src(i), k.ident)
            mm.then_inc(tok.sem, 1)
        for q in range(8):
            i, o = q // 2, 64 * (q % 2)
            if q >= 2:
                pe.wait_ge(prm.sem, prm(q - 1))
            pe.matmul(k.ps[:, 4 + q % 2, 0:256], self.B[o:o + 64, i, :], AR[o:o + 64, i, :], start=True, stop=True)
            pe.matmul(k.ps[:, 4 + q % 2, 256:512], self.K[o:o + 64, i, :], AR[o:o + 64, i, :], start=True, stop=True
                      ).then_inc(pr.sem, 1)
        for b in range(2):
            pe.wait_ge(i1.sem, i1(b + 1))
            if p:
                pe.wait_ge(yc.sem, yc(4))
            for q in range(4):
                mm = pe.transpose(self.bank(6 + b)[:, q, :], self.Tt[:, 4 * b + q, :], k.ident)
            mm.then_inc(t0.sem, 1)

    def products_scalar(self, act, p):
        k = self.k
        tok, tokc, t0, t0c = k.sig("by_token", "by_token_taken", "single_turned", "single_taken")
        for n, dst in enumerate((self.AT, self.BT, self.KT, self.VT)):
            act.wait_ge(tok.sem, tok(n + 1))
            act.activation(dst[:, :, :], self.bank(n), ACT.Copy).then_inc(tokc.sem, 1)
        for b in range(2):
            act.wait_ge(t0.sem, t0(b + 1))
            act.activation(self.T[:, 4 * b:4 * b + 4, :], self.bank(6 + b), ACT.Copy).then_inc(t0c.sem, 1)

    def products_vector(self, v, p):
        k = self.k
        pr, prm, i0, i1 = k.sig("products", "masked", "single_coupled", "single_inverse")
        for q in range(8):
            v.wait_ge(pr.sem, pr(q + 1))
            v.tensor_tensor(self.M[:, q, :], k.ps[:, 4 + q % 2, :], k.cst("m4", 512), ALU.mult).then_inc(prm.sem, 1)
        mask = k.consts[:, CST["levels"]:CST["levels"] + P].unsqueeze(1).to_broadcast([P, 4, P])
        ident = k.ident.unsqueeze(1).to_broadcast([P, 4, P])
        for b in range(2):
            u = self.Tt[:, 4 * b:4 * b + 4, :]
            v.wait_ge(prm.sem, prm(4 * b + 4))
            v.tensor_tensor(u, self.M[:, 4 * b:4 * b + 4, 0:P], mask, ALU.mult).then_inc(i0.sem, 1)
            v.wait_ge(i0.sem, i0(b + 1))
            v.tensor_tensor(u, u, ident, ALU.add).then_inc(i1.sem, 1)

    def advance_products(self):
        for n, c in (("by_token", 4), ("by_token_taken", 4), ("products", 8), ("masked", 8), ("single_coupled", 2),
                     ("single_inverse", 2), ("single_turned", 2), ("single_taken", 2)):
            self.k.sig(n).base += c

    def advance_vectors(self):
        for n, c in (("vec_vector", 19), ("vec_scalar", 13), ("vec_tensor", 2), ("zeroed", 1)):
            self.k.sig(n).base += c

    def first(self):
        with self.k.nc.Block() as block:
            @block.vector
            def _(v):
                for t in (self.S, self.Spc):
                    v.memset(t[:, :], 0.0).then_inc(self.k.sig("made").sem, 1)
                for step in range(5):
                    self.vectors_vector(v, 0, step)
                self.products_vector(v, 0)

            @block.scalar
            def _(act):
                for step in range(4):
                    self.vectors_scalar(act, 0, step)
                self.products_scalar(act, 0)

            @block.tensor
            def _(pe):
                for step in range(2):
                    self.vectors_tensor(pe, 0, step)
                self.products_tensor(pe, 0)

            @block.gpsimd
            def _(g):
                self.vectors_pool(g, 0)
        self.k.sig("made").base += 2
        self.advance_vectors()
        self.advance_products()

    def pair(self, p):
        k = self.k
        more = p + 1 < KD
        mo, ur, uc, gr, gtr, tu, ttu = k.sig("coupling", "mo_t", "mo_t_taken", "t_mo_t", "t_mo_t_turned", "t_joined",
                                             "t_turned_joined")
        xr, xc, hr, hc, gs, gc = k.sig("ak_v", "ak_v_taken", "h_sums", "h_taken", "g_sums", "g_taken")
        sar, sat, snr, st, ss, yr, yc = k.sig("sa_sums", "sa_made", "state_sums", "state_made", "state_scaled", "y_sums",
                                              "y_taken")
        tv = k.sig("vec_vector")
        AR, sm = self.AR[:, p % 2], self.sm[:, p % 2, :]
        M, Tm, Tt, U, Mo = self.M, self.T, self.Tt, self.U, self.Mo
        units = lambda t, b: t[:, 4 * b:4 * b + 4, 0:P]
        LV = 6

        with k.nc.Block() as block:
            @block.gpsimd
            def _(g):
                for l in range(1, LV + 1):
                    for b in range(2):
                        if l >= 3:
                            g.wait_ge(ur.sem, ur(2 * (l - 3) + b + 1))
                        c = CST["levels"] + l * P
                        g.tensor_tensor(Mo[:, l % 2, 4 * b:4 * b + 4, :], units(M, b),
                                        k.consts[:, c:c + P].unsqueeze(1).to_broadcast([P, 4, P]), ALU.mult
                                        ).then_inc(mo.sem, 1)
                    if l == 2 and more:
                        self.vectors_pool(g, p + 1)

            @block.tensor
            def _(pe):
                for q in range(8):
                    mm = pe.matmul(self.bank(6 + q // 4)[:, q % 4, :], M[:, q, 256:384], self.VT[:, q // 2, :],
                                   start=True, stop=True)
                    if q % 4 == 3:
                        mm.then_inc(xr.sem, 1)
                for l in range(1, LV + 1):
                    for b in range(2):
                        pe.wait_ge(mo.sem, mo(2 * (l - 1) + b + 1))
                        if l > 1:
                            pe.wait_ge(tu.sem, tu(2 * (l - 2) + b + 1))
                        for q in range(4):
                            mm = pe.matmul(self.bank(3 * b)[:, q, :], Mo[:, l % 2, 4 * b + q, :], Tm[:, 4 * b + q, :],
                                           start=True, stop=True)
                        mm.then_inc(ur.sem, 1)
                    for b in range(2):
                        pe.wait_ge(uc.sem, uc(2 * (l - 1) + b + 1))
                        if l > 1:
                            pe.wait_ge(ttu.sem, ttu(2 * (l - 2) + b + 1))
                        if l < LV:
                            for q in range(4):
                                mm = pe.matmul(self.bank(1 + 3 * b)[:, q, :], Tt[:, 4 * b + q, :], U[:, 4 * b + q, :],
                                               start=True, stop=True)
                            mm.then_inc(gr.sem, 1)
                        for q in range(4):
                            mm = pe.matmul(self.bank(2 + 3 * b)[:, q, :], U[:, 4 * b + q, :], Tt[:, 4 * b + q, :],
                                           start=True, stop=True)
                        mm.then_inc(gtr.sem, 1)
                    if more and l == 2:
                        pe.wait_ge(xc.sem, xc(4))
                        self.vectors_tensor(pe, p + 1, 0)
                    if more and l == 3:
                        self.vectors_tensor(pe, p + 1, 1)
                pe.wait_ge(xc.sem, xc(4))
                for b in range(2):
                    pe.wait_ge(ttu.sem, ttu(2 * (LV - 1) + b + 1))
                    for q in range(4 * b, 4 * b + 4):
                        mm = pe.matmul(self.bank(b)[:, q % 4, :], Tt[:, q, :], self.X[:, q // 2, :], start=True, stop=True)
                    mm.then_inc(hr.sem, 1)
                for q in range(8):
                    i, o = q // 2, 64 * (q % 2)
                    mm = pe.matmul(k.ps[o:o + 64, 3, i * P:(i + 1) * P], self.AT[:, i, o:o + 64], Tt[:, q, :],
                                   start=True, stop=True)
                mm.then_inc(gs.sem, 1)

                def output(i):
                    if i >= 2:
                        pe.wait_ge(yc.sem, yc(i - 1))
                    elif more:
                        pe.wait_ge(tv.sem, tv(15))
                    y = k.ps[:, 6 + i % 2, 0:P]
                    pe.wait_ge(ss.sem, ss(2 * i + 1))
                    pe.matmul(y, self.Ss[:, i % 2, :], AR[:, i, P:2 * P], start=True, stop=False, skip_group_check=True)
                    for hh in range(2):
                        o, q = 64 * hh, 2 * i + hh
                        yo = k.ps[o:o + 64, 6 + i % 2, 0:P]
                        pe.matmul(yo, self.VT[:, i, o:o + 64], M[:, q, 384:512], start=False, stop=False,
                                  skip_group_check=True)
                        mm = pe.matmul(yo, self.SA[:, i % 2, o:o + 64], M[:, q, P:2 * P], start=False, stop=(hh == 1),
                                       skip_group_check=True)
                    mm.then_inc(yr.sem, 1)

                pe.wait_ge(gc.sem, gc(4))
                for i in range(NB):
                    pe.wait_ge(st.sem, st(2 * i + 2))
                    pe.matmul(k.ps[:, 4, 0:P], self.G[:, i, :], self.S[:, :], start=True, stop=True).then_inc(sar.sem, 1)
                    if i < NB - 1:
                        pe.matmul(k.ps[:, 5, 0:P], self.KT[:, i, :], self.VT[:, i, :], start=True, stop=False)
                        pe.wait_ge(sat.sem, sat(i + 1))
                        pe.matmul(k.ps[:, 5, 0:P], self.BT[:, i, :], self.SA[:, i % 2, :], start=False, stop=True
                                  ).then_inc(snr.sem, 1)
                    else:
                        pe.wait_ge(sat.sem, sat(i + 1))
                    output(i)
                if more:
                    self.products_tensor(pe, p + 1)

            @block.scalar
            def _(act):
                def halves(dst, bank, b, done):
                    t = k.ps[:, bank, :].rearrange("p (i h d) -> p i h d", i=2, h=2)
                    for hh in range(2):
                        act.activation(dst[:, 2 * b:2 * b + 2, 64 * hh:64 * hh + 64], t[:, :, hh, 64 * hh:64 * hh + 64],
                                       ACT.Copy).then_inc(done.sem, 1)
                for l in range(1, LV + 1):
                    for b in range(2):
                        act.wait_ge(ur.sem, ur(2 * (l - 1) + b + 1))
                        act.activation(units(U, b), self.bank(3 * b), ACT.Copy).then_inc(uc.sem, 1)
                    if l == 1:
                        for b in range(2):
                            act.wait_ge(xr.sem, xr(b + 1))
                            halves(self.X, 6 + b, b, xc)
                    if more and l < 5:
                        self.vectors_scalar(act, p + 1, l - 1)
                for b in range(2):
                    act.wait_ge(hr.sem, hr(b + 1))
                    halves(self.H, b, b, hc)
                act.wait_ge(gs.sem, gs(1))
                for i in range(NB):
                    act.activation(self.G[:, i, :], k.ps[:, 3, i * P:(i + 1) * P], ACT.Copy, scale=sm[:, 8 + i:9 + i]
                                   ).then_inc(gc.sem, 1)
                for i in range(NB):
                    act.wait_ge(yr.sem, yr(i + 1))
                    act.activation(self.r[:, p, i * P:(i + 1) * P], k.ps[:, 6 + i % 2, 0:P], ACT.Copy).then_inc(yc.sem, 1)
                if more:
                    self.products_scalar(act, p + 1)

            @block.vector
            def _(v):
                if more:
                    self.vectors_vector(v, p + 1, 0)
                for l in range(1, LV + 1):
                    for b in range(2):
                        if l < LV:
                            v.wait_ge(gr.sem, gr(2 * (l - 1) + b + 1))
                            v.tensor_tensor(units(Tm, b), units(Tm, b), self.bank(1 + 3 * b), ALU.add).then_inc(tu.sem, 1)
                        v.wait_ge(gtr.sem, gtr(2 * (l - 1) + b + 1))
                        v.tensor_tensor(units(Tt, b), units(Tt, b), self.bank(2 + 3 * b), ALU.add).then_inc(ttu.sem, 1)
                    if more and l < 5:
                        self.vectors_vector(v, p + 1, l)
                v.memset(self.S[:, :], 0.0).then_inc(st.sem, 2)
                v.wait_ge(hc.sem, hc(4))
                for i in range(NB):
                    v.wait_ge(st.sem, st(2 * i + 2))
                    v.tensor_scalar(self.Ss[:, i % 2, :], self.S[:, :], sm[:, 8 + i:9 + i], None, ALU.mult).then_inc(ss.sem, 1)
                    v.tensor_scalar(self.Spc[:, :], self.S[:, :], sm[:, 12 + i:13 + i], None, ALU.mult).then_inc(ss.sem, 1)
                    v.wait_ge(sar.sem, sar(i + 1))
                    v.tensor_tensor(self.SA[:, i % 2, :], k.ps[:, 4, 0:P], self.H[:, i, :], ALU.add).then_inc(sat.sem, 1)
                    if i < NB - 1:
                        v.wait_ge(snr.sem, snr(i + 1))
                        v.wait_ge(ss.sem, ss(2 * i + 2))
                        for hh in range(2):
                            o = slice(64 * hh, 64 * hh + 64)
                            v.scalar_tensor_tensor(self.S[o, o], k.ps[o, 5, o], sm[o, 16 + i:17 + i], self.Spc[o, o],
                                                   ALU.mult, ALU.add).then_inc(st.sem, 1)
                if more:
                    self.products_vector(v, p + 1)
        for s, c in ((mo, 12), (ur, 12), (uc, 12), (gr, 10), (gtr, 12), (tu, 10), (ttu, 12), (xr, 2), (xc, 4), (hr, 2),
                     (hc, 4), (gs, 1), (gc, 4), (sar, 4), (sat, 4), (snr, 3), (st, 8), (ss, 8), (yr, 4), (yc, 4)):
            s.base += c
        if more:
            self.advance_vectors()
            self.advance_products()


def group_norm_and_gate(k, a, y, bonus, inner, z):
    rows, pick_cols = 2 * KD, N_CONST - CST["pick"]
    ld, me, ce, sq, va, rt, iv, sp_r, go, n1, n2, nd = k.sig(
        "lora_loaded", "gn_mean", "gn_centred", "gn_squared", "gn_summed", "gn_root", "gn_inverse", "gn_spread", "lora_out",
        "gn_scaled", "gn_shifted", "gn_done")
    with k.tile("gwb", [P, 2, D], F32) as wb, k.tile("gpick", [P, pick_cols], F32) as picks, \
         k.tile("gsq", [P, 2, T], F32) as sqt, k.tile("grt", [P, 2, T], F32) as rtt, k.nc.Block() as block:
        @block.sync
        def _(sp):
            sp.dma_start(picks[:, :], a["consts"][:, CST["pick"]:N_CONST]).then_inc(ld.sem, 16)
            sp.dma_start(wb[:, :, :], a["lora_b"][:, 2:4, :]).then_inc(ld.sem, 16)

        @block.tensor
        def _(pe):
            def mean(m):
                if m >= 2:
                    pe.wait_ge(ce.sem, ce(m - 1))
                pe.matmul(k.ps[:, m % 2, :], k.blockones, y[:, m, :], start=True, stop=True).then_inc(me.sem, 1)

            def gate(m):
                if m >= 3:
                    pe.wait_ge(nd.sem, nd(m - 2))
                pe.matmul(k.ps[:, 5 + m % 3, :], wb[:, 0, m * P:(m + 1) * P], inner[:, 0, :], start=True, stop=False)
                pe.matmul(k.ps[:, 5 + m % 3, :], wb[0:32, 1, m * P:(m + 1) * P], inner[0:32, 1, :], start=False, stop=True
                          ).then_inc(go.sem, 1)

            mean(0)
            mean(1)
            pe.wait_ge(ld.sem, ld(32))
            for m in range(KD):
                pe.wait_ge(sq.sem, sq(m + 1))
                c = HEAD_TILES * 2 - 2 - 2 * m
                pe.matmul(k.ps[0:rows, 2, :], picks[:, c:c + rows], sqt[:, m % 2, :], start=(m == 0), stop=(m == KD - 1)
                          ).then_inc(va.sem, 1)
                if m + 2 < KD:
                    mean(m + 2)
            for m in range(3):
                gate(m)
            pe.wait_ge(iv.sem, iv(1))
            for m in range(KD):
                if m >= 2:
                    pe.wait_ge(n1.sem, n1(m - 1))
                c = CST["spread"] - CST["pick"] + m * P
                pe.matmul(k.ps[:, 3 + m % 2, :], picks[0:rows, c:c + P], rtt[0:rows, 1, :], start=True, stop=True
                          ).then_inc(sp_r.sem, 1)
                if m >= 2 and m + 1 < KD:
                    gate(m + 1)

        @block.scalar
        def _(act):
            for m in range(KD):
                act.wait_ge(ce.sem, ce(m + 1))
                if m >= 2:
                    act.wait_ge(va.sem, va(m - 1))
                act.activation(sqt[:, m % 2, :], y[:, m, :], ACT.Square).then_inc(sq.sem, 1)
            act.wait_ge(va.sem, va(KD))
            act.activation(rtt[0:rows, 0, :], k.ps[0:rows, 2, :], ACT.Sqrt, scale=1.0 / 64, bias=k.bias[64e-5][0:rows]
                           ).then_inc(rt.sem, 1)

        @block.vector
        def _(v):
            for m in range(KD):
                v.wait_ge(me.sem, me(m + 1))
                v.scalar_tensor_tensor(y[:, m, :], k.ps[:, m % 2, :], -1.0 / 64, y[:, m, :], ALU.mult, ALU.add
                                       ).then_inc(ce.sem, 1)
            v.wait_ge(rt.sem, rt(1))
            v.reciprocal(rtt[0:rows, 1, :], rtt[0:rows, 0, :]).then_inc(iv.sem, 1)

            def shift(m):
                v.wait_ge(n1.sem, n1(m + 1))
                v.scalar_tensor_tensor(y[:, m, :], y[:, m, :], k.vec("ln_b", m), bonus[:, m, :], ALU.add, ALU.add
                                       ).then_inc(n2.sem, 1)

            def gated(m):
                v.wait_ge(n2.sem, n2(m + 1))
                v.wait_ge(go.sem, go(m + 1))
                v.tensor_tensor(z[:, m, :], y[:, m, :], k.ps[:, 5 + m % 3, :], ALU.mult).then_inc(nd.sem, 1)

            for m in range(KD + 2):
                if m < KD:
                    v.wait_ge(sp_r.sem, sp_r(m + 1))
                    v.scalar_tensor_tensor(y[:, m, :], y[:, m, :], k.vec("ln_g", m), k.ps[:, 3 + m % 2, :],
                                           ALU.mult, ALU.mult).then_inc(n1.sem, 1)
                if 1 <= m <= KD:
                    shift(m - 1)
                if m >= 2:
                    gated(m - 2)
    ld.base += 32
    for s in (rt, iv):
        s.base += 1
    for s in (me, ce, sq, va, sp_r, go, n1, n2, nd):
        s.base += KD


def rwkv(k, a, r):
    with ExitStack() as outer:
        tile = lambda st, name, *shape: st.enter_context(k.tile(name, [P, *shape], F32))
        kk, vv = (tile(outer, n, KD, T) for n in ("kk", "vv"))
        inner_g, inner_w, inner_a = tile(outer, "inner_g", 2, T), tile(outer, "inner_w", T), tile(outer, "inner_a", T)
        with ExitStack() as first:
            open_ring(k, first, 3 * KD)
            time_mix_inputs(k, a, r, kk, vv, inner_w, inner_a, inner_g)
            close_ring(k)
        with ExitStack() as stack:
            sg, aa = tile(stack, "sg", KD, T), tile(stack, "aa", KD, T)
            low_rank_outputs(k, a, inner_w, inner_a, sg, aa)
            pairs = Pairs(k, stack, r, kk, vv, sg, aa)
            pairs.first()
            for p in range(KD):
                pairs.pair(p)
        group_norm_and_gate(k, a, r, kk, inner_g, r)



def norm_memory(k, mem):
    squared, summed, root, inverse, normed, loaded = k.sig("squared", "summed", "root", "inverse", "normed",
                                                           "memory_loaded")
    with k.tile("sqm", [P, KD, MEM], F32) as sq, k.nc.Block() as block:
        @block.scalar
        def _(act):
            act.wait_ge(loaded.sem, loaded(16))
            for m in range(KD):
                act.activation(sq[:, m, :], mem[:, m, :], ACT.Square).then_inc(squared.sem, 1)
            act.wait_ge(summed.sem, summed(1))
            act.activation(k.root[:, 0:MEM], k.ps[:, 4, 0:MEM], ACT.Sqrt, scale=1.0 / D, bias=k.bias[1e-6]
                           ).then_inc(root.sem, 1)

        @block.tensor
        def _(pe):
            for m in range(KD):
                pe.wait_ge(squared.sem, squared(m + 1))
                mm = pe.matmul(k.ps[:, 4, 0:MEM], k.ones[:, :], sq[:, m, :], start=(m == 0), stop=(m == KD - 1))
            mm.then_inc(summed.sem, 1)

        @block.vector
        def _(v):
            v.wait_ge(root.sem, root(1))
            v.reciprocal(k.root[:, 0:MEM], k.root[:, 0:MEM]).then_inc(inverse.sem, 1)
            v.wait_ge(inverse.sem, inverse(1))
            for m in range(KD):
                v.scalar_tensor_tensor(mem[:, m, :], mem[:, m, :], k.vec("mem_norm", m), k.root[:, 0:MEM],
                                       ALU.mult, ALU.mult).then_inc(normed.sem, 1)
    for s, c in ((squared, KD), (summed, 1), (root, 1), (inverse, 1), (normed, KD), (loaded, 16)):
        s.base += c


def cross_attention(k, a, layer, mem):
    nc = k.nc
    with k.tile("km", [P, KD, MEM], F32) as km, k.tile("vt", [P, 2, D], F32) as vt:
        with k.tile("kvm", [P, 2 * KD, MEM], F32) as kv:
            norm_memory(k, mem)
            with ExitStack() as st:
                ms = Split(st, k, "ms", KD, MEM)
                linear(k, 2 * KD, KD, ms, act=copy_out(k, kv, width=MEM), width=MEM, feed=Parts(k, mem, ms, KD))
            tr, te, kc = k.sig("transposed", "transposed_out", "keys_copied")
            with nc.Block() as block:
                @block.tensor
                def _(pe):
                    for n in range(4):
                        mb, half = n % 2, n // 2
                        for q in range(4):
                            mm = pe.transpose(k.ps[:, n, q * P:(q + 1) * P], kv[:, KD + 4 * half + q, mb * P:(mb + 1) * P], k.ident)
                        mm.then_inc(tr.sem, 1)

                @block.scalar
                def _(act):
                    for n in range(4):
                        act.wait_ge(tr.sem, tr(n + 1))
                        act.activation(vt[:, n % 2, (n // 2) * 512:(n // 2) * 512 + 512], k.ps[:, n, :], ACT.Copy
                                       ).then_inc(te.sem, 1)

                @block.gpsimd
                def _(g):
                    g.tensor_copy(km[:, :, :], kv[:, 0:KD, :]).then_inc(kc.sem, 1)
            tr.base += 4
            te.base += 4
            kc.base += 1
        o_ = k.spare
        with k.tile("q", [P, KD, T], F32) as q_:
            used, free = k.sig("chunk_used", "bank_free")

            def queries(e, i, j):
                e.wait_ge(used.sem, used(i * 4 + (j + 1)))
                e.scalar_tensor_tensor(dyn(q_, i * 4 + j), k.ps[:, j, :], 1.0 / 16, k.root[:, :], ALU.mult, ALU.mult
                                       ).then_inc(free.sem, 1)
            linear(k, KD, KD, k.ahead, vector=queries, norm=True)
            sc, mx, ex, rc, wt, tr, te, po, oe = k.sig("scores", "maxima", "exps", "sums_inverted", "scaled", "transposed",
                                                       "transposed_out", "pv_done", "mixer_out")
            with k.tile("xp", [P, 4, MEM], F32) as p, k.tile("xpt", [P, 2, 2, T], F32) as pt, \
                 k.tile("xst", [P, 3, 16], F32) as st, nc.Block() as block:
                U = 16

                @block.tensor
                def _(pe):
                    def scores(u):
                        h, qb = u // 4, u % 4
                        if u >= 2:
                            pe.wait_ge(ex.sem, ex(u - 1))
                        for c in range(2):
                            mm = pe.matmul(k.ps[:, u % 2, 0:MEM], q_[:, 2 * h + c, qb * P:(qb + 1) * P],
                                           km[:, 2 * h + c, :], start=(c == 0), stop=(c == 1))
                        mm.then_inc(sc.sem, 1)

                    def turn(u):
                        pe.wait_ge(wt.sem, wt(u + 1))
                        if u >= 2:
                            pe.wait_ge(te.sem, te(u - 1))
                        for mb in range(2):
                            mm = pe.transpose(k.ps[:, 2 + u % 2, mb * P:(mb + 1) * P], p[:, u % 4, mb * P:(mb + 1) * P], k.ident)
                        mm.then_inc(tr.sem, 1)

                    def values(h):
                        pe.wait_ge(te.sem, te(4 * h + 4))
                        for db in range(2):
                            if h >= 1:
                                pe.wait_ge(oe.sem, oe(2 * h + db - 1))
                            for mb in range(2):
                                mm = pe.matmul(k.ps[:, 4 + db, :], vt[:, mb, h * 256 + db * P:h * 256 + (db + 1) * P],
                                               pt[:, h % 2, mb, :], start=(mb == 0), stop=(mb == 1))
                            mm.then_inc(po.sem, 1)
                    scores(0)
                    scores(1)
                    for u in range(U):
                        if u + 2 < U:
                            scores(u + 2)
                        turn(u)
                        if u % 4 == 0 and u:
                            values(u // 4 - 1)
                    values(3)

                @block.vector
                def _(v):
                    def out(n):
                        v.wait_ge(po.sem, po(n + 1))
                        v.tensor_copy(o_[:, n, :], k.ps[:, 4 + n % 2, :]).then_inc(oe.sem, 1)

                    def maximum(u):
                        v.wait_ge(sc.sem, sc(u + 1))
                        v.tensor_reduce(st[:, 0, u:u + 1], k.ps[:, u % 2, 0:MEM], AX.X, ALU.max, negate=True
                                        ).then_inc(mx.sem, 1)
                    maximum(0)
                    for u in range(U):
                        if u + 1 < U:
                            maximum(u + 1)
                        v.wait_ge(ex.sem, ex(u + 1))
                        v.reciprocal(st[:, 2, u:u + 1], st[:, 1, u:u + 1]).then_inc(rc.sem, 1)
                        v.wait_ge(rc.sem, rc(u + 1))
                        v.tensor_scalar(p[:, u % 4, :], p[:, u % 4, :], st[:, 2, u:u + 1], None, ALU.mult).then_inc(wt.sem, 1)
                        if u % 4 == 1 and u > 4:
                            out(2 * (u // 4 - 1))
                            out(2 * (u // 4 - 1) + 1)
                    out(6)
                    out(7)

                @block.scalar
                def _(act):
                    def exp(u):
                        act.wait_ge(mx.sem, mx(u + 1))
                        if u >= 4:
                            act.wait_ge(tr.sem, tr(u - 3))
                        act.activation(p[:, u % 4, :], k.ps[:, u % 2, 0:MEM], ACT.Exp, bias=st[:, 0, u:u + 1],
                                       accum_out=st[:, 1, u:u + 1]).then_inc(ex.sem, 1)

                    def take(u):
                        h, qb = u // 4, u % 4
                        act.wait_ge(tr.sem, tr(u + 1))
                        if h >= 2:
                            act.wait_ge(po.sem, po(2 * (h - 1)))
                        act.activation(pt[:, h % 2, :, qb * P:(qb + 1) * P],
                                       k.ps[:, 2 + u % 2, 0:MEM].rearrange("p (m t) -> p m t", m=2), ACT.Copy
                                       ).then_inc(te.sem, 1)
                    exp(0)
                    for u in range(U):
                        if u + 1 < U:
                            exp(u + 1)
                        take(u)
            for s in (sc, mx, ex, rc, wt, tr, te):
                s.base += U
            po.base += 8
            oe.base += 8
        with ExitStack() as st:
            os_ = Split(st, k, "os", KD, T)
            residual(k, KD, os_, gain=f"ffn{layer}", feed=Parts(k, o_, os_, KD))



def conformer(k, a, early):
    nc = k.nc
    used, free, sig_r, dg, padz = k.sig("chunk_used", "bank_free", "sigmoid_made", "diagonals", "zeroed")
    V_TAPS = TAPS - PE_TAPS
    y = k.spare
    scaled = k.sig("normed_sums")
    with ExitStack():
        with k.tile("conv_u", [P, KD, T + TAPS - 1], F32) as u, \
             k.tile("conv_dg", [P, 2, PE_TAPS, P], F32) as diag, k.tile("conv_s", [P, 2, T], F32) as sg:
            def act(e, i, j):
                if j % 2 == 0:
                    return
                f = 2 * i + j // 2
                e.wait_ge(scaled.sem, scaled(2 * f + 2))
                if f >= 2:
                    e.wait_ge(free.sem, free(2 * (f - 1) + RING))
                e.activation(sg[:, f % 2, :], k.ps[:, j, :], ACT.Sigmoid, bias=k.vec("cb_in", 8 + f)).then_inc(sig_r.sem, 1)

            def vector(e, i, j):
                e.wait_ge(used.sem, used(4 * i + j + 1))
                e.tensor_tensor(k.ps[:, j, :], k.ps[:, j, :], k.root[:, :], ALU.mult).then_inc(scaled.sem, 1)
                if j % 2 == 0:
                    return
                f = 2 * i + j // 2
                e.wait_ge(scaled.sem, scaled(2 * f + 1))
                e.wait_ge(sig_r.sem, sig_r(f + 1))
                e.scalar_tensor_tensor(u[:, f, TAPS - 1:], k.ps[:, j - 1, :], k.vec("cb_in", f), sg[:, f % 2, :],
                                       ALU.add, ALU.mult).then_inc(free.sem, 2)

            linear(k, 2 * KD, KD, k.ahead, act=act, vector=vector, unroll=True, norm=True)
            sig_r.base += KD
            scaled.base += 2 * KD
            tp, ac, ye = k.sig("taps_summed", "taps_added", "conv_taken")
            with nc.Block() as block:
                @block.gpsimd
                def _(g):
                    g.memset(u[:, :, 0:TAPS - 1], 0.0).then_inc(padz.sem, 1)
                    for m in range(KD):
                        if m >= 2:
                            g.wait_ge(tp.sem, tp(m - 1))
                        for t in range(PE_TAPS):
                            c = VEC["cdw"] + TAPS * m + t
                            g.tensor_scalar(diag[:, m % 2, t, :], k.ident, k.vecs[:, c:c + 1], None, ALU.mult
                                            ).then_inc(dg.sem, 1)

                @block.tensor
                def _(pe):
                    pe.wait_ge(padz.sem, padz(1))
                    for m in range(KD):
                        if m >= 4:
                            pe.wait_ge(ye.sem, ye(m - 3))
                        for t in range(PE_TAPS):
                            pe.wait_ge(dg.sem, dg(m * PE_TAPS + t + 1))
                            mm = pe.matmul(k.ps[:, m % 4, :], diag[:, m % 2, t, :], u[:, m, t:t + T], start=(t == 0),
                                           stop=(t == PE_TAPS - 1))
                        mm.then_inc(tp.sem, 1)

                @block.vector
                def _(v):
                    n = 0
                    for pair in range(KD // 2):
                        v.wait_ge(tp.sem, tp(2 * pair + 2))
                        for t in range(PE_TAPS, TAPS):
                            for m in (2 * pair, 2 * pair + 1):
                                if t > PE_TAPS:
                                    v.wait_ge(ac.sem, ac(n - 1))
                                c = VEC["cdw"] + TAPS * m + t
                                v.scalar_tensor_tensor(k.ps[:, m % 4, :], u[:, m, t:t + T], k.vecs[:, c:c + 1],
                                                       k.ps[:, m % 4, :], ALU.mult, ALU.add).then_inc(ac.sem, 1)
                                n += 1

                @block.scalar
                def _(act):
                    for m in range(KD):
                        act.wait_ge(ac.sem, ac((m // 2) * 2 * V_TAPS + 2 * V_TAPS - (1 - m % 2)))
                        act.activation(y[:, m, :], k.ps[:, m % 4, :], ACT.Identity, bias=k.vec("cdw_b", m)).then_inc(ye.sem, 1)
            padz.base += 1
            dg.base += KD * PE_TAPS
            tp.base += KD
            ac.base += KD * V_TAPS
            ye.base += KD
        me, ce, sq, va, rt, iv, n1, n2 = k.sig("gn_mean", "gn_centred", "gn_squared", "gn_var", "gn_root", "gn_inverse",
                                               "gn_scaled", "gn_shifted")
        with k.tile("ln_sq", [P, KD, T], F32) as sqt, k.tile("ln_rt", [P, T], F32) as rtt, \
             nc.Block() as block:
            @block.tensor
            def _(pe):
                for m in range(KD):
                    mm = pe.matmul(k.ps[:, 4, :], k.ones[:, :], y[:, m, :], start=(m == 0), stop=(m == KD - 1))
                mm.then_inc(me.sem, 1)
                for m in range(KD):
                    pe.wait_ge(sq.sem, sq(m + 1))
                    mm = pe.matmul(k.ps[:, 5, :], k.ones[:, :], sqt[:, m, :], start=(m == 0), stop=(m == KD - 1))
                mm.then_inc(va.sem, 1)

            @block.vector
            def _(v):
                v.wait_ge(me.sem, me(1))
                for m in range(KD):
                    v.scalar_tensor_tensor(y[:, m, :], k.ps[:, 4, :], -1.0 / D, y[:, m, :], ALU.mult, ALU.add
                                           ).then_inc(ce.sem, 1)
                v.wait_ge(rt.sem, rt(1))
                v.reciprocal(k.ps[:, 6, :], rtt[:, :]).then_inc(iv.sem, 1)
                v.wait_ge(iv.sem, iv(1))
                for m in range(KD):
                    v.scalar_tensor_tensor(y[:, m, :], y[:, m, :], k.vec("cln_g", m), k.ps[:, 6, :], ALU.mult, ALU.mult
                                           ).then_inc(n1.sem, 1)

            @block.scalar
            def _(act):
                for m in range(KD):
                    act.wait_ge(ce.sem, ce(m + 1))
                    act.activation(sqt[:, m, :], y[:, m, :], ACT.Square).then_inc(sq.sem, 1)
                act.wait_ge(va.sem, va(1))
                act.activation(rtt[:, :], k.ps[:, 5, :], ACT.Sqrt, scale=1.0 / D, bias=k.bias[1e-5]).then_inc(rt.sem, 1)
                for m in range(KD):
                    act.wait_ge(n1.sem, n1(m + 1))
                    act.activation(y[:, m, :], y[:, m, :], ACT.Silu, bias=k.vec("cln_b", m)).then_inc(n2.sem, 1)
        me.base += 1
        va.base += 1
        rt.base += 1
        iv.base += 1
        for s in (ce, sq, n1, n2):
            s.base += KD
        with ExitStack() as st:
            ys = Split(st, k, "ys", KD, T)
            residual(k, KD, ys, bias="cb_out", gain="xattn1", feed=Parts(k, y, ys, KD), early=early)


def conv_ffn(k, layer, gain=None):
    nc = k.nc
    used, free, ub_r, cv, silu, hi, lo, padz = k.sig(
        "chunk_used", "bank_free", "ffn_copied", "ffn_conv", "ffn_silu", "hidden_hi", "hidden_lo", "zeroed")
    w0 = VEC[f"fdw{layer}"]
    with ExitStack() as st:
        a_ = Split(st, k, "ffn_a", FFN_PARTS[0], T)
        ub = st.enter_context(k.tile("ffn_u", [P, 4, T + 2], F32))
        sg = st.enter_context(k.tile("ffn_s", [P, 2, T], F32))
        tmp = st.enter_context(k.tile("ffn_t", [P, 2, T], F32))
        with nc.Block() as block:
            @block.gpsimd
            def _(g):
                g.memset(ub[:, :, 0:2], 0.0).then_inc(padz.sem, 1)
        padz.base += 1
        before = 0
        for part, FT in enumerate(FFN_PARTS):
            def act(e, i, j):
                f = 2 * i + j // 2
                if j % 2:
                    e.wait_ge(cv.sem, cv(6 * f + 6))
                    e.activation(sg[:, f % 2, :], k.ps[:, j - 1, :], ACT.Silu).then_inc(silu.sem, 1)
                    e.wait_ge(free.sem, free(2 * f + 2 + RING))
                    e.activation(a_.hi[:, f, :], tmp[:, f % 2, :], ACT.Copy).then_inc(hi.sem, 1)

            def vector(e, i, j):
                m = 4 * i + j
                e.wait_ge(used.sem, used(m + 1))
                if m >= 4:
                    e.wait_ge(cv.sem, cv(6 * ((m - 4) // 2) + 5 + m % 2))
                e.tensor_tensor(ub[:, j, 2:T + 2], k.ps[:, j, :], k.root[:, :], ALU.mult).then_inc(ub_r.sem, 1)
                if j % 2 == 0:
                    return
                f = 2 * i + j // 2
                for t in (2, 1, 0):
                    for jj in range(2):
                        m = 2 * f + jj
                        bank = k.ps[:, m % 4, :]
                        c = w0 + 3 * (2 * before + m) + t
                        col = k.vecs[:, c:c + 1]
                        if t == 2:
                            e.wait_ge(ub_r.sem, ub_r(m + 1))
                            e.scalar_tensor_tensor(bank, bank, col, k.root[:, :], ALU.mult, ALU.mult).then_inc(cv.sem, 1)
                        else:
                            e.wait_ge(cv.sem, cv(6 * f + 2 * (2 - t) + jj - 1))
                            e.scalar_tensor_tensor(bank, ub[:, m % 4, t:t + T], col, bank, ALU.mult, ALU.add
                                                   ).then_inc(cv.sem, 1)
                e.wait_ge(silu.sem, silu(f + 1))
                e.tensor_tensor(tmp[:, f % 2, :], sg[:, f % 2, :], k.ps[:, j, :], ALU.mult).then_inc(free.sem, 2)
                e.wait_ge(hi.sem, hi(f + 1))
                e.tensor_tensor(a_.lo[:, f, :], tmp[:, f % 2, :], as_float(a_.hi[:, f, :]), ALU.subtract).then_inc(lo.sem, 1)
            linear(k, 2 * FT, KD, k.ahead, act=act, vector=vector, unroll=True, norm=(part == 0))
            ub_r.base += 2 * FT
            cv.base += 6 * FT
            for s in (silu, hi, lo):
                s.base += FT
            residual(k, FT, a_, per=2, squares=(part == 1), gain=gain if part else None)
            before += FT


def final_norm(k):
    summed, root, inverse, normed = k.sig("summed", "root", "inverse", "normed")
    with k.nc.Block() as block:
        @block.tensor
        def _(pe):
            pe.matmul(k.ps[:, 4, :], k.ones[:, :], k.squares[:, :], start=True, stop=True).then_inc(summed.sem, 1)

        @block.scalar
        def _(act):
            act.wait_ge(summed.sem, summed(1))
            act.activation(k.root[:, :], k.ps[:, 4, :], ACT.Sqrt, scale=1.0 / D, bias=k.bias[1e-6]).then_inc(root.sem, 1)

        @block.vector
        def _(v):
            v.wait_ge(root.sem, root(1))
            v.reciprocal(k.root[:, :], k.root[:, :]).then_inc(inverse.sem, 1)
            v.wait_ge(inverse.sem, inverse(1))
            for m in range(KD):
                v.scalar_tensor_tensor(k.x[:, m, :], k.x[:, m, :], k.vec("final", m), k.root[:, :],
                                       ALU.mult, ALU.mult).then_inc(normed.sem, 1)
    for s, c in ((summed, 1), (root, 1), (inverse, 1), (normed, KD)):
        s.base += c


def second_block(k, a):
    with ExitStack() as st:
        k.spare = st.enter_context(k.tile("spare", [P, KD, T], F32))
        rwkv(k, a, k.spare)
        open_ring(k, st, k.n_chunks - k.chunk)
        k.ahead = Split(st, k, "ahead", KD, T)

        def load_memory(mem):
            return lambda e: e.dma_start(mem[:, :, :], a["mem"]).then_inc(k.sig("memory_loaded").sem, 16)
        with k.tile("mem", [P, KD, MEM], F32) as mem:
            with ExitStack() as zst:
                zs = Split(zst, k, "z", KD, T)
                residual(k, KD, zs, gain="xattn0", feed=Parts(k, k.spare, zs, KD), early=load_memory(mem))
            cross_attention(k, a, 0, mem)
        conv_ffn(k, 0, gain="mix1")
        with k.tile("mem", [P, KD, MEM], F32) as mem:
            conformer(k, a, load_memory(mem))
            cross_attention(k, a, 1, mem)
        conv_ffn(k, 1)
        final_norm(k)
        close_ring(k)



def build(nc, a, out):
    k = Core(nc)
    k.wall = a["wall"]
    k.n_chunks = a["wall"].shape[0]
    k.x = nc.alloc_sbuf_tensor("x_stream", [P, KD, T], F32)
    k.squares = nc.alloc_sbuf_tensor("squares", [P, T], F32)
    k.root = nc.alloc_sbuf_tensor("root", [P, T], F32)
    k.vecs = nc.alloc_sbuf_tensor("vecs", [P, N_VEC], F32)
    k.consts = nc.alloc_sbuf_tensor("consts", [P, N_KEEP], F32)
    k.ones = nc.alloc_sbuf_tensor("ones", [P, P], F32)
    k.negones = nc.alloc_sbuf_tensor("negones", [P, P], F32)
    k.eps = nc.alloc_sbuf_tensor("eps", [P, 8], F32)
    k.ps = nc.alloc_psum_tensor("ps", [P, 8, 512], F32)
    k.ident = k.cst("ident", 128)
    k.blockones = k.cst("blockones", 128)
    k.negtri = k.cst("negtri", 128)
    load_everything(k, a)
    with ExitStack() as ring:
        open_ring(k, ring, N_PROJ + KD + 64)
        first_block(k, a)
        close_ring(k)
    second_block(k, a)
    stored = k.sig("stored")
    with nc.Block() as block:
        @block.sync
        def _(sp):
            sp.dma_start(out, k.x[:, :, :]).then_inc(stored.sem, 16)
            sp.wait_ge(stored.sem, stored(16))


def chunks(w):
    K, M = w.shape
    per = -(-K // 1024)
    full = np.zeros((per * 1024, M), w.dtype)
    full[:K] = w
    return np.ascontiguousarray(full.reshape(per, 8, P, M // P, P).transpose(3, 0, 2, 1, 4)).reshape(-1, P, 1024)


def interleave(w, pairs):
    K = w.shape[0]
    return w.reshape(K, 2, pairs, P).transpose(0, 2, 1, 3).reshape(K, -1)


def layout(i):
    c = lambda *s: np.arange(*s)
    w_in = np.asarray(i["w_in"])[0]
    q0, kv0, g0, d0, s0 = 0, 256, 640, 652, 1804
    kv = lambda n: c(kv0 + 64 * n, kv0 + 64 * n + 64)
    cols = np.concatenate([c(0, 256), kv(0), kv(1), kv(2), kv(2), kv(4), kv(4), kv(3), kv(5), c(d0, s0), c(s0, s0 + 1152)])
    n = {m: np.asarray(v) for m, v in i.items()}
    fw = lambda l: interleave(n["ffn_w_in_2"][l], F2 // P)
    cut = FFN_PARTS[0] * P
    ffn = lambda l: [fw(l)[:, :2 * cut], n["ffn_w_out_2"][l][:cut], fw(l)[:, 2 * cut:], n["ffn_w_out_2"][l][cut:]]
    wall = np.concatenate([chunks(w) for w in [
        w_in[:, cols], n["w_out"][0],
        n["w_up"][0][:, :F1 // 2], n["w_down"][0][:F1 // 2], n["w_up"][0][:, F1 // 2:], n["w_down"][0][F1 // 2:],
        n["rwkv_w_r_2"][0], n["rwkv_w_k_2"][0], n["rwkv_w_v_2"][0], n["rwkv_w_o_2"][0],
        n["xattn_w_kv_2"][0], n["xattn_w_q_2"][0], n["xattn_w_o_2"][0], *ffn(0),
        interleave(n["conv_w_in_2"][0], 8), n["conv_w_out_2"][0],
        n["xattn_w_kv_2"][1], n["xattn_w_q_2"][1], n["xattn_w_o_2"][1], *ffn(1)]])
    col = lambda v: v.reshape(-1, P).T
    fdw = lambda l: n["ffn_dw_2"][l].reshape(3, 2, F2 // P, P).transpose(3, 2, 1, 0).reshape(P, -1)
    gains = np.concatenate([n["qk_gain_nsa"][0], n["qk_gain_dil"][0]])
    vecs = {"norm_mix": col(n["norm_mix"][0]), "norm_mlp": col(n["norm_mlp"][0]), "mem_norm": col(n["mem_norm_g_2"]),
            "mix0": col(n["norm_mix_g_2"][0]), "mix1": col(n["norm_mix_g_2"][1]),
            "xattn0": col(n["norm_xattn_g_2"][0]), "xattn1": col(n["norm_xattn_g_2"][1]),
            "ffn0": col(n["norm_ffn_g_2"][0]), "ffn1": col(n["norm_ffn_g_2"][1]), "final": col(n["final_norm_g_2"]),
            "mu": col(n["rwkv_mu_2"][0]), "w0": col(n["rwkv_w0_2"][0]), "a0": col(n["rwkv_a0_2"][0]),
            "k_k": col(n["rwkv_k_k_2"][0]), "k_a": col(n["rwkv_k_a_2"][0]), "r_k": col(n["rwkv_r_k_2"][0]),
            "ln_g": col(n["rwkv_ln_g_2"][0]), "ln_b": col(n["rwkv_ln_b_2"][0]), "cb_in": col(n["conv_b_in_2"][0]),
            "cdw": n["conv_dw_2"][0].reshape(TAPS, 8, P).transpose(2, 1, 0).reshape(P, -1),
            "cdw_b": col(n["conv_dw_b_2"][0]), "cln_g": col(n["conv_ln_g_2"][0]), "cln_b": col(n["conv_ln_b_2"][0]),
            "cb_out": col(n["conv_b_out_2"][0]), "fdw0": fdw(0), "fdw1": fdw(1),
            "gains": np.concatenate([gains, gains], axis=1).T}
    act = lambda x: np.ascontiguousarray(x.T.reshape(KD, P, -1).transpose(1, 0, 2))
    lora_a = np.concatenate([n["rwkv_w1_2"][0], n["rwkv_a1_2"][0], n["rwkv_g1_2"][0]], axis=1)
    lora_b = np.zeros((4, P, D), lora_a.dtype)
    lora_b[0, :64], lora_b[1, :64] = n["rwkv_w2_2"][0], n["rwkv_a2_2"][0]
    lora_b[2], lora_b[3, :32] = n["rwkv_g2_2"][0][:P], n["rwkv_g2_2"][0][P:]
    w2 = n["cmp_w2"][0]
    return {
        "x": act(n["x"][0]), "mem": act(n["mem_2"][0]), "wall": wall,
        "vecs": np.ascontiguousarray(np.concatenate([vecs[m] for m, _ in VEC_SIZES], axis=1)),
        "consts": constants(),
        "w_gate": np.ascontiguousarray(w_in[:, g0:d0].reshape(KD, P, 12).transpose(1, 0, 2)),
        "cmp_w1": np.ascontiguousarray(n["cmp_w1"][0].reshape(2, 32, 64, 128).transpose(0, 2, 1, 3)).reshape(P, 32, 128),
        "cmp_w2": np.ascontiguousarray(np.concatenate([w2[0], w2[0], w2[1]], axis=1)),
        "cmp_pe": np.ascontiguousarray(n["cmp_pe"][0].transpose(0, 2, 1)).reshape(P, 32),
        "lora_a": np.ascontiguousarray(lora_a.reshape(KD, P, 288).transpose(1, 0, 2)),
        "lora_b": np.ascontiguousarray(lora_b.transpose(1, 0, 2)),
    }


def constants():
    p = np.arange(P)[:, None]
    q = np.arange(P)[None]
    c = {}
    c["ident"] = (p == q)
    c["blockones"] = (p // 64 == q // 64)
    c["negtri"] = -1.0 * (p >= q)
    c["m4"] = np.concatenate([p < q, p <= q, p < q, p <= q], axis=1)
    c["levels"] = np.concatenate([((p // b) % 2 == 0) & (q // b == p // b + 1) for b in (1, 2, 4, 8, 16, 32, 64)], axis=1)
    far = (p + 3 * P) - np.arange(T)[None]
    ok = [far >= 0, (far >= 0) & (far <= 128), (far >= 0) & (far % 4 == 0), (far >= 0) & (far % 16 == 0)]
    c["dist"] = np.concatenate([np.where(m, -1.0 * far, NEG) for m in ok], axis=1)
    far = (np.arange(NB)[None, :, None] * P + np.arange(P)[:, None, None]) - (16 * np.arange(32)[None, None] + 31)
    c["dist_cmp"] = np.where(far >= 0, -1.0 * far, NEG).reshape(P, -1)
    c["valid"] = (p >= 31)
    u = np.arange(4 * HEAD_TILES - 2)[None] - (2 * HEAD_TILES - 2)
    c["pick"] = (p // 64 == u)
    c["spread"] = np.concatenate([(p == 2 * m + q // 64) for m in range(HEAD_TILES)], axis=1)
    c["pick_scale"] = np.where(p < HEAD_TILES, 1.0, 1.0 / HD)
    c["pick_bias"] = np.where(p < HEAD_TILES, HD * 1e-6, 1e-6)
    return np.ascontiguousarray(np.concatenate([c[m].astype(np.float32) for m, _ in CONST_SIZES], axis=1))


def kernel(**inputs):
    import concourse.bacc as _bacc
    from concourse.bass_utils import run_bass_kernel_spmd as _run

    nc = _bacc.Bacc("TRN2", target_bir_lowering=False, num_devices=1)
    arrays, args = {}, {}
    for name, v in layout(inputs).items():
        arrays[f"in_{name}"] = v
        args[name] = nc.dram_tensor(f"in_{name}", v.shape, mybir.dt.from_np(v.dtype), kind="ExternalInput").ap()
    out = nc.dram_tensor("out_y", [P, KD, T], F32, kind="ExternalOutput").ap()
    build(nc, args, out)
    r = _run(nc, [arrays], core_ids=[0])
    y = r.results[0]["out_y"]
    return np.ascontiguousarray(y.transpose(2, 1, 0)).reshape(1, T, D)
```
